# Optimizing a Trainium2 kernel written in Bass

```python
import math
import jax, jax.numpy as jnp
from jax import lax
import numpy as np

D_MODEL = 1024
BATCH = 1
SEQ = 512
DEPTH = 2

N_MIXERS = 2
N_GLA_LAYERS = (DEPTH + 1) // 2
N_ATTN_LAYERS = DEPTH // 2

GRID_W = 64

GLA_HEADS = 4
GLA_KEY_DIM = D_MODEL // 2
GLA_VAL_DIM = D_MODEL
GLA_DK = GLA_KEY_DIM // GLA_HEADS
GLA_DV = GLA_VAL_DIM // GLA_HEADS
GLA_GATE_RANK = 16
GLA_GATE_NORMALIZER = 16.0
GLA_CHUNK = 64
GLA_IN_DIM = 2 * GLA_KEY_DIM + 2 * GLA_VAL_DIM + 2 * GLA_GATE_RANK

ATTN_HEAD_DIM = 128
ATTN_Q_HEADS = D_MODEL // ATTN_HEAD_DIM
ATTN_KV_HEADS = 2
ATTN_GROUP = ATTN_Q_HEADS // ATTN_KV_HEADS
ATTN_QKV_DIM = (ATTN_Q_HEADS + 2 * ATTN_KV_HEADS) * ATTN_HEAD_DIM
QUERY_BLOCK = 128
ROPE_THETA = 10000.0
ROPE_PAIRS_PER_AXIS = ATTN_HEAD_DIM // 4

D_FF = 2816
CONV_WIDTH = 3

NORM_EPS = 1e-6


def rmsnorm(x, w):
    xf = x.astype(jnp.float32)
    y = xf * lax.rsqrt(jnp.mean(xf * xf, axis=-1, keepdims=True) + NORM_EPS)
    return (y * w.astype(jnp.float32)).astype(x.dtype)

def gla_chunked(q, k, v, log_a, strict):
    B, H, S, dk = q.shape
    dv = v.shape[-1]
    n = S // GLA_CHUNK
    c = lambda t: t.reshape(B, H, n, GLA_CHUNK, t.shape[-1])
    q, k, v, log_a = c(q), c(k), c(v), c(log_a)
    b = jnp.cumsum(log_a, axis=3)
    b_end = b[:, :, :, -1:, :]
    q_dec = q * jnp.exp(b)
    k_inv = k * jnp.exp(-b)
    mask = jnp.tril(jnp.ones((GLA_CHUNK, GLA_CHUNK), dtype=bool), k=-1 if strict else 0)
    att = jnp.where(mask, jnp.einsum('bhncd,bhnsd->bhncs', q_dec, k_inv), 0.0)
    o_intra = jnp.einsum('bhncs,bhnsv->bhncv', att, v)
    kv_chunk = jnp.einsum('bhncd,bhncv->bhndv', k * jnp.exp(b_end - b), v)
    decay_chunk = jnp.exp(b_end[:, :, :, 0, :])

    def step(state, inp):
        d, kv_c = inp
        return d[..., None] * state + kv_c, state

    _, s_prev = lax.scan(step, jnp.zeros((B, H, dk, dv), jnp.float32),
                         (jnp.moveaxis(decay_chunk, 2, 0), jnp.moveaxis(kv_chunk, 2, 0)))
    s_prev = jnp.moveaxis(s_prev, 0, 2)
    o_inter = jnp.einsum('bhncd,bhndv->bhncv', q_dec, s_prev)
    return (o_intra + o_inter).reshape(B, H, S, dv)

def gla_mixer(h, w_in, w_gate_up_f, b_gate_f, w_gate_up_b, b_gate_b, norm_w, w_out):
    B, S, _ = h.shape
    f32 = jnp.float32
    proj = h @ w_in
    q, k, v, g, r = jnp.split(
        proj, [GLA_KEY_DIM, 2 * GLA_KEY_DIM, 2 * GLA_KEY_DIM + GLA_VAL_DIM,
               2 * GLA_KEY_DIM + 2 * GLA_VAL_DIM], axis=-1)
    r_f, r_b = jnp.split(r, 2, axis=-1)

    def heads(t, d):
        return t.reshape(B, S, GLA_HEADS, d).transpose(0, 2, 1, 3).astype(f32)

    def log_decay(r_dir, w_up, b_up):
        logits = (r_dir @ w_up + b_up).astype(f32)
        return heads(jax.nn.log_sigmoid(logits) / GLA_GATE_NORMALIZER, GLA_DK)

    q = heads(q, GLA_DK) * (GLA_DK ** -0.5)
    k = heads(k, GLA_DK)
    v = heads(v, GLA_DV)
    la_f = log_decay(r_f, w_gate_up_f, b_gate_f)
    la_b = log_decay(r_b, w_gate_up_b, b_gate_b)
    flip = lambda t: jnp.flip(t, axis=2)
    o_f = gla_chunked(q, k, v, la_f, strict=False)
    o_b = flip(gla_chunked(flip(q), flip(k), flip(v), flip(la_b), strict=True))
    o = (o_f + o_b).transpose(0, 2, 1, 3)
    o = rmsnorm(o, norm_w) * jax.nn.silu(g.astype(f32).reshape(B, S, GLA_HEADS, GLA_DV))
    return o.reshape(B, S, GLA_VAL_DIM).astype(h.dtype) @ w_out

def apply_rope(x, cos, sin):
    half = x.shape[-1] // 2
    x1, x2 = x[..., :half], x[..., half:]
    return jnp.concatenate([x1 * cos - x2 * sin, x1 * sin + x2 * cos], axis=-1)

def attn_mixer(h, w_qkv, q_norm, k_norm, w_out, cos, sin):
    B, S, _ = h.shape
    proj = h @ w_qkv
    q, k, v = jnp.split(proj, [ATTN_Q_HEADS * ATTN_HEAD_DIM,
                               (ATTN_Q_HEADS + ATTN_KV_HEADS) * ATTN_HEAD_DIM], axis=-1)
    q = q.reshape(B, S, ATTN_Q_HEADS, ATTN_HEAD_DIM)
    k = k.reshape(B, S, ATTN_KV_HEADS, ATTN_HEAD_DIM)
    v = v.reshape(B, S, ATTN_KV_HEADS, ATTN_HEAD_DIM)
    q = apply_rope(rmsnorm(q, q_norm).astype(jnp.float32), cos, sin).astype(h.dtype)
    k = apply_rope(rmsnorm(k, k_norm).astype(jnp.float32), cos, sin).astype(h.dtype)
    n_blk = S // QUERY_BLOCK
    qb = q.reshape(B, S, ATTN_KV_HEADS, ATTN_GROUP, ATTN_HEAD_DIM).transpose(0, 2, 3, 1, 4)
    qb = qb.reshape(B, ATTN_KV_HEADS, ATTN_GROUP, n_blk, QUERY_BLOCK, ATTN_HEAD_DIM)
    qb = qb.transpose(3, 0, 1, 2, 4, 5)
    k = k.transpose(0, 2, 1, 3)
    v = v.transpose(0, 2, 1, 3)
    scale = ATTN_HEAD_DIM ** -0.5

    def block(q_blk):
        s = jnp.einsum('bkgqd,bksd->bkgqs', q_blk, k).astype(jnp.float32) * scale
        p = jax.nn.softmax(s, axis=-1).astype(v.dtype)
        return jnp.einsum('bkgqs,bksd->bkgqd', p, v)

    o = lax.map(block, qb)
    o = o.transpose(1, 0, 4, 2, 3, 5).reshape(B, S, ATTN_Q_HEADS * ATTN_HEAD_DIM)
    return o @ w_out

def conv_ffn(h, w_up, w_conv, b_conv, w_down):
    u = h @ w_up
    u = lax.conv_general_dilated(
        u, w_conv[:, None, :], window_strides=(1,), padding=[(1, 1)],
        dimension_numbers=('NWC', 'WIO', 'NWC'), feature_group_count=u.shape[-1]) + b_conv
    val, gate = jnp.split(u, 2, axis=-1)
    return (jax.nn.silu(gate) * val) @ w_down

def first_inputs(seed: int = 0) -> dict:
    key = jax.random.key(seed)
    ks = jax.random.split(key, 20)
    nrm = lambda k, shape, s: jax.random.normal(k, shape, jnp.float32) * s
    NG, NA = N_GLA_LAYERS, N_ATTN_LAYERS
    return {
        'x': nrm(ks[0], (BATCH, SEQ, D_MODEL), 1.0),
        'norm_mix': 1.0 + nrm(ks[1], (DEPTH, D_MODEL), 0.01),
        'norm_ffn': 1.0 + nrm(ks[2], (DEPTH, D_MODEL), 0.01),
        'gla_w_in': nrm(ks[3], (NG, D_MODEL, GLA_IN_DIM), D_MODEL ** -0.5),
        'gla_w_gate_up_f': nrm(ks[4], (NG, GLA_GATE_RANK, GLA_KEY_DIM), GLA_GATE_RANK ** -0.5),
        'gla_b_gate_f': nrm(ks[5], (NG, GLA_KEY_DIM), 0.1),
        'gla_w_gate_up_b': nrm(ks[6], (NG, GLA_GATE_RANK, GLA_KEY_DIM), GLA_GATE_RANK ** -0.5),
        'gla_b_gate_b': nrm(ks[7], (NG, GLA_KEY_DIM), 0.1),
        'gla_norm': 1.0 + nrm(ks[8], (NG, GLA_DV), 0.01),
        'gla_w_out': nrm(ks[9], (NG, GLA_VAL_DIM, D_MODEL), GLA_VAL_DIM ** -0.5),
        'attn_w_qkv': nrm(ks[10], (NA, D_MODEL, ATTN_QKV_DIM), D_MODEL ** -0.5),
        'attn_q_norm': 1.0 + nrm(ks[11], (NA, ATTN_HEAD_DIM), 0.01),
        'attn_k_norm': 1.0 + nrm(ks[12], (NA, ATTN_HEAD_DIM), 0.01),
        'attn_w_out': nrm(ks[13], (NA, ATTN_Q_HEADS * ATTN_HEAD_DIM, D_MODEL),
                          (ATTN_Q_HEADS * ATTN_HEAD_DIM) ** -0.5),
        'ffn_w_up': nrm(ks[14], (DEPTH, D_MODEL, 2 * D_FF), D_MODEL ** -0.5),
        'ffn_w_conv': nrm(ks[15], (DEPTH, CONV_WIDTH, 2 * D_FF), CONV_WIDTH ** -0.5),
        'ffn_b_conv': nrm(ks[16], (DEPTH, 2 * D_FF), 0.01),
        'ffn_w_down': nrm(ks[17], (DEPTH, D_FF, D_MODEL), D_FF ** -0.5),
    }

def first_block(x, norm_mix, norm_ffn, gla_w_in, gla_w_gate_up_f, gla_b_gate_f,
              gla_w_gate_up_b, gla_b_gate_b, gla_norm, gla_w_out,
              attn_w_qkv, attn_q_norm, attn_k_norm, attn_w_out,
              ffn_w_up, ffn_w_conv, ffn_b_conv, ffn_w_down):
    S = x.shape[1]
    rows = S // GRID_W
    f32 = jnp.float32
    row_idx = jnp.repeat(jnp.arange(rows, dtype=f32), GRID_W)
    col_idx = jnp.tile(jnp.arange(GRID_W, dtype=f32), rows)
    inv_freq = ROPE_THETA ** (-jnp.arange(ROPE_PAIRS_PER_AXIS, dtype=f32) / ROPE_PAIRS_PER_AXIS)
    ang = jnp.concatenate([row_idx[:, None] * inv_freq, col_idx[:, None] * inv_freq], axis=-1)
    cos = jnp.cos(ang)[None, :, None, :]
    sin = jnp.sin(ang)[None, :, None, :]

    for i in range(DEPTH):
        h = rmsnorm(x, norm_mix[i])
        j = i // N_MIXERS
        if i % N_MIXERS == 0:
            x = x + gla_mixer(h, gla_w_in[j], gla_w_gate_up_f[j], gla_b_gate_f[j],
                              gla_w_gate_up_b[j], gla_b_gate_b[j], gla_norm[j], gla_w_out[j])
        else:
            x = x + attn_mixer(h, attn_w_qkv[j], attn_q_norm[j], attn_k_norm[j],
                               attn_w_out[j], cos, sin)
        x = x + conv_ffn(rmsnorm(x, norm_ffn[i]), ffn_w_up[i], ffn_w_conv[i],
                         ffn_b_conv[i], ffn_w_down[i])
    return x


DEPTH_2 = 1

MIX_WIDTH = D_MODEL
N_MLSTM_HEADS = 4
MLSTM_HEAD_DIM = 128
MLSTM_WIDTH = N_MLSTM_HEADS * MLSTM_HEAD_DIM
N_SB_HEADS = 8
SB_HEAD_DIM = 64
SB_WIDTH = N_SB_HEADS * SB_HEAD_DIM
CONV_WIDTH_2 = 4
MLSTM_CHUNK = 128
SB_BLOCK = 128
PROJ_WIDTH = 4 * MLSTM_WIDTH + 2 * N_MLSTM_HEADS + 3 * SB_WIDTH
PROJ_SPLITS = (2 * MLSTM_WIDTH, 3 * MLSTM_WIDTH, 4 * MLSTM_WIDTH,
               4 * MLSTM_WIDTH + N_MLSTM_HEADS, 4 * MLSTM_WIDTH + 2 * N_MLSTM_HEADS)
MEM_TOKENS = 256
N_XATTN_HEADS = 4
XATTN_HEAD_DIM = D_MODEL // N_XATTN_HEADS
PEER_HEADS = 8
PEER_N_KEYS = 128
PEER_N_EXPERTS = PEER_N_KEYS * PEER_N_KEYS
PEER_TOPK = 16
PEER_QUERY_DIM = 256
PEER_HALF = PEER_QUERY_DIM // 2
PEER_CHUNK = 128
EPS = 1e-6


def rms_norm(x, g):
    xf = x.astype(jnp.float32)
    y = xf * lax.rsqrt(jnp.mean(xf * xf, axis=-1, keepdims=True) + EPS) * g.astype(jnp.float32)
    return y.astype(x.dtype)

def head_rms_norm(a, g):
    H, dh = a.shape[1], a.shape[3]
    y = a * lax.rsqrt(jnp.mean(a * a, axis=-1, keepdims=True) + EPS)
    return y * g.astype(jnp.float32).reshape(H, 1, dh)

def split_heads(a, n):
    B_, S, W = a.shape
    return a.reshape(B_, S, n, W // n).transpose(0, 2, 1, 3)

def merge_heads(a):
    B_, H, S, dh = a.shape
    return a.transpose(0, 2, 1, 3).reshape(B_, S, H * dh)

def causal_depthwise_conv(a, w, b):
    C = a.shape[-1]
    out = lax.conv_general_dilated(a, w[:, None, :].astype(a.dtype), window_strides=(1,),
                                   padding=[(CONV_WIDTH_2 - 1, 0)],
                                   dimension_numbers=('NWC', 'WIO', 'NWC'),
                                   feature_group_count=C)
    return out + b.astype(a.dtype)

def mlstm_chunkwise(q, k, v, log_i, log_f):
    B_, H, S, dh = q.shape
    L = MLSTM_CHUNK
    nc = S // L

    def to_chunks(a):
        return jnp.moveaxis(a.reshape(B_, H, nc, L, *a.shape[3:]), 2, 0)

    xs = (to_chunks(q), to_chunks(k), to_chunks(v), to_chunks(log_i), to_chunks(log_f))
    causal = jnp.tril(jnp.ones((L, L), dtype=bool))

    def step(carry, inp):
        C, n, m = carry
        qb, kb, vb, ib, fb = inp
        b = jnp.cumsum(fb, axis=-1)
        g = b + m[..., None]
        Dm = jnp.where(causal, b[..., :, None] - b[..., None, :] + ib[..., None, :], -jnp.inf)
        m_t = jnp.maximum(g, jnp.max(Dm, axis=-1))
        W = jnp.exp(Dm - m_t[..., None])
        inter = jnp.exp(g - m_t)
        qk = jnp.einsum('bhtd,bhsd->bhts', qb, kb) * W
        num = inter[..., None] * jnp.einsum('bhvk,bhtk->bhtv', C, qb) + jnp.einsum('bhts,bhsv->bhtv', qk, vb)
        den = inter * jnp.einsum('bhk,bhtk->bht', n, qb) + jnp.sum(qk, axis=-1)
        h = num / jnp.maximum(jnp.abs(den), jnp.exp(-m_t))[..., None]
        F = b[..., -1]
        a = F[..., None] - b + ib
        m_new = jnp.maximum(F + m, jnp.max(a, axis=-1))
        decay = jnp.exp(F + m - m_new)
        w_s = jnp.exp(a - m_new[..., None])
        C_new = decay[..., None, None] * C + jnp.einsum('bhsv,bhsk->bhvk', vb * w_s[..., None], kb)
        n_new = decay[..., None] * n + jnp.einsum('bhs,bhsk->bhk', w_s, kb)
        return (C_new, n_new, m_new), h

    init = (jnp.zeros((B_, H, dh, dh), jnp.float32), jnp.zeros((B_, H, dh), jnp.float32),
            jnp.zeros((B_, H), jnp.float32))
    _, hs = lax.scan(step, init, xs)
    return jnp.moveaxis(hs, 0, 2).reshape(B_, H, S, dh)

def stick_breaking_attention(q, k, v):
    B_, H, S, dh = q.shape
    L = SB_BLOCK
    scale = dh ** -0.5
    outs = []
    for blk in range(S // L):
        n_prefix = (blk + 1) * L
        q_blk = q[:, :, blk * L:(blk + 1) * L]
        k_pre = k[:, :, :n_prefix]
        v_pre = v[:, :, :n_prefix]
        z = jnp.einsum('bhtd,bhsd->bhts', q_blk, k_pre) * scale
        t_idx = blk * L + jnp.arange(L)[:, None]
        s_idx = jnp.arange(n_prefix)[None, :]
        strict = s_idx < t_idx
        log_1m_beta = jnp.where(strict, jax.nn.log_sigmoid(-z), 0.0)
        log_a = z + lax.cumsum(log_1m_beta, axis=3, reverse=True)
        A = jnp.exp(jnp.where(strict, log_a, -jnp.inf))
        outs.append(jnp.einsum('bhts,bhsd->bhtd', A, v_pre))
    return jnp.concatenate(outs, axis=2)

def parallel_mixer(h, w_in, conv_w, conv_b, igate_b, fgate_b, mlstm_norm_g, sb_norm_g, w_out):
    dtype = h.dtype
    f32 = jnp.float32
    proj = h @ w_in
    qk_m, v_m, o_m, i_pre, f_pre, qkv_s = jnp.split(proj, PROJ_SPLITS, axis=-1)
    qk_m = jax.nn.silu(causal_depthwise_conv(qk_m, conv_w, conv_b))
    q_m, k_m = jnp.split(qk_m, 2, axis=-1)
    q_m = split_heads(q_m, N_MLSTM_HEADS).astype(f32)
    k_m = split_heads(k_m, N_MLSTM_HEADS).astype(f32) * (MLSTM_HEAD_DIM ** -0.5)
    v_m = split_heads(v_m, N_MLSTM_HEADS).astype(f32)
    log_i = jnp.swapaxes((i_pre + igate_b).astype(f32), 1, 2)
    log_f = jax.nn.log_sigmoid(jnp.swapaxes((f_pre + fgate_b).astype(f32), 1, 2))
    h_m = mlstm_chunkwise(q_m, k_m, v_m, log_i, log_f)
    h_m = jax.nn.sigmoid(split_heads(o_m, N_MLSTM_HEADS).astype(f32)) * h_m
    h_m = head_rms_norm(h_m, mlstm_norm_g)
    q_s, k_s, v_s = jnp.split(qkv_s, 3, axis=-1)
    h_s = stick_breaking_attention(split_heads(q_s, N_SB_HEADS).astype(f32),
                                   split_heads(k_s, N_SB_HEADS).astype(f32),
                                   split_heads(v_s, N_SB_HEADS).astype(f32))
    h_s = head_rms_norm(h_s, sb_norm_g)
    mixed = jnp.concatenate([merge_heads(h_m), merge_heads(h_s)], axis=-1).astype(dtype)
    return mixed @ w_out

def memory_cross_attention(h, mem_n, wq, wkv, wo):
    B_, S, _ = h.shape
    M = mem_n.shape[1]
    q = (h @ wq).reshape(B_, S, N_XATTN_HEADS, XATTN_HEAD_DIM).astype(jnp.float32)
    k, v = jnp.split(mem_n @ wkv, 2, axis=-1)
    k = k.reshape(B_, M, N_XATTN_HEADS, XATTN_HEAD_DIM).astype(jnp.float32)
    v = v.reshape(B_, M, N_XATTN_HEADS, XATTN_HEAD_DIM).astype(jnp.float32)
    p = jax.nn.softmax(jnp.einsum('bshd,bmhd->bhsm', q, k) * (XATTN_HEAD_DIM ** -0.5), axis=-1)
    o = jnp.einsum('bhsm,bmhd->bshd', p, v).reshape(B_, S, N_XATTN_HEADS * XATTN_HEAD_DIM)
    return o.astype(h.dtype) @ wo

def peer_ffn(h, wq, subkeys, u, v):
    B_, S, D = h.shape
    T = B_ * S
    xt = h.reshape(T, D)
    q = (xt @ wq).reshape(T, PEER_HEADS, 2, PEER_HALF)
    s = jnp.einsum('thpc,hpnc->thpn', q, subkeys).astype(jnp.float32)
    s_top, i_top = lax.top_k(s, PEER_TOPK)
    cand = s_top[:, :, 0, :, None] + s_top[:, :, 1, None, :]
    cand_idx = i_top[:, :, 0, :, None] * PEER_N_KEYS + i_top[:, :, 1, None, :]
    best, pos = lax.top_k(cand.reshape(T, PEER_HEADS, PEER_TOPK * PEER_TOPK), PEER_TOPK)
    experts = jnp.take_along_axis(cand_idx.reshape(T, PEER_HEADS, PEER_TOPK * PEER_TOPK), pos, axis=-1)
    gates = jax.nn.softmax(best, axis=-1).astype(h.dtype)
    nb = T // PEER_CHUNK
    E = PEER_HEADS * PEER_TOPK

    def block(args):
        xb, eb, gb = args
        ub = u[eb]
        vb = v[eb]
        act = jax.nn.gelu(jnp.einsum('cd,ced->ce', xb, ub), approximate=False) * gb
        return jnp.einsum('ce,ced->cd', act, vb)

    y = lax.map(block, (xt.reshape(nb, PEER_CHUNK, D), experts.reshape(nb, PEER_CHUNK, E),
                        gates.reshape(nb, PEER_CHUNK, E)))
    return y.reshape(B_, S, D)

def second_inputs(seed: int = 0) -> dict:
    key = jax.random.key(seed)
    ks = jax.random.split(key, 24)
    f32 = jnp.float32

    def nrm(k, shape, scale):
        return jax.random.normal(k, shape, f32) * scale

    def gain(k, shape):
        return 1.0 + 0.02 * jax.random.normal(k, shape, f32)

    return {
        'x': nrm(ks[0], (BATCH, SEQ, D_MODEL), 1.0),
        'mem': nrm(ks[1], (BATCH, MEM_TOKENS, D_MODEL), 1.0),
        'mix_norm_g': gain(ks[2], (DEPTH_2, D_MODEL)),
        'w_in': nrm(ks[3], (DEPTH_2, D_MODEL, PROJ_WIDTH), D_MODEL ** -0.5),
        'conv_w': nrm(ks[4], (DEPTH_2, CONV_WIDTH_2, 2 * MLSTM_WIDTH), CONV_WIDTH_2 ** -0.5),
        'conv_b': nrm(ks[5], (DEPTH_2, 2 * MLSTM_WIDTH), 0.02),
        'igate_b': nrm(ks[6], (DEPTH_2, N_MLSTM_HEADS), 0.1),
        'fgate_b': jnp.linspace(3.0, 6.0, N_MLSTM_HEADS, dtype=f32)[None, :] + nrm(ks[7], (DEPTH_2, N_MLSTM_HEADS), 0.1),
        'mlstm_norm_g': gain(ks[8], (DEPTH_2, MLSTM_WIDTH)),
        'sb_norm_g': gain(ks[9], (DEPTH_2, SB_WIDTH)),
        'w_out': nrm(ks[10], (DEPTH_2, MIX_WIDTH, D_MODEL), MIX_WIDTH ** -0.5),
        'xattn_norm_g': gain(ks[11], (DEPTH_2, D_MODEL)),
        'mem_norm_g': gain(ks[12], (DEPTH_2, D_MODEL)),
        'xattn_wq': nrm(ks[13], (DEPTH_2, D_MODEL, D_MODEL), D_MODEL ** -0.5),
        'xattn_wkv': nrm(ks[14], (DEPTH_2, D_MODEL, 2 * D_MODEL), D_MODEL ** -0.5),
        'xattn_wo': nrm(ks[15], (DEPTH_2, D_MODEL, D_MODEL), D_MODEL ** -0.5),
        'ffn_norm_g': gain(ks[16], (DEPTH_2, D_MODEL)),
        'peer_wq': nrm(ks[17], (DEPTH_2, D_MODEL, PEER_HEADS * PEER_QUERY_DIM), D_MODEL ** -0.5),
        'peer_subkeys': nrm(ks[18], (DEPTH_2, PEER_HEADS, 2, PEER_N_KEYS, PEER_HALF), PEER_HALF ** -0.5),
        'peer_u': nrm(ks[19], (DEPTH_2, PEER_N_EXPERTS, D_MODEL), D_MODEL ** -0.5),
        'peer_v': nrm(ks[20], (DEPTH_2, PEER_N_EXPERTS, D_MODEL), (PEER_HEADS * PEER_TOPK) ** -0.5),
        'final_norm_g': gain(ks[21], (D_MODEL,)),
    }

def second_block(x, mem, mix_norm_g, w_in, conv_w, conv_b, igate_b, fgate_b, mlstm_norm_g, sb_norm_g,
              w_out, xattn_norm_g, mem_norm_g, xattn_wq, xattn_wkv, xattn_wo, ffn_norm_g, peer_wq,
              peer_subkeys, peer_u, peer_v, final_norm_g):
    for l in range(DEPTH_2):
        x = x + parallel_mixer(rms_norm(x, mix_norm_g[l]), w_in[l], conv_w[l], conv_b[l], igate_b[l],
                               fgate_b[l], mlstm_norm_g[l], sb_norm_g[l], w_out[l])
        x = x + memory_cross_attention(rms_norm(x, xattn_norm_g[l]), rms_norm(mem, mem_norm_g[l]),
                                       xattn_wq[l], xattn_wkv[l], xattn_wo[l])
        x = x + peer_ffn(rms_norm(x, ffn_norm_g[l]), peer_wq[l], peer_subkeys[l], peer_u[l], peer_v[l])
    return rms_norm(x, final_norm_g)


def setup_inputs(seed=0):
    out = dict(first_inputs(seed))
    for name, value in second_inputs(seed + 1).items():
        if name != "x":
            out[name + "_2"] = value
    return out


def reference(
    x, norm_mix, norm_ffn, gla_w_in, gla_w_gate_up_f, gla_b_gate_f, gla_w_gate_up_b,
    gla_b_gate_b, gla_norm, gla_w_out, attn_w_qkv, attn_q_norm, attn_k_norm, attn_w_out,
    ffn_w_up, ffn_w_conv, ffn_b_conv, ffn_w_down, mem_2, mix_norm_g_2, w_in_2, conv_w_2,
    conv_b_2, igate_b_2, fgate_b_2, mlstm_norm_g_2, sb_norm_g_2, w_out_2, xattn_norm_g_2,
    mem_norm_g_2, xattn_wq_2, xattn_wkv_2, xattn_wo_2, ffn_norm_g_2, peer_wq_2, peer_subkeys_2,
    peer_u_2, peer_v_2, final_norm_g_2,
):
    x = first_block(
        x, norm_mix, norm_ffn, gla_w_in, gla_w_gate_up_f, gla_b_gate_f, gla_w_gate_up_b,
        gla_b_gate_b, gla_norm, gla_w_out, attn_w_qkv, attn_q_norm, attn_k_norm, attn_w_out,
        ffn_w_up, ffn_w_conv, ffn_b_conv, ffn_w_down,
    )
    return second_block(
        x, mem_2, mix_norm_g_2, w_in_2, conv_w_2, conv_b_2, igate_b_2, fgate_b_2,
        mlstm_norm_g_2, sb_norm_g_2, w_out_2, xattn_norm_g_2, mem_norm_g_2, xattn_wq_2,
        xattn_wkv_2, xattn_wo_2, ffn_norm_g_2, peer_wq_2, peer_subkeys_2, peer_u_2, peer_v_2,
        final_norm_g_2,
    )


_drawn_inputs = setup_inputs


def setup_inputs(seed=0):
    import zlib

    import numpy as np

    out = dict(_drawn_inputs(seed))
    spreads = {}
    factors = {'norm_mix': 3.595,
     'norm_ffn': 4.75,
     'gla_norm': 7.672,
     'attn_q_norm': 8.0,
     'attn_k_norm': 8.0,
     'ffn_b_conv': 4.468,
     'mix_norm_g_2': 3.25,
     'conv_b_2': 49.152,
     'igate_b_2': 200.0,
     'mlstm_norm_g_2': 53.824,
     'sb_norm_g_2': 59.496,
     'xattn_norm_g_2': 8.0,
     'mem_norm_g_2': 8.0,
     'ffn_norm_g_2': 64.0,
     'final_norm_g_2': 22.894}
    for name, (base, spread) in spreads.items():
        noise = np.random.default_rng([zlib.crc32(name.encode()), seed]).standard_normal(out[name].shape)
        drawn = base * np.exp(spread * noise) if base else spread * noise
        out[name] = __import__('jax').numpy.asarray(drawn.astype(out[name].dtype))
    for name, factor in factors.items():
        out[name] = (out[name] * factor).astype(out[name].dtype)
    return out
```

```python
from contextlib import ExitStack

import concourse.bass as bass
from concourse import mybir

ALU = mybir.AluOpType
ACT = mybir.ActivationFunctionType
F32 = mybir.dt.float32
F32R = mybir.dt.float32r
U32 = mybir.dt.uint32
AX_X = mybir.AxisListType.X

P = 128
S = 512
TT = S // P
D = 1024
KD = D // P
EPS = 1e-6
LOWEST = -3.4028234e38

RING = 3
UNIT = 1024

GLA_H, GLA_DV, GLA_C = 4, 256, 64
GLA_SCALE = 128 ** -0.5
FF = 2816
FF_TILES = FF // P
FF_GROUP = FF_TILES // 2
AT_H, AT_KV = 8, 2
AT_SCALE = 128 ** -0.5
ML_H = 4
ML_SCALE = 128 ** -0.5
SB_H, SB_D = 8, 64
SB_SCALE = 64 ** -0.5
XA_H = 4
XA_SCALE = 256 ** -0.5
MEM_T = 2
PH, TOPK = 8, 16
NKEY = 128
PG = 12
PEER_LOOPS = NKEY // PG
PEER_TAIL = NKEY - PEER_LOOPS * PG

CONST = {}
PARAM = {}


def _lay(table, sizes):
    at = 0
    for name, size in sizes:
        table[name] = (at, size)
        at += size
    return at


N_CONST = _lay(CONST, [("ident", 128), ("negtri", 128), ("negones", 128), ("iota", 128), ("reset64", 512),
                       ("reset128", 512), ("causal", 128), ("strict", 128), ("cos", 256), ("sin", 256),
                       ("sel", 512)])
N_PARAM = _lay(PARAM, [("norm_mix", 16), ("norm_ffn", 16), ("gla_b_f", 4), ("gla_b_b", 4), ("gla_norm", 8),
                       ("mix_norm", 8), ("head_gain", 8), ("xattn_norm", 8), ("mem_norm", 8), ("ffn_norm_2", 8),
                       ("conv2_w", 32), ("conv2_b", 8), ("igate", 1), ("fgate", 1),
                       ("q_norm", 128), ("k_norm", 128)])


class Place:

    def __init__(self):
        self.unit = 0
        self.tjob = 0
        self.njob = 0
        self.nready = 0
        self.tr = 0
        self.norm = 0
        self.phase = 0
        self.ffn = 0
        self.sc = 0
        self.pv = 0
        self.loop = None


def build(nc, T, out, stop=None, NU=0):
    ctx = ExitStack()
    with ctx:
        def sb(name, shape, dt=F32, where=ctx):
            return where.enter_context(nc.sbuf_tensor(name, shape, dt))

        def sem(name):
            return ctx.enter_context(nc.semaphore(name))

        X = sb("X", [P, TT, D])
        hT_hi = sb("hT_hi", [P, KD, S], F32R)
        hT_lo = sb("hT_lo", [P, KD, S], F32R)
        w_raw = sb("w_raw", [P, RING, UNIT])
        w_hi = sb("w_hi", [P, RING, UNIT], F32R)
        w_lo = sb("w_lo", [P, RING, UNIT], F32R)
        cst = sb("cst", [P, N_CONST])
        par = sb("par", [P, N_PARAM])
        zero = sb("zero", [P, 1])
        gmask = sb("gmask", [P, 2, P], U32)
        stat = sb("stat", [P, 192])
        idxT = sb("idxT", [P, 3, S])

        def C(name):
            a, n = CONST[name]
            return cst[:, a:a + n]

        def PR(name, i=0, n=1):
            a, _ = PARAM[name]
            return par[:, a + i:a + i + n]

        ident = C("ident")

        def overlay(*tensors):
            group = ExitStack()
            got = [sb(*t, where=group) if len(t) == 3 else sb(*t, F32, group) for t in tensors]
            group.close()
            return got

        wup = sb("wup", [P, S])
        XN, = overlay(("XN", [P, TT, D]))
        q1, k1, v1, g1, r1, la, bb, qd, ki, ke, keN, St, att, dch = overlay(
            ("gla_q", [P, 4, S]), ("gla_k", [P, 4, S]), ("gla_v", [P, TT, D]), ("gla_g", [P, TT, D]),
            ("gla_r", [P, 2, S]), ("gla_la", [P, S]), ("gla_b", [P, 2, S]), ("gla_qd", [P, 2, S]),
            ("gla_ki", [P, 2, S]), ("gla_ke", [P, 2, S]), ("gla_keN", [P, 2, S]),
            ("gla_state", [P, 2, 8, GLA_DV]), ("gla_att", [P, 2, S]), ("gla_dch", [P, 2, 8]))
        act_hi, act_lo, cw, cb, yv, yg, yw, ys = overlay(
            ("act_hi", [P, PG, S], F32R), ("act_lo", [P, PG, S], F32R), ("ffn_cw", [P, 3 * 2 * FF_TILES]),
            ("ffn_cb", [P, 2 * FF_TILES]), ("ffn_yv", [P, S]), ("ffn_yg", [P, S]), ("ffn_w", [P, S]),
            ("ffn_s", [P, S]))
        qkv, qn, qr, qT, kT = overlay(
            ("at_qkv", [P, TT, 1536]), ("at_qn", [P, TT, 1280]), ("at_qr", [P, TT, 1280]), ("at_qT", [P, AT_H, S]),
            ("at_kT", [P, AT_KV, S]))
        at_pb = qn[:, 0, 0:2 * S].rearrange("p (b x) -> p b x", b=2)
        at_pT = qn[:, :, :].rearrange("p t x -> p (t x)")[:, 2 * S:10 * S].rearrange("p (b k x) -> p b k x", b=2, k=TT)
        mixg = ExitStack()
        ml_q = sb("ml_q", [P, 4, S], F32, mixg)
        ml_k = sb("ml_k", [P, 4, S], F32, mixg)
        sb_q = sb("sb_q", [P, 4, S], F32, mixg)
        sb_k = sb("sb_k", [P, 4, S], F32, mixg)
        vx = sb("ml_v", [P, TT, ML_H, P + 1], F32, mixg)
        og = sb("ml_o", [P, TT, S], F32, mixg)
        sb_v = sb("sb_v", [P, TT, S], F32, mixg)
        mixed = sb("mixed", [P, TT, D], F32, mixg)
        sub = ExitStack()
        rows = sb("ml_rows", [4, 6, S], F32, sub)
        cols = sb("ml_cols", [P, 64], F32, sub)
        dec = sb("ml_dec", [P, 16], F32, sub)
        kw = sb("ml_kw", [P, TT, P], F32, sub)
        cT = sb("ml_state", [P, 4, P + 1], F32, sub)
        wT = sb("ml_wT", [P, S], F32, sub)
        aT = sb("ml_aT", [P, S], F32, sub)
        nd = sb("ml_nd", [P, TT, P + 1], F32, sub)
        mp = sb("ml_mp", [4, 16], F32, sub)
        sub.close()
        sub = ExitStack()
        stT = sb("st_T", [P, TT, S], F32, sub)
        stL = sb("st_L", [P, TT, S], F32, sub)
        stA = sb("st_A", [P, TT, S], F32, sub)
        sub.close()
        mixg.close()
        mem, xq, xk, xv, xp, xpT = overlay(
            ("mem", [P, MEM_T, D]), ("xa_q", [P, KD, S]), ("xa_k", [P, KD, 256]), ("xa_v", [P, MEM_T, D]),
            ("xa_p", [P, 2, 256]), ("xa_pT", [P, 2, MEM_T, S]))
        rq, rs, subT, tv, ti, tif, srep, cand, crep, best, pos, ab, abf, eqt, sel_ij = overlay(
            ("ro_q", [P, 2, S]), ("ro_s", [P, TT, 16, NKEY]), ("ro_subkeys", [P, 16 * NKEY]),
            ("ro_top", [P, 16, TOPK]), ("ro_idx", [P, 16, TOPK], U32), ("ro_idxf", [P, 16, TOPK]),
            ("ro_rep", [P, NKEY]), ("ro_cand", [P, PH, TOPK * TOPK]), ("ro_crep", [P, TOPK * TOPK]),
            ("ro_best", [P, PH, TOPK]), ("ro_pos", [P, PH, TOPK], U32), ("ro_ab", [P, 2, PH * TOPK], U32),
            ("ro_abf", [P, 2, PH * TOPK]), ("ro_eq", [P, PH * TOPK * TOPK]), ("ro_sel", [P, 3, P]))
        stage, ohI, ohJ = overlay(("g_stage", [P, 2, NKEY, 64]), ("g_ohI", [P, 8, P]), ("g_ohJ", [P, 8, P]))
        _, _, gt, ga, gw = overlay(("act_hi2", [P, PG, S], F32R), ("act_lo2", [P, PG, S], F32R),
                                   ("g_tile", [P, 4, S]), ("g_act", [P, 2, S]), ("g_w", [P, 2, S]))
        fgain, fout = overlay(("final_gain", [P, D]), ("final_out", [P, TT, D]))

        PS = [ctx.enter_context(nc.psum_tensor(f"bank{i}", [P, 512], F32)) for i in range(8)]
        gates = nc.dram_tensor("gates", [NKEY, P, S], F32, kind="Internal").ap()

        raw_landed = [sem(f"raw_landed{i}") for i in range(RING)]
        w_hi_done = sem("w_hi_done")
        w_split = sem("w_split")
        w_used = sem("w_used")
        t_free = sem("t_free")
        n_ready = sem("n_ready")
        n_free = sem("n_free")
        tr_ready = sem("tr_ready")
        tr_hi = sem("tr_hi")
        tr_free = sem("tr_free")
        ss_ready = sem("ss_ready")
        ms_ready = sem("ms_ready")
        sd_ready = sem("sd_ready")
        xn_ready = sem("xn_ready")
        phase_done = sem("phase_done")
        a_chain = sem("a_chain")
        v_chain = sem("v_chain")
        c_in = sem("c_in")
        p_in = sem("p_in")
        x_in = sem("x_in")
        o_sem = sem("out_stored")
        zero_set = sem("zero_set")

        class Chain:

            def __init__(self, eng, s):
                self.eng, self.s, self.n = eng, s, 0

            def link(self, ins):
                self.n += 1
                ins.then_inc(self.s, 1)
                self.eng.wait_ge(self.s, self.n)

        def phase_over(eng, at):
            at.phase += 1
            eng.drain().then_inc(phase_done, 1)
            eng.wait_ge(phase_done, 3 * at.phase)

        def parts3(wh, wl, hh, hl):
            return ((wh, hh), (wh, hl), (wl, hh))

        def pe_t_unit(pe, at, n=S):
            s = at.unit % RING
            pe.wait_ge(w_split, at.unit + 1 if at.loop is None else at.loop * (2 * PG) + (at.unit + 1))
            if at.tjob >= 2:
                pe.wait_ge(t_free, at.tjob - 1 if at.loop is None else at.loop * PG + (at.tjob - 1))
            bank = PS[at.tjob % 2]
            for k in range(KD):
                for i, (w, h) in enumerate(parts3(w_hi, w_lo, hT_hi, hT_lo)):
                    mm = nc.tensor.matmul(bank[:, 0:n], w[:, s, k * P:(k + 1) * P], h[:, k, 0:n],
                                          start=(k == 0 and i == 0), stop=(k == KD - 1 and i == 2))
            mm.then_inc(w_used, 1)
            at.unit += 1
            at.tjob += 1

        def n_shape(at, K, nbs, toks):
            ends = []
            for nb in range(nbs):
                last = (nb + 1) * K - 1
                ends.append((at.unit + last // 2, last % 2 == 1))
            return ends

        def pe_n_pass(pe, at, hi, lo, K, nbs, toks=TT, need=None):
            base = at.unit
            ends = n_shape(at, K, nbs, toks)
            lp = (lambda a, m: a) if at.loop is None else (lambda a, m: at.loop * m + a)
            for nb in range(nbs):
                k = 0
                while k < K:
                    h0 = nb * K + k
                    u = base + h0 // 2
                    s = u % RING
                    halves = [(k, h0 % 2)]
                    if h0 % 2 == 0:
                        pe.wait_ge(w_split, lp(u + 1, 2 * PG))
                        if k + 1 < K:
                            halves.append((k + 1, 1))
                    if need and nb == 0:
                        pe.wait_ge(need[0], lp(need[1] + halves[-1][0] + 1, PG))
                    for t in range(toks):
                        if k == 0 and at.njob + nb * toks + t >= toks:
                            pe.wait_ge(n_free, lp(at.njob + nb * toks + t - toks + 1, 8))
                        for kk, part in halves:
                            w0 = part * 512
                            for i, (h, w) in enumerate(((hi, w_hi), (hi, w_lo), (lo, w_hi))):
                                mm = nc.tensor.matmul(PS[4 + t][:, :], h[:, kk, t * P:(t + 1) * P],
                                                      w[:, s, w0:w0 + 512],
                                                      start=(kk == 0 and i == 0), stop=(kk == K - 1 and i == 2))
                        whole = halves[-1][1] == 1
                        if t == toks - 1 and whole:
                            mm.then_inc(w_used, 1)
                        elif halves[-1][0] == K - 1:
                            mm.then_inc(n_ready, 1)
                    k = halves[-1][0] + 1
            n_advance(at, K, nbs, toks)

        def n_advance(at, K, nbs, toks):
            for u, whole in n_shape(at, K, nbs, toks):
                at.nready += toks - 1 if whole else toks
            at.unit += nbs * K // 2
            at.njob += nbs * toks

        def n_results(eng, at, K, nbs, toks=TT):
            lp = (lambda a, m: a) if at.loop is None else (lambda a, m: at.loop * m + a)
            seen = at.nready
            for nb, (u, whole) in enumerate(n_shape(at, K, nbs, toks)):
                for t in range(toks):
                    if t == toks - 1 and whole:
                        eng.wait_ge(w_used, lp(u + 1, 2 * PG))
                    else:
                        seen += 1
                        eng.wait_ge(n_ready, lp(seen, 6))
                    yield nb, t
            n_advance(at, K, nbs, toks)

        def t_result(eng, at):
            eng.wait_ge(w_used, at.unit + 1 if at.loop is None else at.loop * (2 * PG) + (at.unit + 1))
            bank = PS[at.tjob % 2]
            at.unit += 1
            at.tjob += 1
            return bank

        def skip_t(at, n=1):
            at.unit += n
            at.tjob += n

        def pe_transposes(pe, at, src, toks=TT):
            for k in range(KD):
                if at.tr >= 4:
                    pe.wait_ge(tr_free, at.tr - 3)
                for t in range(toks):
                    mm = nc.tensor.transpose(PS[at.tr % 4][:, t * P:(t + 1) * P], src[:, t, k * P:(k + 1) * P], ident)
                mm.then_inc(tr_ready, 1)
                at.tr += 1

        def act_transposed(a, at, gain, toks=TT):
            n = toks * P
            for k in range(KD):
                a.wait_ge(tr_ready, at.tr + 1)
                nc.scalar.activation(hT_hi[:, k, 0:n], PS[at.tr % 4][:, 0:n], ACT.Identity, scale=gain(k)).then_inc(tr_hi, 1)
                at.tr += 1

        def dve_transposed(v, at, gain, toks=TT):
            n = toks * P
            for k in range(KD):
                v.wait_ge(tr_hi, at.tr + 1)
                nc.vector.scalar_tensor_tensor(out=hT_lo[:, k, 0:n], in0=PS[at.tr % 4][:, 0:n], scalar=gain(k),
                                               in1=hT_hi[:, k, 0:n].bitcast(F32), op0=ALU.mult, op1=ALU.subtract).then_inc(tr_free, 1)
                at.tr += 1

        def act_norm(a, at, src, squares, gain, toks=TT):
            for t in range(toks):
                last = nc.scalar.activation(squares[:, t, :], src[:, t, :], ACT.Square, accum_out=stat[:, t:t + 1])
            last.then_inc(ss_ready, 1)
            a.wait_ge(ms_ready, at.norm + 1)
            nc.scalar.activation(stat[:, 8:8 + toks], stat[:, 4:4 + toks], ACT.Sqrt).then_inc(sd_ready, 1)
            at.norm += 1
            act_transposed(a, at, gain, toks)
            phase_over(a, at)

        def dve_norm(v, ch, at, src, dst, gain, toks=TT):
            v.wait_ge(ss_ready, at.norm + 1)
            nc.vector.tensor_scalar(stat[:, 4:4 + toks], stat[:, 0:toks], 1.0 / D, EPS, ALU.mult, ALU.add).then_inc(ms_ready, 1)
            v.wait_ge(sd_ready, at.norm + 1)
            ch.link(nc.vector.reciprocal(stat[:, 12:12 + toks], stat[:, 8:8 + toks]))
            for t in range(toks):
                last = nc.vector.tensor_scalar(dst[:, t, :], src[:, t, :], stat[:, 12 + t:13 + t], None, ALU.mult)
            last.then_inc(xn_ready, 1)
            at.norm += 1
            dve_transposed(v, at, gain, toks)
            phase_over(v, at)

        def pe_norm(pe, at, src, toks=TT):
            at.norm += 1
            pe.wait_ge(xn_ready, at.norm)
            pe_transposes(pe, at, src, toks)
            phase_over(pe, at)

        gl_free = sem("gl_free")
        gl_bank = sem("gl_bank")
        gl_opnd = sem("gl_opnd")
        gl_soft = sem("gl_soft")
        gl_scan = sem("gl_scan")
        gl_diff = sem("gl_diff")
        gl_exp = sem("gl_exp")
        gl_ss = sem("gl_ss")
        gl_ms = sem("gl_ms")
        gl_sd = sem("gl_sd")
        gl_norm = sem("gl_norm")
        ff_y = sem("ff_y")
        ff_s = sem("ff_s")
        ff_w = sem("ff_w")
        ff_h = sem("ff_h")
        ff_ready = sem("ff_ready")
        ff_par = sem("ff_par")
        sc_bank = sem("sc_bank")
        sc_max = sem("sc_max")
        sc_exp = sem("sc_exp")
        sc_norm = sem("sc_norm")
        pt_bank = sem("pt_bank")
        pt_sbuf = sem("pt_sbuf")
        pv_bank = sem("pv_bank")
        oT_hi = sem("oT_hi")
        oT_lo = sem("oT_lo")
        at_rope = sem("at_rope")
        at_bank = sem("at_bank")
        at_sbuf = sem("at_sbuf")
        at_sq = sem("at_sq")
        at_ms = sem("at_ms")
        at_sd = sem("at_sd")
        mx_y = sem("mx_y")
        mx_sq = sem("mx_sq")
        mx_ms = sem("mx_ms")
        mx_sd = sem("mx_sd")
        mx_norm = sem("mx_norm")
        ml_soft = sem("ml_soft")
        ml_arg = sem("ml_arg")
        ml_rexp = sem("ml_rexp")
        ml_bc = sem("ml_bc")
        ml_qk = sem("ml_qk")
        ml_kt = sem("ml_kt")
        ml_kw = sem("ml_kw")
        ml_upd = sem("ml_upd")
        ml_A = sem("ml_A")
        ml_intra = sem("ml_intra")
        ml_st = sem("ml_st")
        ml_inter = sem("ml_inter")
        ml_diff = sem("ml_diff")
        ml_wexp = sem("ml_wexp")
        ml_nd = sem("ml_nd")
        ml_out = sem("ml_out")
        st_z = sem("st_z")
        st_L = sem("st_L")
        st_A = sem("st_A")
        st_o = sem("st_o")
        st_of = sem("st_of")
        st_r = sem("st_r")
        st_ln = sem("st_ln")
        st_min = sem("st_min")
        st_exp = sem("st_exp")
        m_in = sem("m_in")
        ro_bank = sem("ro_bank")
        ro_sbuf = sem("ro_sbuf")
        ro_gate = sem("ro_gate")
        ro_tr = sem("ro_tr")
        ro_arg = sem("ro_arg")
        ro_exp = sem("ro_exp")
        ro_idx_in = sem("ro_idx_in")
        oh_ready = sem("oh_ready")
        oh_used = sem("oh_used")
        g_evac = sem("g_evac")
        peer_w = sem("peer_w")
        peer_h = sem("peer_h")
        peer_ready = sem("peer_ready")
        fin = sem("fin")
        g_out = [sem(f"g_out{i}") for i in range(2)]
        g_in = [sem(f"g_in{i}") for i in range(4)]

        GJ = 16

        def gla_pe(pe, at):
            for _ in range(10):
                pe_t_unit(pe, at)
            pe_n_pass(pe, at, hT_hi, hT_lo, KD, 4)
            phase_over(pe, at)
            for h in range(GLA_H):
                job = [GJ * h]

                def bank():
                    if job[0] >= 8:
                        pe.wait_ge(gl_free, job[0] - 7)
                    job[0] += 1
                    return PS[(job[0] - 1) % 8]

                for d in range(2):
                    b = bank()
                    nc.tensor.matmul(b[:, :], wup[32 * d:32 * d + 16, h * P:(h + 1) * P], r1[32 * d:32 * d + 16, d, :],
                                     start=True, stop=True).then_inc(gl_bank, 1)
                for d in range(2):
                    pe.wait_ge(gl_opnd, 2 * h + d + 1)
                    b = bank()
                    for t in range(TT):
                        mm = nc.tensor.transpose(b[:, t * P:(t + 1) * P], ke[:, d, t * P:(t + 1) * P], ident)
                    mm.then_inc(gl_bank, 1)
                for d in range(2):
                    b = bank()
                    for t in range(TT):
                        c = slice(t * P, (t + 1) * P)
                        mm = nc.tensor.matmul(b[:, c], ki[:, d, c], qd[:, d, c], start=True, stop=True)
                    mm.then_inc(gl_bank, 1)
                for d in range(2):
                    pe.wait_ge(gl_free, GJ * h + 3 + d)
                    for j in range(4):
                        b = bank()
                        for half, c in enumerate(gla_chunks(d, j)):
                            r = slice((c % 2) * 64, (c % 2) * 64 + 64)
                            mm = nc.tensor.matmul(b[:, half * 256:half * 256 + 256], keN[r, d, (c // 2) * P:(c // 2 + 1) * P],
                                                  v1[r, c // 2, h * 256:(h + 1) * 256], start=True, stop=True)
                        mm.then_inc(gl_bank, 1)
                pe.wait_ge(gl_free, GJ * h + 14)
                for j in range(2):
                    b = bank()
                    for e in range(2):
                        t = 2 * j + e
                        o = slice(e * 256, e * 256 + 256)
                        for d in range(2):
                            nc.tensor.matmul(b[:, o], att[:, d, t * P:(t + 1) * P], v1[:, t, h * 256:(h + 1) * 256],
                                             start=(d == 0), stop=False)
                        for c in (2 * t, 2 * t + 1):
                            rows_ = slice((c % 2) * 64, (c % 2) * 64 + 64)
                            ds_ = [d for d in range(2) if (c > 0, c < 7)[d]]
                            for d in ds_:
                                mm = nc.tensor.matmul(b[rows_, o], qd[:, d, c * 64:(c + 1) * 64], St[:, d, c, :],
                                                      start=False, stop=(d == ds_[-1]))
                    mm.then_inc(gl_bank, 1)
            pe.wait_ge(gl_norm, 1)
            pe_transposes(pe, at, v1)
            phase_over(pe, at)
            pe_n_pass(pe, at, hT_hi, hT_lo, KD, 2)
            phase_over(pe, at)

        def gla_chunks(d, j):
            seq = list(range(0, 7)) if d == 0 else list(range(7, 0, -1))
            return seq[4 * (j // 2) + j % 2:4 * (j // 2) + 4:2]

        def gla_act(a, ch, at):
            for i in range(10):
                b = t_result(a, at)
                if i < 4:
                    dst, src = q1[:, i, :], b[:, :]
                elif i < 8:
                    dst, src = k1[:, i - 4, :], b[:, :]
                else:
                    d = i - 8
                    dst, src = r1[32 * d:32 * d + 16, d, :], b[32 * d:32 * d + 16, :]
                nc.scalar.activation(dst, src, ACT.Copy).then_inc(t_free, 1)
            for nb, t in n_results(a, at, KD, 4):
                dst = (v1 if nb < 2 else g1)[:, t, (nb % 2) * 512:(nb % 2) * 512 + 512]
                nc.scalar.activation(dst, PS[4 + t][:, :], ACT.Copy).then_inc(n_free, 1)
            phase_over(a, at)
            for h in range(GLA_H):
                for d in range(2):
                    n = 2 * h + d
                    bias = PR(("gla_b_f", "gla_b_b")[d], h)
                    a.wait_ge(gl_bank, GJ * h + d + 1)
                    if h:
                        a.wait_ge(gl_bank, GJ * h)
                    ch.link(nc.scalar.activation(bb[:, d, :], PS[(GJ * h + d) % 8][:, :], ACT.Abs, bias=bias))
                    ch.link(nc.scalar.activation(bb[:, d, :], bb[:, d, :], ACT.Exp, scale=-1.0))
                    nc.scalar.activation(bb[:, d, :], bb[:, d, :], ACT.Ln, bias=1.0).then_inc(gl_soft, 1)
                    a.wait_ge(gl_scan, n + 1)
                    nc.scalar.activation(qd[:, d, :], bb[:, d, :], ACT.Exp, scale=1.0 / 16)
                    nc.scalar.activation(ki[:, d, :], bb[:, d, :], ACT.Exp, scale=-1.0 / 16)
                    nc.scalar.activation(dch[:, d, :], bb[:, d, (63, 0)[d]::64], ACT.Exp, scale=1.0 / 16)
                    a.wait_ge(gl_diff, n + 1)
                    nc.scalar.activation(ke[:, d, :], ke[:, d, :], ACT.Exp, scale=1.0 / 16).then_inc(gl_exp, 1)
            for t in range(TT):
                nc.scalar.activation(g1[:, t, :], g1[:, t, :], ACT.Silu)
            a.wait_ge(gl_free, GJ * GLA_H)
            for t in range(TT):
                for h in range(GLA_H):
                    last = nc.scalar.activation(St[:, t // 2, (t % 2) * 4 + h, :], v1[:, t, h * 256:(h + 1) * 256], ACT.Square,
                                                accum_out=stat[:, 16 + 4 * t + h:17 + 4 * t + h])
            last.then_inc(gl_ss, 1)
            a.wait_ge(gl_ms, 1)
            nc.scalar.activation(stat[:, 48:64], stat[:, 32:48], ACT.Sqrt).then_inc(gl_sd, 1)
            act_transposed(a, at, lambda k: PR("gla_norm", k))
            phase_over(a, at)
            add_skip(at, KD, 2)
            phase_over(a, at)

        def add_skip(at, K, nbs):
            n_advance(at, K, nbs, TT)

        def dve_add(v, at, K, nbs):
            for nb, t in n_results(v, at, K, nbs):
                x = X[:, t, nb * 512:nb * 512 + 512]
                nc.vector.tensor_tensor(x, PS[4 + t][:, :], x, ALU.add).then_inc(n_free, 1)

        def gla_dve(v, ch, at):
            skip_t(at, 10)
            n_advance(at, KD, 4, TT)
            phase_over(v, at)
            ch.link(nc.vector.memset(att[:, :, :], 0.0))
            c64 = lambda ap: ap.rearrange("p (c x) -> p c x", x=64)
            for h in range(GLA_H):
                for d in range(2):
                    n = 2 * h + d
                    v.wait_ge(gl_soft, n + 1)
                    nc.vector.tensor_scalar(la[:, :], PS[(GJ * h + d) % 8][:, :], PR(("gla_b_f", "gla_b_b")[d], h), 0.0,
                                            ALU.add, ALU.min).then_inc(gl_free, 1)
                    v.wait_ge(gl_free, GJ * h + d + 1)
                    ch.link(nc.vector.tensor_tensor(la[:, :], la[:, :], bb[:, d, :], ALU.subtract))
                    ways = slice(None) if d == 0 else slice(None, None, -1)
                    nc.vector.tensor_tensor_scan(out=bb[:, d, ways], data0=C("reset64"), data1=la[:, ways],
                                                 initial=0.0, op0=ALU.mult, op1=ALU.add).then_inc(gl_scan, 1)
                    v.wait_ge(gl_scan, n + 1)
                    e = (63, 0)[d]
                    nc.vector.tensor_tensor(c64(ke[:, d, :]), c64(bb[:, d, :])[:, :, e:e + 1].broadcast_to([P, 8, 64]),
                                            c64(bb[:, d, :]), ALU.subtract).then_inc(gl_diff, 1)
                    v.wait_ge(gl_exp, n + 1)
                    nc.vector.scalar_tensor_tensor(out=qd[:, d, :], in0=q1[:, h, :], scalar=GLA_SCALE, in1=qd[:, d, :],
                                                   op0=ALU.mult, op1=ALU.mult)
                    nc.vector.tensor_tensor(ki[:, d, :], k1[:, h, :], ki[:, d, :], ALU.mult)
                    nc.vector.tensor_tensor(ke[:, d, :], k1[:, h, :], ke[:, d, :], ALU.mult).then_inc(gl_opnd, 1)
                job = GJ * h + 2
                for d in range(2):
                    v.wait_ge(gl_bank, job + 1)
                    nc.vector.tensor_copy(keN[:, d, :], PS[job % 8][:, :]).then_inc(gl_free, 1)
                    job += 1
                for d in range(2):
                    v.wait_ge(gl_bank, job + 1)
                    nc.vector.copy_predicated(att[:, d, :].rearrange("p (t x) -> p t x", x=P),
                                              gmask[:, d, :].unsqueeze(1).broadcast_to([P, TT, P]),
                                              PS[job % 8][:, :].rearrange("p (t x) -> p t x", x=P)).then_inc(gl_free, 1)
                    job += 1
                for d in range(2):
                    for half in range(2):
                        v.wait_ge(gl_bank, job + 2)
                        cs = (list(range(0, 7)) if d == 0 else list(range(7, 0, -1)))[4 * half:4 * half + 4]
                        for e, c in enumerate(cs):
                            to = c + 1 if d == 0 else c - 1
                            kv = PS[(job + e % 2) % 8][:, (e // 2) * 256:(e // 2) * 256 + 256]
                            if c == (0, 7)[d]:
                                ins = nc.vector.tensor_copy(St[:, d, to, :], kv)
                            else:
                                ins = nc.vector.scalar_tensor_tensor(out=St[:, d, to, :], in0=St[:, d, c, :],
                                                                     scalar=dch[:, d, c:c + 1], in1=kv,
                                                                     op0=ALU.mult, op1=ALU.add)
                            if e == len(cs) - 1:
                                ins.then_inc(gl_free, 2)
                                v.wait_ge(gl_free, job + 2)
                            else:
                                ch.link(ins)
                        job += 2
                for j in range(2):
                    v.wait_ge(gl_bank, job + 1)
                    nc.vector.tensor_copy(v1[:, 2 * j:2 * j + 2, h * 256:(h + 1) * 256],
                                          PS[job % 8][:, :].rearrange("p (e x) -> p e x", x=256)).then_inc(gl_free, 1)
                    job += 1
            v.wait_ge(gl_ss, 1)
            nc.vector.tensor_scalar(stat[:, 32:48], stat[:, 16:32], 1.0 / GLA_DV, EPS, ALU.mult, ALU.add).then_inc(gl_ms, 1)
            v.wait_ge(gl_sd, 1)
            ch.link(nc.vector.reciprocal(stat[:, 64:80], stat[:, 48:64]))
            for t in range(TT):
                for h in range(GLA_H):
                    o = slice(h * 256, (h + 1) * 256)
                    last = nc.vector.scalar_tensor_tensor(out=v1[:, t, o], in0=v1[:, t, o],
                                                          scalar=stat[:, 64 + 4 * t + h:65 + 4 * t + h],
                                                          in1=g1[:, t, o], op0=ALU.mult, op1=ALU.mult)
            last.then_inc(gl_norm, 1)
            dve_transposed(v, at, lambda k: PR("gla_norm", k))
            phase_over(v, at)
            dve_add(v, at, KD, 2)
            phase_over(v, at)

        def ffn_pe(pe, at):
            layer = at.ffn
            at.ffn += 1
            pe_norm(pe, at, XN)
            for g in range(2):
                for f in range(2 * FF_GROUP):
                    pe_t_unit(pe, at)
                pe_n_pass(pe, at, act_hi, act_lo, FF_GROUP, 2, need=(ff_ready, FF_GROUP * (2 * layer + g)))
            phase_over(pe, at)

        def ffn_act(a, ch, at, layer):
            act_norm(a, at, X, XN, lambda k: PR("norm_ffn", 8 * layer + k))
            a.dma_start(cw[:, :], T["ffn_cw"][layer]).then_inc(ff_par, 16)
            a.dma_start(cb[:, :], T["ffn_cb"][layer]).then_inc(ff_par, 16)
            a.wait_ge(ff_par, 32 * (layer + 1))
            for g in range(2):
                for f in range(FF_GROUP):
                    n = FF_GROUP * (2 * layer + g) + f
                    tile = g * FF_GROUP + f
                    for side, y in enumerate((yv, yg)):
                        b = t_result(a, at)
                        if n and side == 0:
                            a.wait_ge(ff_w, n)
                        c = side * FF_TILES + tile
                        nc.scalar.activation(y[:, :], b[:, :], ACT.Identity, bias=cb[:, c:c + 1],
                                             scale=cw[:, 3 * c + 1:3 * c + 2]).then_inc(ff_y, 1)
                    a.wait_ge(t_free, at.tjob)
                    nc.scalar.activation(ys[:, :], yg[:, :], ACT.Silu).then_inc(ff_s, 1)
                    a.wait_ge(ff_w, n + 1)
                    nc.scalar.activation(act_hi[:, f, :], yw[:, :], ACT.Copy).then_inc(ff_h, 1)
                n_advance(at, FF_GROUP, 2, TT)
            phase_over(a, at)

        def ffn_dve(v, ch, at, layer):
            dve_norm(v, ch, at, X, XN, lambda k: PR("norm_ffn", 8 * layer + k))
            v.wait_ge(ff_par, 32 * (layer + 1))
            for g in range(2):
                for f in range(FF_GROUP):
                    n = FF_GROUP * (2 * layer + g) + f
                    tile = g * FF_GROUP + f
                    for side, y in enumerate((yv, yg)):
                        b = PS[at.tjob % 2]
                        at.unit += 1
                        at.tjob += 1
                        c = side * FF_TILES + tile
                        v.wait_ge(ff_y, 2 * n + side + 1)
                        ch.link(nc.vector.scalar_tensor_tensor(out=y[:, 1:S], in0=b[:, 0:S - 1], scalar=cw[:, 3 * c:3 * c + 1],
                                                               in1=y[:, 1:S], op0=ALU.mult, op1=ALU.add))
                        nc.vector.scalar_tensor_tensor(out=y[:, 0:S - 1], in0=b[:, 1:S], scalar=cw[:, 3 * c + 2:3 * c + 3],
                                                       in1=y[:, 0:S - 1], op0=ALU.mult, op1=ALU.add).then_inc(t_free, 1)
                    v.wait_ge(ff_s, n + 1)
                    nc.vector.tensor_tensor(yw[:, :], ys[:, :], yv[:, :], ALU.mult).then_inc(ff_w, 1)
                    v.wait_ge(ff_h, n + 1)
                    nc.vector.tensor_tensor(act_lo[:, f, :], yw[:, :], act_hi[:, f, :].bitcast(F32), ALU.subtract).then_inc(ff_ready, 1)
                dve_add(v, at, FF_GROUP, 2)
            phase_over(v, at)

        def pe_attend(pe, at, H, KT, NB, score, value, pbuf, pTbuf):
            jobs = H * TT
            for i in range(jobs + 2):
                if i < jobs:
                    g = at.sc + i
                    if i >= 2:
                        pe.wait_ge(sc_exp, g - 1)
                    mm = score(i // TT, i % TT, PS[i % 2])
                    mm.then_inc(sc_bank, 1)
                j = i - 1
                if 0 <= j < jobs:
                    g = at.sc + j
                    pe.wait_ge(sc_norm, g + 1)
                    if j >= 2:
                        pe.wait_ge(pt_sbuf, g - 1)
                    for kk in range(KT):
                        mm = nc.tensor.transpose(PS[2 + j % 2][:, kk * P:(kk + 1) * P], pbuf[:, j % 2, kk * P:(kk + 1) * P], ident)
                    mm.then_inc(pt_bank, 1)
                j = i - 2
                if j >= 0 and j % TT == TT - 1:
                    h = j // TT
                    pe.wait_ge(pt_sbuf, at.sc + j + 1)
                    for nb in range(NB):
                        q = h * NB + nb
                        if q >= 4:
                            pe.wait_ge(oT_lo, at.pv + q - 3)
                        for kk in range(KT):
                            mm = nc.tensor.matmul(PS[4 + q % 4][:, :], value(kk, h, nb), pTbuf[:, h % 2, kk, :],
                                                  start=(kk == 0), stop=(kk == KT - 1))
                        mm.then_inc(pv_bank, 1)
            pe.wait_ge(oT_lo, at.pv + H * NB)
            at.sc += jobs
            at.pv += H * NB

        def act_attend(a, at, H, KT, NB, scale, pbuf, pTbuf):
            jobs = H * TT
            n = KT * P
            for i in range(jobs + 2):
                if i < jobs:
                    g = at.sc + i
                    a.wait_ge(sc_max, g + 1)
                    if i >= 2:
                        a.wait_ge(pt_bank, g - 1)
                    nc.scalar.activation(pbuf[:, i % 2, 0:n], PS[i % 2][:, 0:n], ACT.Exp, bias=stat[:, 96 + i:97 + i], scale=scale,
                                         accum_out=stat[:, 128 + i:129 + i]).then_inc(sc_exp, 1)
                j = i - 1
                if 0 <= j < jobs:
                    h, t = j // TT, j % TT
                    a.wait_ge(pt_bank, at.sc + j + 1)
                    if h >= 2 and t == 0:
                        a.wait_ge(pv_bank, at.pv + (h - 1) * NB)
                    nc.scalar.activation(pTbuf[:, h % 2, :, t * P:(t + 1) * P],
                                         PS[2 + j % 2][:, 0:n].rearrange("p (k x) -> p k x", x=P), ACT.Copy).then_inc(pt_sbuf, 1)
                j = i - 2
                if j >= 0 and j % TT == TT - 1:
                    h = j // TT
                    for nb in range(NB):
                        q = h * NB + nb
                        a.wait_ge(pv_bank, at.pv + q + 1)
                        nc.scalar.activation(hT_hi[:, q, :], PS[4 + q % 4][:, :], ACT.Copy).then_inc(oT_hi, 1)
            at.sc += jobs
            at.pv += H * NB

        def dve_attend(v, ch, at, H, KT, NB, scale, pbuf):
            jobs = H * TT
            n = KT * P
            for i in range(jobs + 2):
                if i < jobs:
                    g = at.sc + i
                    v.wait_ge(sc_bank, g + 1)
                    ch.link(nc.vector.reduce_max(stat[:, 64 + i:65 + i], PS[i % 2][:, 0:n], AX_X))
                    nc.vector.tensor_scalar(stat[:, 96 + i:97 + i], stat[:, 64 + i:65 + i], -scale, None, ALU.mult).then_inc(sc_max, 1)
                j = i - 1
                if 0 <= j < jobs:
                    v.wait_ge(sc_exp, at.sc + j + 1)
                    ch.link(nc.vector.reciprocal(stat[:, 160 + j:161 + j], stat[:, 128 + j:129 + j]))
                    nc.vector.tensor_scalar(pbuf[:, j % 2, 0:n], pbuf[:, j % 2, 0:n], stat[:, 160 + j:161 + j], None,
                                            ALU.mult).then_inc(sc_norm, 1)
                j = i - 2
                if j >= 0 and j % TT == TT - 1:
                    h = j // TT
                    for nb in range(NB):
                        q = h * NB + nb
                        v.wait_ge(oT_hi, at.pv + q + 1)
                        nc.vector.tensor_tensor(hT_lo[:, q, :], PS[4 + q % 4][:, :], hT_hi[:, q, :].bitcast(F32),
                                                ALU.subtract).then_inc(oT_lo, 1)
            at.sc += jobs
            at.pv += H * NB

        NQK = AT_H + AT_KV

        def attn_pe(pe, at):
            pe_norm(pe, at, XN)
            pe_n_pass(pe, at, hT_hi, hT_lo, KD, 3)
            phase_over(pe, at)
            pe.wait_ge(at_rope, 1)
            for j in range(NQK):
                if j >= 4:
                    pe.wait_ge(at_sbuf, j - 3)
                for t in range(TT):
                    mm = nc.tensor.transpose(PS[j % 4][:, t * P:(t + 1) * P], qr[:, t, j * P:(j + 1) * P], ident)
                mm.then_inc(at_bank, 1)
            phase_over(pe, at)

            def score(h, t, bank):
                return nc.tensor.matmul(bank[:, :], qT[:, h, t * P:(t + 1) * P], kT[:, h // (AT_H // AT_KV), :], start=True, stop=True)

            def value(kk, h, nb):
                g = h // (AT_H // AT_KV)
                return qkv[:, kk, (NQK + g) * P:(NQK + g + 1) * P]

            pe_attend(pe, at, AT_H, TT, 1, score, value, at_pb, at_pT)
            pe_n_pass(pe, at, hT_hi, hT_lo, KD, 2)
            phase_over(pe, at)

        def attn_act(a, ch, at):
            act_norm(a, at, X, XN, lambda k: PR("norm_mix", 8 + k))
            for nb, t in n_results(a, at, KD, 3):
                nc.scalar.activation(qkv[:, t, nb * 512:nb * 512 + 512], PS[4 + t][:, :], ACT.Copy).then_inc(n_free, 1)
            phase_over(a, at)
            for t in range(TT):
                last = nc.scalar.activation(qr[:, t, :], qkv[:, t, 0:NQK * P], ACT.Square)
            last.then_inc(at_sq, 1)
            a.wait_ge(at_ms, 1)
            nc.scalar.activation(stat[:, 64:104], stat[:, 64:104], ACT.Sqrt).then_inc(at_sd, 1)
            for j in range(NQK):
                a.wait_ge(at_bank, j + 1)
                dst = qT[:, j, :] if j < AT_H else kT[:, j - AT_H, :]
                nc.scalar.activation(dst, PS[j % 4][:, :], ACT.Copy).then_inc(at_sbuf, 1)
            phase_over(a, at)
            act_attend(a, at, AT_H, TT, 1, AT_SCALE, at_pb, at_pT)
            n_advance(at, KD, 2, TT)
            phase_over(a, at)

        def attn_dve(v, ch, at):
            dve_norm(v, ch, at, X, XN, lambda k: PR("norm_mix", 8 + k))
            n_advance(at, KD, 3, TT)
            phase_over(v, at)
            heads = lambda ap: ap.rearrange("p t (h x) -> p t h x", x=P)
            v.wait_ge(at_sq, 1)
            ch.link(nc.vector.tensor_reduce(stat[:, 16:56], qr[:, :, :].rearrange("p t (h x) -> p (t h) x", x=P), AX_X, ALU.add))
            nc.vector.tensor_scalar(stat[:, 64:104], stat[:, 16:56], 1.0 / P, EPS, ALU.mult, ALU.add).then_inc(at_ms, 1)
            v.wait_ge(at_sd, 1)
            ch.link(nc.vector.reciprocal(stat[:, 112:152], stat[:, 64:104]))
            rstd = stat[:, 112:152].rearrange("p (t h) -> p t h", t=TT).unsqueeze(3).broadcast_to([P, TT, NQK, P])
            ch.link(nc.vector.tensor_tensor(heads(qn[:, :, :]), heads(qkv[:, :, 0:NQK * P]), rstd, ALU.mult))
            for name, h0, h1 in (("q_norm", 0, AT_H), ("k_norm", AT_H, NQK)):
                w = PR(name, 0, P).unsqueeze(1).unsqueeze(1).broadcast_to([P, TT, h1 - h0, P])
                part = heads(qn[:, :, h0 * P:h1 * P])
                ch.link(nc.vector.tensor_tensor(part, part, w, ALU.mult))
            x1, x2 = heads(qn[:, :, :])[:, :, :, 0:64], heads(qn[:, :, :])[:, :, :, 64:128]
            o1, o2 = heads(qr[:, :, :])[:, :, :, 0:64], heads(qr[:, :, :])[:, :, :, 64:128]
            turn = lambda name: C(name).rearrange("p (t x) -> p t x", t=TT).unsqueeze(2).broadcast_to([P, TT, NQK, 64])
            tmp = qT[:, 0:5, :].rearrange("p a x -> p (a x)").rearrange("p (t h x) -> p t h x", t=TT, x=64)
            ch.link(nc.vector.tensor_tensor(o1, x1, turn("cos"), ALU.mult))
            ch.link(nc.vector.tensor_tensor(tmp, x2, turn("sin"), ALU.mult))
            ch.link(nc.vector.tensor_tensor(o1, o1, tmp, ALU.subtract))
            ch.link(nc.vector.tensor_tensor(o2, x1, turn("sin"), ALU.mult))
            ch.link(nc.vector.tensor_tensor(tmp, x2, turn("cos"), ALU.mult))
            nc.vector.tensor_tensor(o2, o2, tmp, ALU.add).then_inc(at_rope, 1)
            phase_over(v, at)
            dve_attend(v, ch, at, AT_H, TT, 1, AT_SCALE, at_pb)
            dve_add(v, at, KD, 2)
            phase_over(v, at)

        def mixer_pe(pe, at):
            pe_norm(pe, at, XN)
            for _ in range(18):
                pe_t_unit(pe, at)
            pe_n_pass(pe, at, hT_hi, hT_lo, KD, 3)
            phase_over(pe, at)
            pe.wait_ge(ml_rexp, 1)
            for kind, row in enumerate((0, 1, 2, 5)):
                for n in range(TT):
                    c = kind * 16 + n * 4
                    nc.tensor.transpose(PS[7][:, c:c + 4], rows[0:4, row, n * P:(n + 1) * P], ident[0:4, 0:4])
            for h in range(ML_H):
                nc.tensor.matmul(PS[6][:, 4 * h:4 * h + 4], C("sel")[0:4, h * P:(h + 1) * P], mp[0:4, 8:12], start=True, stop=True)
            for h in range(ML_H):
                mm = nc.tensor.matmul(PS[h][:, :], C("sel")[0:4, h * P:(h + 1) * P], rows[0:4, 4, :], start=True, stop=True)
            mm.then_inc(ml_bc, 1)
            for h in range(ML_H):
                pe.wait_ge(ml_out, h + 1)
                for n in range(TT):
                    c = slice(n * P, (n + 1) * P)
                    mm = nc.tensor.matmul(PS[4][:, c], ml_k[:, h, c], ml_q[:, h, c], start=True, stop=True)
                mm.then_inc(ml_qk, 1)
                for n in range(TT):
                    c = slice(n * P, (n + 1) * P)
                    mm = nc.tensor.transpose(PS[5][:, c], ml_k[:, h, c], ident)
                mm.then_inc(ml_kt, 1)
                pe.wait_ge(ml_kw, h + 1)
                for n in range(TT - 1):
                    mm = nc.tensor.matmul(PS[5][:, n * 129:(n + 1) * 129], kw[:, n, :], vx[:, n, h, :], start=True, stop=True)
                mm.then_inc(ml_upd, 1)
                pe.wait_ge(ml_A, h + 1)
                for n in range(TT):
                    mm = nc.tensor.matmul(PS[6 + n // 2][:, (n % 2) * 129:(n % 2) * 129 + 129], aT[:, n * P:(n + 1) * P],
                                          vx[:, n, h, :], start=True, stop=True)
                mm.then_inc(ml_intra, 1)
                pe.wait_ge(ml_st, h + 1)
                for n in range(1, TT):
                    mm = nc.tensor.matmul(PS[4][:, (n - 1) * 129:n * 129], ml_q[:, h, n * P:(n + 1) * P], cT[:, n, :],
                                          start=True, stop=True)
                mm.then_inc(ml_inter, 1)
            phase_over(pe, at)

            def z(h, block, start, stop):
                r = slice((h % 2) * 64, (h % 2) * 64 + 64)
                return lambda bank: nc.tensor.matmul(bank[:, block * P:S], sb_k[r, h // 2, block * P:(block + 1) * P],
                                                     sb_q[r, h // 2, block * P:S], start=start, stop=stop)

            for h in range(SB_H + 1):
                if h < SB_H:
                    if h:
                        pe.wait_ge(st_L, h)
                    for b in range(TT):
                        mm = z(h, b, True, True)(PS[b])
                    mm.then_inc(st_z, 1)
                if h:
                    g = h - 1
                    pe.wait_ge(st_A, g + 1)
                    for t in range(TT):
                        for b in range(t + 1):
                            mm = nc.tensor.matmul(PS[4][:, t * 64:(t + 1) * 64], stA[:, b, t * P:(t + 1) * P],
                                                  sb_v[:, b, g * 64:(g + 1) * 64], start=(b == 0), stop=(b == t))
                    mm.then_inc(st_o, 1)
                if h < SB_H:
                    pe.wait_ge(st_L, h + 1)
                    if h:
                        pe.wait_ge(st_of, h)
                    for b in range(TT):
                        bank = PS[4 + b]
                        z(h, b, True, False)(bank)
                        mm = nc.tensor.matmul(bank[:, b * P:S], C("negtri"), stL[:, b, b * P:S], start=False, stop=(b == TT - 1))
                        for b2 in range(b + 1, TT):
                            mm = nc.tensor.matmul(bank[:, b2 * P:S], C("negones"), stL[:, b2, b2 * P:S], start=False, stop=(b2 == TT - 1))
                    mm.then_inc(st_r, 1)
            pe.wait_ge(mx_norm, 1)
            pe_transposes(pe, at, mixed)
            phase_over(pe, at)
            pe_n_pass(pe, at, hT_hi, hT_lo, KD, 2)
            phase_over(pe, at)

        def mixer_act(a, ch, at):
            act_norm(a, at, X, XN, lambda k: PR("mix_norm", k))
            for c in range(8):
                b = t_result(a, at)
                y = ml_q[:, c, :] if c < 4 else ml_k[:, c - 4, :]
                nc.scalar.activation(y, b[:, :], ACT.Identity, bias=PR("conv2_b", c), scale=PR("conv2_w", 4 * c + 3)).then_inc(mx_y, 1)
                a.wait_ge(t_free, at.tjob)
                nc.scalar.activation(y, y, ACT.Silu)
            b = t_result(a, at)
            nc.scalar.activation(rows[0:4, 0, :], b[0:4, :], ACT.Identity, bias=PR("igate")[0:4, :]).then_inc(t_free, 1)
            b = t_result(a, at)
            ch.link(nc.scalar.activation(rows[0:4, 1, :], b[0:4, :], ACT.Abs, bias=PR("fgate")[0:4, :]))
            nc.scalar.activation(rows[0:4, 2, :], b[0:4, :], ACT.Identity, bias=PR("fgate")[0:4, :]).then_inc(t_free, 1)
            for c in range(8):
                b = t_result(a, at)
                dst, scale = (sb_q[:, c, :], SB_SCALE) if c < 4 else (sb_k[:, c - 4, :], 1.0)
                nc.scalar.activation(dst, b[:, :], ACT.Copy, scale=scale).then_inc(t_free, 1)
            for nb, t in n_results(a, at, KD, 3):
                src = PS[4 + t][:, :]
                if nb == 0:
                    ins = nc.scalar.activation(vx[:, t, :, 0:P], src.rearrange("p (h x) -> p h x", x=P), ACT.Copy)
                elif nb == 1:
                    ins = nc.scalar.activation(og[:, t, :], src, ACT.Sigmoid)
                else:
                    ins = nc.scalar.activation(sb_v[:, t, :], src, ACT.Copy)
                ins.then_inc(n_free, 1)
            phase_over(a, at)
            ch.link(nc.scalar.activation(rows[0:4, 1, :], rows[0:4, 1, :], ACT.Exp, scale=-1.0))
            nc.scalar.activation(rows[0:4, 1, :], rows[0:4, 1, :], ACT.Ln, bias=1.0).then_inc(ml_soft, 1)
            a.wait_ge(ml_arg, 1)
            for r in (1, 2, 5):
                nc.scalar.activation(rows[0:4, r, :], rows[0:4, r, :], ACT.Exp)
            nc.scalar.activation(mp[0:4, 8:12], mp[0:4, 8:12], ACT.Exp).then_inc(ml_rexp, 1)
            for h in range(ML_H):
                a.wait_ge(ml_diff, h + 1)
                nc.scalar.activation(wT[:, :], wT[:, :], ACT.Exp, scale=-1.0).then_inc(ml_wexp, 1)
                a.wait_ge(ml_intra, h + 1)
                for n in range(2):
                    last = nc.scalar.activation(nd[:, 2 * n:2 * n + 2, :], PS[6 + n][:, 0:258].rearrange("p (e x) -> p e x", x=129), ACT.Copy)
                last.then_inc(ml_nd, 1)
            phase_over(a, at)
            for h in range(SB_H + 1):
                if h < SB_H:
                    a.wait_ge(st_z, h + 1)
                    for b in range(TT):
                        c = slice(b * P, S)
                        last = nc.scalar.activation(stT[:, b, c], PS[b][:, c], ACT.Abs)
                    ch.link(last)
                    for b in range(TT):
                        c = slice(b * P, S)
                        last = nc.scalar.activation(stT[:, b, c], stT[:, b, c], ACT.Exp, scale=-1.0)
                    ch.link(last)
                    for b in range(TT):
                        c = slice(b * P, S)
                        last = nc.scalar.activation(stT[:, b, c], stT[:, b, c], ACT.Ln, bias=1.0)
                    last.then_inc(st_ln, 1)
                    a.wait_ge(st_min, h + 1)
                    for b in range(TT):
                        c = slice(b * P, S)
                        last = nc.scalar.activation(stA[:, b, c], stA[:, b, c], ACT.Exp)
                    last.then_inc(st_exp, 1)
            a.wait_ge(st_of, SB_H)
            for t in range(TT):
                nc.scalar.activation(ml_q[:, t, :], mixed[:, t, 0:512], ACT.Square)
                last = nc.scalar.activation(ml_k[:, t, :], mixed[:, t, 512:1024], ACT.Square)
            last.then_inc(mx_sq, 1)
            a.wait_ge(mx_ms, 1)
            nc.scalar.activation(stat[:, 64:112], stat[:, 64:112], ACT.Sqrt).then_inc(mx_sd, 1)
            act_transposed(a, at, lambda k: PR("head_gain", k))
            phase_over(a, at)
            n_advance(at, KD, 2, TT)
            phase_over(a, at)

        def mixer_dve(v, ch, at):
            dve_norm(v, ch, at, X, XN, lambda k: PR("mix_norm", k))
            nc.vector.memset(vx[:, :, :, P:P + 1], 1.0)
            for c in range(8):
                b = PS[at.tjob % 2]
                skip_t(at)
                y = ml_q[:, c, :] if c < 4 else ml_k[:, c - 4, :]
                v.wait_ge(mx_y, c + 1)
                for j in range(1, 4):
                    ins = nc.vector.scalar_tensor_tensor(out=y[:, j:S], in0=b[:, 0:S - j], scalar=PR("conv2_w", 4 * c + 3 - j),
                                                         in1=y[:, j:S], op0=ALU.mult, op1=ALU.add)
                    if j < 3:
                        ch.link(ins)
                    else:
                        ins.then_inc(t_free, 1)
            skip_t(at, 10)
            n_advance(at, KD, 3, TT)
            phase_over(v, at)
            v.wait_ge(ml_soft, 1)
            R = lambda i: rows[0:4, i, :]
            lastcol = lambda i: rows[0:4, i, P - 1::P]
            ch.link(nc.vector.memset(mp[0:4, 0:1], 0.0))
            ch.link(nc.vector.memset(kw[0:4, :, :], 0.0))
            zrow = kw[0:4, :, :].rearrange("p a x -> p (a x)")
            ch.link(nc.vector.scalar_tensor_tensor(out=R(2), in0=R(2), scalar=0.0, in1=R(1), op0=ALU.min, op1=ALU.subtract))
            ch.link(nc.vector.tensor_tensor_scan(out=R(3), data0=C("reset128")[0:4, :], data1=R(2), initial=0.0, op0=ALU.mult, op1=ALU.add))
            ch.link(nc.vector.tensor_tensor(R(0), R(0), R(3), ALU.subtract))
            for n in range(TT):
                c = slice(n * P, (n + 1) * P)
                e = (n + 1) * P - 1
                ch.link(nc.vector.tensor_tensor_scan(out=rows[0:4, 4, c], data0=zrow[:, c], data1=rows[0:4, 0, c],
                                                     initial=mp[0:4, n:n + 1], op0=ALU.add, op1=ALU.max))
                ch.link(nc.vector.tensor_tensor(mp[0:4, n + 1:n + 2], rows[0:4, 3, e:e + 1], rows[0:4, 4, e:e + 1], ALU.add))
                nc.vector.tensor_scalar(rows[0:4, 1, c], rows[0:4, 4, c], -1.0, mp[0:4, n:n + 1], ALU.mult, ALU.add)
                nc.vector.tensor_scalar(rows[0:4, 5, c], rows[0:4, 0, c], rows[0:4, 4, e:e + 1], None, ALU.subtract)
            nc.vector.scalar_tensor_tensor(out=R(2), in0=R(3), scalar=-1.0, in1=R(4), op0=ALU.mult, op1=ALU.subtract)
            nc.vector.tensor_tensor(mp[0:4, 8:12], mp[0:4, 0:4], lastcol(4), ALU.subtract).then_inc(ml_arg, 1)
            v.wait_ge(ml_bc, 1)
            ch.link(nc.vector.tensor_copy(cols[:, :], PS[7][:, 0:64]))
            nc.vector.tensor_copy(dec[:, :], PS[6][:, 0:16]).then_inc(ml_out, 1)
            v.wait_ge(ml_out, 1)
            col = lambda kind, n, h: cols[:, kind * 16 + n * 4 + h:kind * 16 + n * 4 + h + 1]
            for h in range(ML_H):
                for n in range(TT):
                    c = slice(n * P, (n + 1) * P)
                    last = nc.vector.tensor_scalar(wT[:, c], PS[h][:, c], col(0, n, h), 0.0, ALU.subtract, ALU.max)
                last.then_inc(ml_diff, 1)
                v.wait_ge(ml_kt, h + 1)
                for n in range(TT):
                    last = nc.vector.tensor_scalar(kw[:, n, :], PS[5][:, n * P:(n + 1) * P], col(3, n, h), ML_SCALE, ALU.mult, ALU.mult)
                last.then_inc(ml_kw, 1)
                v.wait_ge(ml_wexp, h + 1)
                w3 = wT[:, :].rearrange("p (n x) -> p n x", x=P)
                ch.link(nc.vector.tensor_tensor(w3, w3, C("causal").unsqueeze(1).broadcast_to([P, TT, P]), ALU.mult))
                nc.vector.scalar_tensor_tensor(out=aT[:, :], in0=PS[4][:, :], scalar=ML_SCALE, in1=wT[:, :], op0=ALU.mult,
                                               op1=ALU.mult).then_inc(ml_A, 1)
                v.wait_ge(ml_upd, h + 1)
                ch.link(nc.vector.tensor_copy(cT[:, 1, :], PS[5][:, 0:129]))
                ch.link(nc.vector.scalar_tensor_tensor(out=cT[:, 2, :], in0=cT[:, 1, :], scalar=dec[:, 4 * h + 1:4 * h + 2],
                                                       in1=PS[5][:, 129:258], op0=ALU.mult, op1=ALU.add))
                nc.vector.scalar_tensor_tensor(out=cT[:, 3, :], in0=cT[:, 2, :], scalar=dec[:, 4 * h + 2:4 * h + 3],
                                               in1=PS[5][:, 258:387], op0=ALU.mult, op1=ALU.add).then_inc(ml_st, 1)
                v.wait_ge(ml_nd, h + 1)
                v.wait_ge(ml_inter, h + 1)
                for n in range(1, TT):
                    last = nc.vector.scalar_tensor_tensor(out=nd[:, n, :], in0=PS[4][:, (n - 1) * 129:n * 129], scalar=col(1, n, h),
                                                          in1=nd[:, n, :], op0=ALU.mult, op1=ALU.add)
                ch.link(last)
                guard = cols[:, 32 + h:32 + h + 13:4]
                den = nd[:, :, P:P + 1].rearrange("p n x -> p (n x)")
                ch.link(nc.vector.scalar_tensor_tensor(out=stat[:, 16:20], in0=den, scalar=-1.0, in1=den, op0=ALU.mult, op1=ALU.max))
                ch.link(nc.vector.tensor_tensor(stat[:, 16:20], stat[:, 16:20], guard, ALU.max))
                ch.link(nc.vector.reciprocal(stat[:, 20:24], stat[:, 16:20]))
                for n in range(TT):
                    last = nc.vector.tensor_scalar(mixed[:, n, h * P:(h + 1) * P], nd[:, n, 0:P], stat[:, 20 + n:21 + n], None, ALU.mult)
                last.then_inc(ml_out, 1)
            v.wait_ge(ml_out, ML_H + 1)
            ch.link(nc.vector.tensor_tensor(mixed[:, :, 0:512], mixed[:, :, 0:512], og[:, :, :], ALU.mult))
            phase_over(v, at)
            strict = C("strict")
            for h in range(SB_H):
                v.wait_ge(st_ln, h + 1)
                for b in range(TT):
                    c = slice(b * P, S)
                    ch.link(nc.vector.scalar_tensor_tensor(out=stL[:, b, c], in0=PS[b][:, c], scalar=0.0, in1=stT[:, b, c],
                                                           op0=ALU.max, op1=ALU.add))
                for b in range(TT):
                    c = slice(b * P, (b + 1) * P)
                    last = nc.vector.tensor_tensor(stL[:, b, c], stL[:, b, c], strict, ALU.mult)
                last.then_inc(st_L, 1)
                if h:
                    v.wait_ge(st_o, h)
                    nc.vector.tensor_copy(mixed[:, :, 512 + (h - 1) * 64:512 + h * 64],
                                          PS[4][:, 0:256].rearrange("p (t x) -> p t x", x=64)).then_inc(st_of, 1)
                v.wait_ge(st_r, h + 1)
                for b in range(TT):
                    c = slice(b * P, S)
                    last = nc.vector.tensor_scalar(stA[:, b, c], PS[4 + b][:, c], 80.0, None, ALU.min)
                last.then_inc(st_min, 1)
                v.wait_ge(st_exp, h + 1)
                for b in range(TT):
                    c = slice(b * P, (b + 1) * P)
                    last = nc.vector.tensor_tensor(stA[:, b, c], stA[:, b, c], strict, ALU.mult)
                last.then_inc(st_A, 1)
            v.wait_ge(st_o, SB_H)
            nc.vector.tensor_copy(mixed[:, :, 960:1024],
                                  PS[4][:, 0:256].rearrange("p (t x) -> p t x", x=64)).then_inc(st_of, 1)
            v.wait_ge(mx_sq, 1)
            nc.vector.tensor_reduce(stat[:, 16:32], ml_q[:, :, :].rearrange("p t (h x) -> p (t h) x", x=P), AX_X, ALU.add)
            ch.link(nc.vector.tensor_reduce(stat[:, 32:64], ml_k[:, :, :].rearrange("p t (h x) -> p (t h) x", x=64), AX_X, ALU.add))
            nc.vector.tensor_scalar(stat[:, 64:80], stat[:, 16:32], 1.0 / P, EPS, ALU.mult, ALU.add)
            nc.vector.tensor_scalar(stat[:, 80:112], stat[:, 32:64], 1.0 / SB_D, EPS, ALU.mult, ALU.add).then_inc(mx_ms, 1)
            v.wait_ge(mx_sd, 1)
            ch.link(nc.vector.reciprocal(stat[:, 112:160], stat[:, 64:112]))
            for c0, n, w, s0 in ((0, 4, P, 112), (512, 8, 64, 128)):
                part = mixed[:, :, c0:c0 + 512].rearrange("p t (h x) -> p t h x", x=w)
                r = stat[:, s0:s0 + TT * n].rearrange("p (t h) -> p t h", t=TT).unsqueeze(3).broadcast_to([P, TT, n, w])
                last = nc.vector.tensor_tensor(part, part, r, ALU.mult)
            last.then_inc(mx_norm, 1)
            dve_transposed(v, at, lambda k: PR("head_gain", k))
            phase_over(v, at)
            dve_add(v, at, KD, 2)
            phase_over(v, at)

        def xattn_pe(pe, at):
            pe_norm(pe, at, XN)
            for _ in range(8):
                pe_t_unit(pe, at)
            phase_over(pe, at)
            pe_norm(pe, at, mem, MEM_T)
            for _ in range(8):
                pe_t_unit(pe, at, 256)
            pe_n_pass(pe, at, hT_hi, hT_lo, KD, 2, toks=MEM_T)
            phase_over(pe, at)

            def score(h, t, bank):
                for c in range(2):
                    mm = nc.tensor.matmul(bank[:, 0:256], xq[:, 2 * h + c, t * P:(t + 1) * P], xk[:, 2 * h + c, :],
                                          start=(c == 0), stop=(c == 1))
                return mm

            def value(kk, h, nb):
                return xv[:, kk, h * 256 + nb * P:h * 256 + (nb + 1) * P]

            pe_attend(pe, at, XA_H, MEM_T, 2, score, value, xp, xpT)
            pe_n_pass(pe, at, hT_hi, hT_lo, KD, 2)
            phase_over(pe, at)

        def xattn_act(a, ch, at):
            act_norm(a, at, X, XN, lambda k: PR("xattn_norm", k))
            a.dma_start(mem[:, :, :], T["mem"]).then_inc(m_in, 16)
            for c in range(8):
                b = t_result(a, at)
                nc.scalar.activation(xq[:, c, :], b[:, :], ACT.Copy).then_inc(t_free, 1)
            a.wait_ge(m_in, 16)
            phase_over(a, at)
            act_norm(a, at, mem, xv, lambda k: PR("mem_norm", k), MEM_T)
            for c in range(8):
                b = t_result(a, at)
                nc.scalar.activation(xk[:, c, :], b[:, 0:256], ACT.Copy).then_inc(t_free, 1)
            for nb, t in n_results(a, at, KD, 2, MEM_T):
                nc.scalar.activation(xv[:, t, nb * 512:nb * 512 + 512], PS[4 + t][:, :], ACT.Copy).then_inc(n_free, 1)
            phase_over(a, at)
            act_attend(a, at, XA_H, MEM_T, 2, XA_SCALE, xp, xpT)
            n_advance(at, KD, 2, TT)
            phase_over(a, at)

        def xattn_dve(v, ch, at):
            dve_norm(v, ch, at, X, XN, lambda k: PR("xattn_norm", k))
            skip_t(at, 8)
            phase_over(v, at)
            v.wait_ge(m_in, 16)
            dve_norm(v, ch, at, mem, mem, lambda k: PR("mem_norm", k), MEM_T)
            skip_t(at, 8)
            n_advance(at, KD, 2, MEM_T)
            phase_over(v, at)
            dve_attend(v, ch, at, XA_H, MEM_T, 2, XA_SCALE, xp)
            dve_add(v, at, KD, 2)
            phase_over(v, at)

        def onehot_steps(eng, first, rest):
            pass

        def peer_pe(pe, at):
            pe_norm(pe, at, XN)
            pe.wait_ge(m_in, 32)
            for j in range(2 * PH + 1):
                if j < 2 * PH:
                    pe_t_unit(pe, at)
                if j:
                    i = j - 1
                    pe.wait_ge(t_free, at.tjob - (1 if j < 2 * PH else 0))
                    if i >= 4:
                        pe.wait_ge(ro_sbuf, i - 3)
                    for t in range(TT):
                        mm = nc.tensor.matmul(PS[4 + i % 4][:, t * P:(t + 1) * P], rq[:, i % 2, t * P:(t + 1) * P],
                                              subT[:, i * NKEY:(i + 1) * NKEY], start=True, stop=True)
                    mm.then_inc(ro_bank, 1)
            phase_over(pe, at)
            for t in range(TT):
                pe.wait_ge(ro_gate, t + 1)
                for kind in range(3):
                    mm = nc.tensor.transpose(PS[t % 2][:, kind * P:(kind + 1) * P], sel_ij[:, kind, :], ident)
                mm.then_inc(ro_tr, 1)
            phase_over(pe, at)

            def tokens(n0):
                for k in range(16):
                    pe.wait_ge(oh_ready, n0 + (k + 1))
                    if k % 4 == 0:
                        if not isinstance(n0, int) or n0:
                            pe.wait_ge(g_evac, (n0 + k) // 4 - 3 if isinstance(n0, int) else g_step[0] * 4 + (g_step[1] + k // 4 - 3))
                    nc.tensor.matmul(PS[k // 4][:, (k % 4) * P:(k % 4 + 1) * P], ohI[:, k % 8, :], ohJ[:, k % 8, :],
                                     start=True, stop=True).then_inc(oh_used, 1)

            g_step = [None, 0]
            for c in range(8):
                first = 0
                if c == 0:
                    tokens(0)
                    first = 1
                with pe.Fori(first, 4) as i:
                    g_step[0], g_step[1] = i, c * 16
                    tokens(i * 16 + c * 64)
            phase_over(pe, at)

            def group(n, base, looped):
                for _ in range(n):
                    pe_t_unit(pe, at)
                pe_n_pass(pe, at, act_hi, act_lo, n, 2, need=(peer_ready, base))

            with pe.Fori(0, PEER_LOOPS) as i:
                at.loop = i
                group(PG, 0, True)
            loops_done(at)
            group(PEER_TAIL, PEER_LOOPS * PG, False)
            phase_over(pe, at)

        def loops_done(at):
            at.loop = None
            at.unit += (PEER_LOOPS - 1) * 2 * PG
            at.tjob += (PEER_LOOPS - 1) * PG
            at.njob += (PEER_LOOPS - 1) * 8
            at.nready += (PEER_LOOPS - 1) * 6

        def peer_act(a, ch, at):
            act_norm(a, at, X, XN, lambda k: PR("ffn_norm_2", k))
            a.dma_start(subT[:, :], T["subkeys"]).then_inc(m_in, 16)
            for j in range(2 * PH):
                b = t_result(a, at)
                if j >= 2:
                    a.wait_ge(ro_bank, j - 1)
                nc.scalar.activation(rq[:, j % 2, :], b[:, :], ACT.Copy).then_inc(t_free, 1)
            phase_over(a, at)
            for t in range(TT):
                a.wait_ge(ro_arg, t + 1)
                nc.scalar.activation(sel_ij[:, 2, :], sel_ij[:, 2, :], ACT.Exp).then_inc(ro_exp, 1)
                a.wait_ge(ro_tr, t + 1)
                nc.scalar.activation(idxT[:, :, t * P:(t + 1) * P], PS[t % 2][:, 0:384].rearrange("p (k x) -> p k x", x=P), ACT.Copy).then_inc(ro_idx_in, 1)
            phase_over(a, at)

            def step(c, i):
                for q in range(4):
                    if isinstance(i, int):
                        a.wait_ge(oh_used, c * 64 + i * 16 + 4 * (q + 1))
                        where = stage[:, c % 2, :, i * 16 + 4 * q:i * 16 + 4 * q + 4]
                    else:
                        a.wait_ge(oh_used, i * 16 + (c * 64 + 4 * (q + 1)))
                        where = stage[:, c % 2, :, bass.ds(i * 16 + 4 * q, 4)]
                    nc.scalar.activation(where, PS[q][:, :].rearrange("p (t j) -> p j t", j=NKEY), ACT.Copy).then_inc(g_evac, 1)

            for c in range(8):
                first = 0
                if c >= 2:
                    a.wait_ge(g_out[c % 2], 16 * (c // 2))
                if c == 0:
                    step(0, 0)
                    first = 1
                with a.Fori(first, 4) as i:
                    step(c, i)
                a.wait_ge(g_evac, 16 * (c + 1))
                a.dma_start(gates[:, :, c * 64:(c + 1) * 64].rearrange("j p t -> p j t"), stage[:, c % 2, :, :]).then_inc(g_out[c % 2], 16)
            for s in range(2):
                a.wait_ge(g_out[s], 64)
            phase_over(a, at)

            def load(j, s):
                src = gates[j] if isinstance(j, int) else gates[bass.ds(j, 1)].rearrange("a p t -> p (a t)")
                a.dma_start(gt[:, s, :], src).then_inc(g_in[s], 16)

            def group(n, j0, ahead):
                for jj in range(n):
                    j = j0 + jj
                    if jj + 2 < n or ahead:
                        a.wait_ge(peer_w, j + 3)
                        load(j + 2, (jj + 2) % 4)
                    b = t_result(a, at)
                    nc.scalar.activation(ga[:, jj % 2, :], b[:, :], ACT.Gelu).then_inc(t_free, 1)
                    a.wait_ge(peer_w, j + 5)
                    nc.scalar.activation(act_hi[:, jj, :], gw[:, jj % 2, :], ACT.Copy).then_inc(peer_h, 1)
                n_advance(at, n, 2, TT)

            load(0, 0)
            load(1, 1)
            with a.Fori(0, PEER_LOOPS) as i:
                at.loop = i
                group(PG, i * PG, True)
            loops_done(at)
            group(PEER_TAIL, PEER_LOOPS * PG, False)
            phase_over(a, at)
            a.dma_start(fgain[:, :], T["final_gain"]).then_inc(m_in, 16)
            for t in range(TT):
                last = nc.scalar.activation(fout[:, t, :], X[:, t, :], ACT.Square, accum_out=stat[:, t:t + 1])
            last.then_inc(ss_ready, 1)
            a.wait_ge(ms_ready, at.norm + 1)
            nc.scalar.activation(stat[:, 8:12], stat[:, 4:8], ACT.Sqrt).then_inc(sd_ready, 1)
            for t in range(TT):
                a.wait_ge(fin, t + 1)
                a.dma_start(out[:, t, :], fout[:, t, :]).then_inc(o_sem, 16)
            a.wait_ge(o_sem, 16 * TT)

        def peer_dve(v, ch, at):
            dve_norm(v, ch, at, X, XN, lambda k: PR("ffn_norm_2", k))
            skip_t(at, 2 * PH)
            for j in range(2 * PH):
                v.wait_ge(ro_bank, j + 1)
                nc.vector.tensor_copy(rs[:, :, j, :], PS[4 + j % 4][:, :].rearrange("p (t x) -> p t x", x=P)).then_inc(ro_sbuf, 1)
            phase_over(v, at)
            iota16 = C("iota")[:, 0:TOPK]
            for t in range(TT):
                for j in range(2 * PH):
                    top, idx, s_ = tv[:, j, :], ti[:, j, :], rs[:, t, j, :]
                    ch.link(nc.vector.max(top[:, 0:8], s_))
                    nc.vector.max_index(idx[:, 0:8], top[:, 0:8], s_)
                    ch.link(nc.vector.match_replace(srep[:, :], top[:, 0:8], s_, LOWEST))
                    ch.link(nc.vector.max(top[:, 8:16], srep[:, :]))
                    ch.link(nc.vector.max_index(idx[:, 8:16], top[:, 8:16], srep[:, :]))
                tv4 = tv[:, :, :].rearrange("p (h e) k -> p h e k", e=2)
                c4 = cand[:, :, :].rearrange("p h (a b) -> p h a b", a=TOPK)
                ch.link(nc.vector.tensor_copy(tif[:, :, :], ti[:, :, :]))
                ch.link(nc.vector.tensor_tensor(c4, tv4[:, :, 0, :].unsqueeze(3).broadcast_to([P, PH, TOPK, TOPK]),
                                                tv4[:, :, 1, :].unsqueeze(2).broadcast_to([P, PH, TOPK, TOPK]), ALU.add))
                for h in range(PH):
                    top, idx, s_ = best[:, h, :], pos[:, h, :], cand[:, h, :]
                    ch.link(nc.vector.max(top[:, 0:8], s_))
                    nc.vector.max_index(idx[:, 0:8], top[:, 0:8], s_)
                    ch.link(nc.vector.match_replace(crep[:, :], top[:, 0:8], s_, LOWEST))
                    ch.link(nc.vector.max(top[:, 8:16], crep[:, :]))
                    ch.link(nc.vector.max_index(idx[:, 8:16], top[:, 8:16], crep[:, :]))
                flat = pos[:, :, :].rearrange("p h k -> p (h k)")
                nc.vector.tensor_single_scalar(ab[:, 0, :], flat, 4, ALU.logical_shift_right)
                ch.link(nc.vector.tensor_single_scalar(ab[:, 1, :], flat, 15, ALU.bitwise_and))
                ch.link(nc.vector.tensor_copy(abf[:, :, :], ab[:, :, :]))
                if t:
                    v.wait_ge(ro_tr, t)
                tif4 = tif[:, :, :].rearrange("p (h e) k -> p h e k", e=2)
                eq4 = eqt[:, :].rearrange("p (h k a) -> p h k a", h=PH, k=TOPK)
                for e in range(2):
                    ch.link(nc.vector.tensor_tensor(eqt[:, :].rearrange("p (k a) -> p k a", a=TOPK),
                                                    abf[:, e, :].unsqueeze(2).broadcast_to([P, P, TOPK]),
                                                    iota16.unsqueeze(1).broadcast_to([P, P, TOPK]), ALU.is_equal))
                    ch.link(nc.vector.tensor_tensor(eq4, eq4, tif4[:, :, e, :].unsqueeze(2).broadcast_to([P, PH, TOPK, TOPK]), ALU.mult))
                    ch.link(nc.vector.tensor_reduce(sel_ij[:, e, :], eqt[:, :].rearrange("p (k a) -> p k a", a=TOPK), AX_X, ALU.add))
                g3 = sel_ij[:, 2, :].rearrange("p (h k) -> p h k", h=PH)
                nc.vector.tensor_tensor(g3, best[:, :, :], best[:, :, 0:1].broadcast_to([P, PH, TOPK]), ALU.subtract).then_inc(ro_arg, 1)
                v.wait_ge(ro_exp, t + 1)
                ch.link(nc.vector.tensor_reduce(stat[:, 16:24], g3, AX_X, ALU.add))
                ch.link(nc.vector.reciprocal(stat[:, 24:32], stat[:, 16:24]))
                nc.vector.tensor_tensor(g3, g3, stat[:, 24:32].unsqueeze(2).broadcast_to([P, PH, TOPK]), ALU.mult).then_inc(ro_gate, 1)
            phase_over(v, at)

            def tokens(c, i):
                for k in range(16):
                    if isinstance(i, int):
                        n = c * 64 + i * 16 + k
                        if n >= 8:
                            v.wait_ge(oh_used, n - 7)
                        col = slice(n, n + 1)
                    else:
                        v.wait_ge(oh_used, i * 16 + (c * 64 + k - 7))
                        col = bass.ds(i * 16 + (c * 64 + k), 1)
                    nc.vector.tensor_scalar(ohI[:, k % 8, :], C("iota"), idxT[:, 0, col], None, ALU.is_equal)
                    nc.vector.tensor_scalar(ohJ[:, k % 8, :], C("iota"), idxT[:, 1, col], idxT[:, 2, col], ALU.is_equal, ALU.mult).then_inc(oh_ready, 1)

            for c in range(8):
                first = 0
                if c == 0:
                    tokens(0, 0)
                    first = 1
                with v.Fori(first, 4) as i:
                    tokens(c, i)
            phase_over(v, at)
            nc.vector.memset(stat[:, 0:1], 0.0).then_inc(peer_w, 4)

            def group(n, j0):
                for jj in range(n):
                    j = j0 + jj
                    skip_t(at)
                    v.wait_ge(g_in[jj % 4], 16 * (j // 4 + 1) if isinstance(j, int) else at.loop * (4 * PG) + 16 * (jj // 4 + 1))
                    v.wait_ge(t_free, at.tjob if at.loop is None else at.loop * PG + at.tjob)
                    nc.vector.tensor_tensor(gw[:, jj % 2, :], ga[:, jj % 2, :], gt[:, jj % 4, :], ALU.mult).then_inc(peer_w, 1)
                    v.wait_ge(peer_h, j + 1)
                    nc.vector.tensor_tensor(act_lo[:, jj, :], gw[:, jj % 2, :], act_hi[:, jj, :].bitcast(F32), ALU.subtract).then_inc(peer_ready, 1)
                dve_add(v, at, n, 2)

            with v.Fori(0, PEER_LOOPS) as i:
                at.loop = i
                group(PG, i * PG)
            loops_done(at)
            group(PEER_TAIL, PEER_LOOPS * PG)
            phase_over(v, at)
            v.wait_ge(ss_ready, at.norm + 1)
            nc.vector.tensor_scalar(stat[:, 4:8], stat[:, 0:4], 1.0 / D, EPS, ALU.mult, ALU.add).then_inc(ms_ready, 1)
            v.wait_ge(sd_ready, at.norm + 1)
            ch.link(nc.vector.reciprocal(stat[:, 12:16], stat[:, 8:12]))
            v.wait_ge(m_in, 48)
            for t in range(TT):
                nc.vector.scalar_tensor_tensor(out=fout[:, t, :], in0=X[:, t, :], scalar=stat[:, 12 + t:13 + t], in1=fgain[:, :],
                                               op0=ALU.mult, op1=ALU.mult).then_inc(fin, 1)


        block = ctx.enter_context(nc.Block())

        def store(a):
            a.dma_start(out, X[:, :, :]).then_inc(o_sem, 16)
            a.wait_ge(o_sem, 16)

        def stopping(name):
            return stop == name

        @block.sync
        def _(sp):
            ws = T["weights"]

            def load(u, s):
                src = ws[u] if isinstance(u, int) else ws[bass.ds(u, 1)].rearrange("a p n -> p (a n)")
                sp.dma_start(w_raw[:, s, :], src).then_inc(raw_landed[s], 16)

            for u in range(RING):
                load(u, u)
            loops = NU // RING - 1
            with sp.Fori(0, loops) as i:
                for s in range(RING):
                    sp.wait_ge(w_split, i * RING + (s + 1))
                    load(i * RING + (s + RING), s)
            for u in range((loops + 1) * RING, NU):
                sp.wait_ge(w_split, u - RING + 1)
                load(u, u % RING)

        @block.gpsimd
        def _(pool):
            nc.gpsimd.memset(zero[:, :], 0.0).then_inc(zero_set, 1)
            pool.wait_ge(zero_set, 1)
            zeros = zero[:, 0:1].broadcast_to([P, UNIT])

            def split(s, landed, hi_count, used):
                pool.wait_ge(raw_landed[s], landed)
                if used is not None:
                    pool.wait_ge(w_used, used)
                nc.gpsimd.tensor_tensor(w_hi[:, s, :], w_raw[:, s, :], zeros, ALU.add).then_inc(w_hi_done, 1)
                pool.wait_ge(w_hi_done, hi_count)
                nc.gpsimd.tensor_tensor(w_lo[:, s, :], w_raw[:, s, :], w_hi[:, s, :].bitcast(F32), ALU.subtract).then_inc(w_split, 1)

            for u in range(RING):
                split(u, 16, u + 1, None)
            loops = NU // RING - 1
            with pool.Fori(0, loops) as i:
                for s in range(RING):
                    split(s, i * 16 + 32, i * RING + (s + RING + 1), i * RING + (s + 1))
            for u in range((loops + 1) * RING, NU):
                split(u % RING, 16 * (u // RING + 1), u + 1, u - RING + 1)

        @block.tensor
        def _(pe):
            at = Place()
            pe.wait_ge(c_in, 16 * 2)
            pe_norm(pe, at, XN)
            gla_pe(pe, at)
            if stopping("gla"):
                return
            ffn_pe(pe, at)
            if stopping("ffn0"):
                return
            attn_pe(pe, at)
            if stopping("attn"):
                return
            ffn_pe(pe, at)
            if stopping("ffn1"):
                return
            mixer_pe(pe, at)
            if stopping("mixer"):
                return
            xattn_pe(pe, at)
            if stopping("xattn"):
                return
            peer_pe(pe, at)

        @block.scalar
        def _(a):
            at = Place()
            ch = Chain(a, a_chain)
            a.dma_start(X[:, :, :], T["x"]).then_inc(x_in, 16)
            a.dma_start(cst[:, :], T["consts"]).then_inc(c_in, 16)
            a.dma_start(gmask[:, :, :], T["masks"]).then_inc(c_in, 16)
            a.dma_start(par[:, :], T["params"]).then_inc(p_in, 16)
            a.dma_start(wup[0:16, :], T["gate_up_f"]).then_inc(p_in, 16)
            a.dma_start(wup[32:48, :], T["gate_up_b"]).then_inc(p_in, 16)
            a.wait_ge(x_in, 16)
            a.wait_ge(p_in, 48)
            a.wait_ge(c_in, 32)
            act_norm(a, at, X, XN, lambda k: PR("norm_mix", k))
            gla_act(a, ch, at)
            if stopping("gla"):
                return store(a)
            ffn_act(a, ch, at, 0)
            if stopping("ffn0"):
                return store(a)
            attn_act(a, ch, at)
            if stopping("attn"):
                return store(a)
            ffn_act(a, ch, at, 1)
            if stopping("ffn1"):
                return store(a)
            mixer_act(a, ch, at)
            if stopping("mixer"):
                return store(a)
            xattn_act(a, ch, at)
            if stopping("xattn"):
                return store(a)
            peer_act(a, ch, at)

        @block.vector
        def _(v):
            at = Place()
            ch = Chain(v, v_chain)
            v.wait_ge(x_in, 16)
            v.wait_ge(p_in, 48)
            v.wait_ge(c_in, 32)
            dve_norm(v, ch, at, X, XN, lambda k: PR("norm_mix", k))
            gla_dve(v, ch, at)
            if stopping("gla"):
                return
            ffn_dve(v, ch, at, 0)
            if stopping("ffn0"):
                return
            attn_dve(v, ch, at)
            if stopping("attn"):
                return
            ffn_dve(v, ch, at, 1)
            if stopping("ffn1"):
                return
            mixer_dve(v, ch, at)
            if stopping("mixer"):
                return
            xattn_dve(v, ch, at)
            if stopping("xattn"):
                return
            peer_dve(v, ch, at)


UNITS = {"gla": 34, "ffn0": 100, "attn": 120, "ffn1": 186, "mixer": 224, "xattn": 256, None: 528}


def constants():
    import numpy as np
    c = np.zeros((P, N_CONST), np.float32)

    def put(name, a):
        at, n = CONST[name]
        c[:, at:at + n] = a

    s, t = np.arange(P)[:, None], np.arange(P)[None, :]
    put("ident", s == t)
    put("negtri", -(s >= t).astype(np.float32))
    put("negones", -1.0)
    put("iota", np.broadcast_to(t, (P, P)))
    put("reset64", np.broadcast_to((np.arange(S) % 64 != 0), (P, S)))
    put("reset128", np.broadcast_to((np.arange(S) % P != 0), (P, S)))
    put("causal", s <= t)
    put("strict", s < t)
    rows = S // 64
    row = np.repeat(np.arange(rows, dtype=np.float32), 64)
    col = np.tile(np.arange(64, dtype=np.float32), rows)
    inv = (np.float32(10000.0) ** (-np.arange(32, dtype=np.float32) / np.float32(32))).astype(np.float32)
    ang = np.concatenate([row[:, None] * inv, col[:, None] * inv], axis=-1).astype(np.float32)
    for name, f in (("cos", np.cos), ("sin", np.sin)):
        put(name, f(ang).astype(np.float32).reshape(TT, P, 64).transpose(1, 0, 2).reshape(P, -1))
    sel = np.zeros((P, 4, P), np.float32)
    for h in range(4):
        sel[h, h, :] = 1.0
    put("sel", sel.reshape(P, -1))
    same = (s // 64) == (t // 64)
    masks = np.stack([same & (s <= t), same & (s > t)], axis=1).astype(np.uint32)
    return c, masks


def t_units(w):
    n = w.shape[1]
    return w.reshape(KD, P, n // P, P).transpose(2, 1, 0, 3).reshape(n // P, P, UNIT)


def n_units(w):
    import numpy as np
    k = w.shape[0] // P
    n = w.shape[1]
    halves = w.reshape(k, P, n // 512, 512).transpose(2, 0, 1, 3).reshape(k * n // 512, P, 512)
    return halves.reshape(-1, 2, P, 512).transpose(0, 2, 1, 3).reshape(-1, P, UNIT)


def weight_stream(a):
    import numpy as np

    def padded(w, at=0):
        z = np.zeros((D, P), w.dtype)
        z[:, at:at + w.shape[1]] = w
        return z

    parts = []
    w = a["gla_w_in"][0]
    parts += [t_units(w[:, 0:1024]), t_units(padded(w[:, 3072:3088])), t_units(padded(w[:, 3088:3104], 32)),
              n_units(w[:, 1024:3072]), n_units(a["gla_w_out"][0])]

    def ffn(layer):
        up, down = a["ffn_w_up"][layer], a["ffn_w_down"][layer]
        out = []
        for g in range(2):
            lo, hi = g * FF_GROUP * P, (g + 1) * FF_GROUP * P
            val, gate = t_units(up[:, lo:hi]), t_units(up[:, FF + lo:FF + hi])
            out.append(np.stack([val, gate], axis=1).reshape(-1, P, UNIT))
            out.append(n_units(down[lo:hi]))
        return out

    parts += ffn(0)
    parts += [n_units(a["attn_w_qkv"][0]), n_units(a["attn_w_out"][0])]
    parts += ffn(1)
    w = a["w_in_2"][0]
    parts += [t_units(w[:, 0:1024]), t_units(padded(w[:, 2048:2052])), t_units(padded(w[:, 2052:2056])),
              t_units(w[:, 2056:3080]), n_units(w[:, 1024:1536]), n_units(w[:, 1536:2048]), n_units(w[:, 3080:3592]),
              n_units(a["w_out_2"][0])]
    kv = a["xattn_wkv_2"][0]
    parts += [t_units(a["xattn_wq_2"][0]), t_units(kv[:, 0:D]), n_units(kv[:, D:]), n_units(a["xattn_wo_2"][0])]
    parts.append(t_units(a["peer_wq_2"][0]))
    u = a["peer_u_2"][0].reshape(NKEY, NKEY, KD, P).transpose(1, 3, 2, 0).reshape(NKEY, P, UNIT)
    v = a["peer_v_2"][0].reshape(NKEY, NKEY, D).transpose(1, 0, 2)
    j = 0
    while j < NKEY:
        n = min(PG, NKEY - j)
        parts += [u[j:j + n], n_units(v[j:j + n].reshape(n * P, D))]
        j += n
    return np.concatenate(parts, axis=0)


def columns(v):
    return v.reshape(-1, P).T


def parameters(a):
    import numpy as np
    p = np.zeros((P, N_PARAM), np.float32)

    def put(name, v):
        at, n = PARAM[name]
        p[:v.shape[0], at:at + n] = v

    put("norm_mix", columns(a["norm_mix"]))
    put("norm_ffn", columns(a["norm_ffn"]))
    put("gla_b_f", columns(a["gla_b_gate_f"][0]))
    put("gla_b_b", columns(a["gla_b_gate_b"][0]))
    put("gla_norm", np.tile(columns(a["gla_norm"][0]), (1, GLA_H)))
    put("mix_norm", columns(a["mix_norm_g_2"][0]))
    put("head_gain", columns(np.concatenate([a["mlstm_norm_g_2"][0], a["sb_norm_g_2"][0]])))
    put("xattn_norm", columns(a["xattn_norm_g_2"][0]))
    put("mem_norm", columns(a["mem_norm_g_2"][0]))
    put("ffn_norm_2", columns(a["ffn_norm_g_2"][0]))
    put("conv2_w", a["conv_w_2"][0].reshape(4, 8, P).transpose(2, 1, 0).reshape(P, 32))
    put("conv2_b", columns(a["conv_b_2"][0]))
    put("igate", a["igate_b_2"][0][:, None])
    put("fgate", a["fgate_b_2"][0][:, None])
    put("q_norm", np.broadcast_to(a["attn_q_norm"][0], (P, P)))
    put("k_norm", np.broadcast_to(a["attn_k_norm"][0], (P, P)))
    return p


def tiles(x):
    return x.reshape(-1, P, x.shape[-1]).transpose(1, 0, 2)


def kernel(**inputs):
    import numpy as np
    import concourse.bacc as bacc
    from concourse import mybir as mb
    from concourse.bass_utils import run_bass_kernel_spmd as run

    a = {k: np.asarray(v) for k, v in inputs.items()}
    consts, masks = constants()
    NU = UNITS[None]
    data = {
        "x": tiles(a["x"][0]), "mem": tiles(a["mem_2"][0]), "weights": weight_stream(a)[:NU],
        "consts": consts, "masks": masks, "params": parameters(a),
        "gate_up_f": a["gla_w_gate_up_f"][0], "gate_up_b": a["gla_w_gate_up_b"][0],
        "ffn_cw": a["ffn_w_conv"].reshape(2, 3, 2 * FF_TILES, P).transpose(0, 3, 2, 1).reshape(2, P, -1),
        "ffn_cb": a["ffn_b_conv"].reshape(2, 2 * FF_TILES, P).transpose(0, 2, 1),
        "subkeys": a["peer_subkeys_2"][0].reshape(16, NKEY, P).transpose(2, 0, 1).reshape(P, -1),
        "final_gain": np.broadcast_to(a["final_norm_g_2"], (P, D)),
    }
    nc = bacc.Bacc("TRN2", target_bir_lowering=False, num_devices=1)
    arrays, T = {}, {}
    for name, v in data.items():
        v = np.ascontiguousarray(v)
        arrays[f"in_{name}"] = v
        T[name] = nc.dram_tensor(f"in_{name}", v.shape, mb.dt.from_np(v.dtype), kind="ExternalInput").ap()
    o = nc.dram_tensor("out_0", (S, D), mb.dt.float32, kind="ExternalOutput").ap()
    build(nc, T, o.rearrange("(t p) d -> p t d", p=P), None, NU)
    r = run(nc, [arrays], core_ids=[0])
    return r.results[0]["out_0"].reshape(1, S, D)
```

```python
from contextlib import ExitStack

import concourse.bass as bass
from concourse import mybir

ALU = mybir.AluOpType
ACT = mybir.ActivationFunctionType
F32 = mybir.dt.float32
F32R = mybir.dt.float32r
U32 = mybir.dt.uint32
AX_X = mybir.AxisListType.X

P = 128
S = 512
TT = S // P
D = 1024
KD = D // P
EPS = 1e-6
LOWEST = -3.4028234e38

RING = 3
UNIT = 1024

GLA_H, GLA_DV, GLA_C = 4, 256, 64
GLA_SCALE = 128 ** -0.5
FF = 2816
FF_TILES = FF // P
FF_GROUP = FF_TILES // 2
AT_H, AT_KV = 8, 2
AT_SCALE = 128 ** -0.5
ML_H = 4
ML_SCALE = 128 ** -0.5
SB_H, SB_D = 8, 64
SB_SCALE = 64 ** -0.5
XA_H = 4
XA_SCALE = 256 ** -0.5
MEM_T = 2
PH, TOPK = 8, 16
NKEY = 128
PG = 12
GT = 32
PEER_LOOPS = NKEY // PG
PEER_TAIL = NKEY - PEER_LOOPS * PG

CONST = {}
PARAM = {}


def _lay(table, sizes):
    at = 0
    for name, size in sizes:
        table[name] = (at, size)
        at += size
    return at


N_CONST = _lay(CONST, [("ident", 128), ("negtri", 128), ("negones", 128), ("iota", 128), ("reset64", 512),
                       ("reset128", 512), ("causal", 128), ("strict", 128), ("cos", 256), ("sin", 256),
                       ("sel", 512)])
N_PARAM = _lay(PARAM, [("norm_mix", 16), ("norm_ffn", 16), ("gla_b_f", 4), ("gla_b_b", 4), ("gla_norm", 8),
                       ("mix_norm", 8), ("head_gain", 8), ("xattn_norm", 8), ("mem_norm", 8), ("ffn_norm_2", 8),
                       ("conv2_w", 32), ("conv2_b", 8), ("igate", 1), ("fgate", 1),
                       ("q_norm", 128), ("k_norm", 128)])


class Place:

    def __init__(self):
        self.unit = 0
        self.tjob = 0
        self.njob = 0
        self.nready = 0
        self.tr = 0
        self.fresh = False
        self.norm = 0
        self.phase = 0
        self.ffn = 0
        self.sc = 0
        self.pv = 0
        self.loop = None
        self.adds = {}

    def enter(self, register, **adds):
        self.loop, self.adds = register, adds

    def leave(self, times):
        self.unit += self.adds["unit"] * (times - 1)
        self.tjob += self.adds.get("tjob", 0) * (times - 1)
        self.njob += self.adds.get("njob", 0) * (times - 1)
        self.nready += self.adds.get("nready", 0) * (times - 1)
        self.loop = None

    def val(self, base, name):
        return base if self.loop is None else self.loop * self.adds[name] + base


def build(nc, T, out):
    ctx = ExitStack()
    with ctx:
        def sb(name, shape, dt=F32, where=ctx):
            return where.enter_context(nc.sbuf_tensor(name, shape, dt))

        def sem(name):
            return ctx.enter_context(nc.semaphore(name))

        X = sb("X", [P, TT, D])
        hT_hi = sb("hT_hi", [P, KD, S], F32R)
        hT_lo = sb("hT_lo", [P, KD, S], F32R)
        w_raw = sb("w_raw", [P, RING, UNIT])
        w_hi = sb("w_hi", [P, RING, UNIT], F32R)
        w_lo = sb("w_lo", [P, RING, UNIT], F32R)
        cst = sb("cst", [P, N_CONST])
        par = sb("par", [P, N_PARAM])
        zero = sb("zero", [P, 1])
        gmask = sb("gmask", [P, 2, P], U32)
        stat = sb("stat", [P, 192])
        idxT = sb("idxT", [P, 3, P])

        def C(name):
            a, n = CONST[name]
            return cst[:, a:a + n]

        def PR(name, i=0, n=1):
            a, _ = PARAM[name]
            return par[:, a + i:a + i + n]

        ident = C("ident")

        def overlay(*tensors):
            group = ExitStack()
            got = [sb(*t, where=group) if len(t) == 3 else sb(*t, F32, group) for t in tensors]
            group.close()
            return got

        wup = sb("wup", [P, S])
        XN, = overlay(("XN", [P, TT, D]))
        q1, k1, v1, g1, r1, la, bb, qd, ki, ke, keN, St, att = overlay(
            ("gla_q", [P, 4, S]), ("gla_k", [P, 4, S]), ("gla_v", [P, TT, D]), ("gla_g", [P, TT, D]),
            ("gla_r", [P, 2, S]), ("gla_la", [P, S]), ("gla_b", [P, 2, S]), ("gla_qd", [P, 2, 2, S]),
            ("gla_ki", [P, 2, 2, S]), ("gla_ke", [P, 2, 2, S]), ("gla_keN", [P, 2, S]),
            ("gla_state", [P, 2, 8, GLA_DV]), ("gla_att", [P, 2, S]))
        dch = stat[:, 80:112].rearrange("p (b d c) -> p b d c", b=2, d=2)
        act_hi, act_lo, cw, cb, yv, yg, yw, ys = overlay(
            ("act_hi", [P, PG, S], F32R), ("act_lo", [P, PG, S], F32R), ("ffn_cw", [P, 3 * 2 * FF_TILES]),
            ("ffn_cb", [P, 2 * FF_TILES]), ("ffn_yv", [P, S]), ("ffn_yg", [P, S]), ("ffn_w", [P, S]),
            ("ffn_s", [P, S]))
        qkv, qn, qr, qT, kT, at_tmp = overlay(
            ("at_qkv", [P, TT, 1536]), ("at_qn", [P, TT, 1280]), ("at_qr", [P, TT, 1280]), ("at_qT", [P, AT_H, S]),
            ("at_kT", [P, AT_KV, S]), ("at_tmp", [P, 1024]))
        at_pb = qr[:, :, :].rearrange("p t x -> p (t x)")[:, 0:3 * S].rearrange("p (b x) -> p b x", b=3)
        at_pT = qn[:, :, :].rearrange("p t x -> p (t x)")[:, 2 * S:10 * S].rearrange("p (b k x) -> p b k x", b=2, k=TT)
        mixg = ExitStack()
        ml_q = sb("ml_q", [P, 4, S], F32, mixg)
        ml_k = sb("ml_k", [P, 4, S], F32, mixg)
        sb_q = sb("sb_q", [P, 4, S], F32, mixg)
        sb_k = sb("sb_k", [P, 4, S], F32, mixg)
        vx = sb("ml_v", [P, TT, ML_H, P + 1], F32, mixg)
        og = sb("ml_o", [P, TT, S], F32, mixg)
        sb_v = sb("sb_v", [P, TT, S], F32, mixg)
        mixed = sb("mixed", [P, TT, D], F32, mixg)
        sub = ExitStack()
        cols = sb("ml_cols", [P, 64], F32, sub)
        dec = sb("ml_dec", [P, 16], F32, sub)
        mp = sb("ml_mp", [4, 16], F32, sub)
        kw = sb("ml_kw", [P, TT, P], F32, sub)
        cT = sb("ml_state", [P, 4, P + 1], F32, sub)
        wT = sb("ml_wT", [P, S], F32, sub)
        aT = sb("ml_aT", [P, S], F32, sub)
        nd = sb("ml_nd", [P, TT, P + 1], F32, sub)
        rows = sb("ml_rows", [4, 6, S], F32, sub)
        sub.close()
        sub = ExitStack()
        stA = sb("st_A", [P, 2, 1280], F32, sub)
        sb("st_gap", [P, 192], F32, sub)
        stT = sb("st_T", [P, 1280], F32, sub)
        stL = sb("st_L", [P, 2, 1280], F32, sub)
        sub.close()
        mixg.close()
        mem, xq, xk, xv, xp, xpT = overlay(
            ("mem", [P, MEM_T, D]), ("xa_q", [P, KD, S]), ("xa_k", [P, KD, 256]), ("xa_v", [P, MEM_T, D]),
            ("xa_p", [P, 3, 256]), ("xa_pT", [P, 2, MEM_T, S]))
        routing = ExitStack()
        rs = sb("ro_s", [P, TT, 16, NKEY], F32, routing)
        rq, subT = overlay(("ro_q", [P, 2, S]), ("ro_subkeys", [P, 16 * NKEY]))
        tv, ti, tif, srep, cand, crep, best, pos, ab, abf, sel_ij, stage, ohI, ohJ, ga = overlay(
            ("ro_top", [P, 16, TOPK]), ("ro_idx", [P, 16, TOPK], U32), ("ro_idxf", [P, 16, TOPK]),
            ("ro_rep", [P, NKEY]), ("ro_cand", [P, PH, TOPK * TOPK]), ("ro_crep", [P, TOPK * TOPK]),
            ("ro_best", [P, PH, TOPK]), ("ro_pos", [P, PH, TOPK], U32), ("ro_ab", [P, 2, PH * TOPK], U32),
            ("ro_abf", [P, 2, PH * TOPK]), ("ro_sel", [P, 3, P]), ("g_stage", [P, 2, NKEY, GT]),
            ("g_ohI", [P, 8, P]), ("g_ohJ", [P, 8, P]), ("g_act", [P, 3, S]))
        eqt = cand[:, :, :].rearrange("p h c -> p (h c)")
        routing.close()
        pv_hi, pv_lo, gh, act_in, gw, fgain, fout = overlay(
            ("pv_hi", [P, PG, S], F32R), ("pv_lo", [P, PG, S], F32R), ("g_half", [P, 2, S // GT, PG // 2, GT]),
            ("g_act_in", [P, 4, S]), ("g_w", [P, 2, S]), ("final_gain", [P, D]), ("final_out", [P, TT, D]))

        PS = [ctx.enter_context(nc.psum_tensor(f"bank{i}", [P, 512], F32)) for i in range(8)]
        gates = nc.dram_tensor("gates", [S // GT, P, NKEY, GT], F32, kind="Internal").ap()
        acts = nc.dram_tensor("acts", [NKEY, P, S], F32, kind="Internal").ap()

        raw_landed = [sem(f"raw_landed{i}") for i in range(RING)]
        w_hi_done = sem("w_hi_done")
        w_split = sem("w_split")
        w_used = sem("w_used")
        t_free = sem("t_free")
        n_ready = sem("n_ready")
        n_free = sem("n_free")
        tr_ready = sem("tr_ready")
        tr_hi = sem("tr_hi")
        tr_free = sem("tr_free")
        ss_ready = sem("ss_ready")
        ms_ready = sem("ms_ready")
        sd_ready = sem("sd_ready")
        rs_ready = sem("rs_ready")
        xn_ready = sem("xn_ready")
        xa_ready = sem("xa_ready")
        phase_done = sem("phase_done")
        a_chain = sem("a_chain")
        v_chain = sem("v_chain")
        c_in = sem("c_in")
        p_in = sem("p_in")
        x_in = [sem(f"x_in{t}") for t in range(TT)]
        o_sem = sem("out_stored")
        zero_set = sem("zero_set")

        class Chain:

            def __init__(self, eng, s):
                self.eng, self.s, self.n = eng, s, 0

            def link(self, ins):
                self.n += 1
                ins.then_inc(self.s, 1)
                self.eng.wait_ge(self.s, self.n)

        def phase_over(eng, at):
            at.phase += 1
            eng.drain().then_inc(phase_done, 1)
            eng.wait_ge(phase_done, 3 * at.phase)

        def parts3(wh, wl, hh, hl):
            return ((wh, hh), (wh, hl), (wl, hh))

        def pe_t_unit(pe, at, n=S):
            s = at.unit % RING
            pe.wait_ge(w_split, at.val(at.unit + 1, "unit"))
            if at.tjob >= 2:
                pe.wait_ge(t_free, at.val(at.tjob - 1, "tjob"))
            bank = PS[at.tjob % 2]
            for k in range(KD):
                if at.fresh and (k == 0 or k >= 6):
                    pe.wait_ge(tr_free, at.tr - KD + max(k + 1, 6))
                for i, (w, h) in enumerate(parts3(w_hi, w_lo, hT_hi, hT_lo)):
                    mm = nc.tensor.matmul(bank[:, 0:n], w[:, s, k * P:(k + 1) * P], h[:, k, 0:n],
                                          start=(k == 0 and i == 0), stop=(k == KD - 1 and i == 2))
            mm.then_inc(w_used, 1)
            at.fresh = False
            at.unit += 1
            at.tjob += 1

        def n_ends(at, K, nbs):
            ends = []
            for nb in range(nbs):
                last = (nb + 1) * K - 1
                ends.append((at.unit + last // 2, last % 2 == 1))
            return ends

        def pe_n_pass(pe, at, hi, lo, K, nbs, toks=TT, need=None):
            base = at.unit
            ends = n_ends(at, K, nbs)
            for nb in range(nbs):
                k = 0
                while k < K:
                    h0 = nb * K + k
                    u = base + h0 // 2
                    s = u % RING
                    halves = [(k, h0 % 2)]
                    if h0 % 2 == 0:
                        pe.wait_ge(w_split, at.val(u + 1, "unit"))
                        if k + 1 < K:
                            halves.append((k + 1, 1))
                    if need and nb == 0:
                        pe.wait_ge(need[0], at.val(need[1] + halves[-1][0] + 1, "tile"))
                    if at.fresh and nb == 0:
                        pe.wait_ge(tr_free, at.tr - KD + halves[-1][0] + 1)
                    for t in range(toks):
                        if k == 0 and at.njob + nb * toks + t >= toks:
                            pe.wait_ge(n_free, at.val(at.njob + nb * toks + t - toks + 1, "njob"))
                        for kk, part in halves:
                            w0 = part * 512
                            for i, (h, w) in enumerate(((hi, w_hi), (hi, w_lo), (lo, w_hi))):
                                mm = nc.tensor.matmul(PS[4 + t][:, :], h[:, kk, t * P:(t + 1) * P],
                                                      w[:, s, w0:w0 + 512],
                                                      start=(kk == 0 and i == 0), stop=(kk == K - 1 and i == 2))
                        whole = halves[-1][1] == 1
                        if t == toks - 1 and whole:
                            mm.then_inc(w_used, 1)
                        elif halves[-1][0] == K - 1:
                            mm.then_inc(n_ready, 1)
                    k = halves[-1][0] + 1
            at.fresh = False
            n_advance(at, K, nbs, toks)

        def n_advance(at, K, nbs, toks):
            for u, whole in n_ends(at, K, nbs):
                at.nready += toks - 1 if whole else toks
            at.unit += nbs * K // 2
            at.njob += nbs * toks

        def n_results(eng, at, K, nbs, toks=TT):
            seen = at.nready
            for nb, (u, whole) in enumerate(n_ends(at, K, nbs)):
                for t in range(toks):
                    if t == toks - 1 and whole:
                        eng.wait_ge(w_used, at.val(u + 1, "unit"))
                    else:
                        seen += 1
                        eng.wait_ge(n_ready, at.val(seen, "nready"))
                    yield nb, t
            n_advance(at, K, nbs, toks)

        def t_result(eng, at):
            eng.wait_ge(w_used, at.val(at.unit + 1, "unit"))
            bank = PS[at.tjob % 2]
            at.unit += 1
            at.tjob += 1
            return bank

        def skip_t(at, n=1):
            at.unit += n
            at.tjob += n

        def pe_transposes(pe, at, src, toks=TT, ks=range(KD)):
            for k in ks:
                if at.tr >= 4:
                    pe.wait_ge(tr_free, at.tr - 3)
                for t in range(toks):
                    mm = nc.tensor.transpose(PS[at.tr % 4][:, t * P:(t + 1) * P], src[:, t, k * P:(k + 1) * P], ident)
                mm.then_inc(tr_ready, 1)
                at.tr += 1
            at.fresh = True

        def act_transposed(a, at, gain, toks=TT):
            n = toks * P
            for k in range(KD):
                a.wait_ge(tr_ready, at.tr + 1)
                nc.scalar.activation(hT_hi[:, k, 0:n], PS[at.tr % 4][:, 0:n], ACT.Identity, scale=gain(k)).then_inc(tr_hi, 1)
                at.tr += 1

        def dve_transposed(v, at, gain, toks=TT):
            n = toks * P
            for k in range(KD):
                v.wait_ge(tr_hi, at.tr + 1)
                nc.vector.scalar_tensor_tensor(out=hT_lo[:, k, 0:n], in0=PS[at.tr % 4][:, 0:n], scalar=gain(k),
                                               in1=hT_hi[:, k, 0:n].bitcast(F32), op0=ALU.mult, op1=ALU.subtract).then_inc(tr_free, 1)
                at.tr += 1

        def act_squares(a, src, squares, toks=TT):
            for t in range(toks):
                last = nc.scalar.activation(squares[:, t, :], src[:, t, :], ACT.Square, accum_out=stat[:, t:t + 1])
            last.then_inc(ss_ready, 1)

        def act_added(a, at, K, nbs, squares=XN):
            added = at.njob + (nbs - 1) * TT
            n_advance(at, K, nbs, TT)
            nc.scalar.activation(stat[:, 191:192], zero[:, :], ACT.Sqrt)
            for t in range(TT):
                a.wait_ge(n_free, added + t + 1)
                last = nc.scalar.activation(squares[:, t, :], X[:, t, :], ACT.Square, accum_out=stat[:, t:t + 1])
            last.then_inc(ss_ready, 1)

        def act_norm(a, at, src, dst, gain, toks=TT):
            a.wait_ge(ms_ready, at.norm + 1)
            nc.scalar.activation(stat[:, 8:8 + toks], stat[:, 4:4 + toks], ACT.Sqrt).then_inc(sd_ready, 1)
            a.wait_ge(rs_ready, at.norm + 1)
            for t in range(toks // 2, toks):
                last = nc.scalar.activation(dst[:, t, :], src[:, t, :], ACT.Copy, scale=stat[:, 12 + t:13 + t])
            last.then_inc(xa_ready, 1)
            at.norm += 1
            act_transposed(a, at, gain, toks)

        def dve_norm(v, ch, at, src, dst, gain, toks=TT):
            v.wait_ge(ss_ready, at.norm + 1)
            nc.vector.tensor_scalar(stat[:, 4:4 + toks], stat[:, 0:toks], 1.0 / D, EPS, ALU.mult, ALU.add).then_inc(ms_ready, 1)
            v.wait_ge(sd_ready, at.norm + 1)
            nc.vector.reciprocal(stat[:, 12:12 + toks], stat[:, 8:8 + toks]).then_inc(rs_ready, 1)
            v.wait_ge(rs_ready, at.norm + 1)
            for t in range(toks // 2):
                last = nc.vector.tensor_scalar(dst[:, t, :], src[:, t, :], stat[:, 12 + t:13 + t], None, ALU.mult)
            last.then_inc(xn_ready, 1)
            at.norm += 1
            dve_transposed(v, at, gain, toks)

        def pe_norm(pe, at, src, toks=TT):
            at.norm += 1
            pe.wait_ge(xn_ready, at.norm)
            pe.wait_ge(xa_ready, at.norm)
            pe_transposes(pe, at, src, toks)

        gl_free = sem("gl_free")
        gl_bank = sem("gl_bank")
        lg_free = sem("lg_free")
        lg_bank = sem("lg_bank")
        gl_opnd = sem("gl_opnd")
        gl_soft = sem("gl_soft")
        gl_scan = sem("gl_scan")
        gl_diff = sem("gl_diff")
        gl_exp = sem("gl_exp")
        gl_ss = sem("gl_ss")
        gl_ms = sem("gl_ms")
        gl_sd = sem("gl_sd")
        gl_norm = sem("gl_norm")
        ff_y = sem("ff_y")
        ff_s = sem("ff_s")
        ff_w = sem("ff_w")
        ff_h = sem("ff_h")
        ff_ready = sem("ff_ready")
        ff_par = sem("ff_par")
        sc_bank = sem("sc_bank")
        sc_max = sem("sc_max")
        sc_exp = sem("sc_exp")
        sc_norm = sem("sc_norm")
        pt_bank = sem("pt_bank")
        pt_sbuf = sem("pt_sbuf")
        pv_bank = sem("pv_bank")
        oT_hi = sem("oT_hi")
        oT_lo = sem("oT_lo")
        at_rope = sem("at_rope")
        at_bank = sem("at_bank")
        at_sbuf = sem("at_sbuf")
        at_sq = sem("at_sq")
        at_ms = sem("at_ms")
        at_sd = sem("at_sd")
        mx_y = sem("mx_y")
        mx_sq = sem("mx_sq")
        mx_ms = sem("mx_ms")
        mx_sd = sem("mx_sd")
        mx_norm = sem("mx_norm")
        ml_soft = sem("ml_soft")
        ml_arg = sem("ml_arg")
        ml_rexp = sem("ml_rexp")
        ml_bc = sem("ml_bc")
        ml_qk = sem("ml_qk")
        ml_kt = sem("ml_kt")
        ml_kw = sem("ml_kw")
        ml_upd = sem("ml_upd")
        ml_A = sem("ml_A")
        ml_intra = sem("ml_intra")
        ml_st = sem("ml_st")
        ml_inter = sem("ml_inter")
        ml_diff = sem("ml_diff")
        ml_wexp = sem("ml_wexp")
        ml_nd = sem("ml_nd")
        ml_out = sem("ml_out")
        st_z = sem("st_z")
        st_L = sem("st_L")
        st_A = sem("st_A")
        st_o = sem("st_o")
        st_of = sem("st_of")
        st_r = sem("st_r")
        st_ln = sem("st_ln")
        st_min = sem("st_min")
        st_exp = sem("st_exp")
        m_in = sem("m_in")
        ro_bank = sem("ro_bank")
        ro_sbuf = sem("ro_sbuf")
        ro_gate = sem("ro_gate")
        ro_tr = sem("ro_tr")
        ro_arg = sem("ro_arg")
        ro_exp = sem("ro_exp")
        ro_idx_in = sem("ro_idx_in")
        oh_ready = sem("oh_ready")
        oh_used = sem("oh_used")
        g_evac = sem("g_evac")
        peer_w = sem("peer_w")
        peer_h = sem("peer_h")
        peer_ready = sem("peer_ready")
        fin = sem("fin")
        g_out = [sem(f"g_out{i}") for i in range(2)]
        g_in = [sem(f"g_in{i}") for i in range(2)]
        a_out = [sem(f"a_out{i}") for i in range(3)]
        a_in = [sem(f"a_in{i}") for i in range(4)]

        GJ = 14
        GB = (2, 3, 4, 5, 6, 7)

        def gla_pe(pe, at):
            def logits(h):
                for d in range(2):
                    if h:
                        pe.wait_ge(lg_free, 2 * h + d - 1)
                    nc.tensor.matmul(PS[d][:, :], wup[32 * d:32 * d + 16, h * P:(h + 1) * P], r1[32 * d:32 * d + 16, d, :],
                                     start=True, stop=True).then_inc(lg_bank, 1)

            for _ in range(10):
                pe_t_unit(pe, at)
            pe.wait_ge(t_free, at.tjob)
            logits(0)
            pe_n_pass(pe, at, hT_hi, hT_lo, KD, 1)
            logits(1)
            pe_n_pass(pe, at, hT_hi, hT_lo, KD, 3)
            pe.wait_ge(n_free, at.njob)
            for h in range(GLA_H):
                job = [GJ * h]
                sl = h % 2

                def bank():
                    if job[0] >= 6:
                        pe.wait_ge(gl_free, job[0] - 5)
                    job[0] += 1
                    return PS[GB[(job[0] - 1) % 6]]

                if 1 <= h < GLA_H - 1:
                    logits(h + 1)
                for d in range(2):
                    pe.wait_ge(gl_opnd, 2 * h + d + 1)
                    b = bank()
                    for t in range(TT):
                        mm = nc.tensor.transpose(b[:, t * P:(t + 1) * P], ke[:, sl, d, t * P:(t + 1) * P], ident)
                    mm.then_inc(gl_bank, 1)
                for d in range(2):
                    b = bank()
                    for t in range(TT):
                        c = slice(t * P, (t + 1) * P)
                        mm = nc.tensor.matmul(b[:, c], ki[:, sl, d, c], qd[:, sl, d, c], start=True, stop=True)
                    mm.then_inc(gl_bank, 1)
                for d in range(2):
                    pe.wait_ge(gl_free, GJ * h + 1 + d)
                    for j in range(4):
                        b = bank()
                        for half, c in enumerate(gla_chunks(d, j)):
                            r = slice((c % 2) * 64, (c % 2) * 64 + 64)
                            mm = nc.tensor.matmul(b[:, half * 256:half * 256 + 256], keN[r, d, (c // 2) * P:(c // 2 + 1) * P],
                                                  v1[r, c // 2, h * 256:(h + 1) * 256], start=True, stop=True)
                        mm.then_inc(gl_bank, 1)
                pe.wait_ge(gl_free, GJ * h + 12)
                for j in range(2):
                    b = bank()
                    for e in range(2):
                        t = 2 * j + e
                        o = slice(e * 256, e * 256 + 256)
                        for d in range(2):
                            nc.tensor.matmul(b[:, o], att[:, d, t * P:(t + 1) * P], v1[:, t, h * 256:(h + 1) * 256],
                                             start=(d == 0), stop=False)
                        for c in (2 * t, 2 * t + 1):
                            rows_ = slice((c % 2) * 64, (c % 2) * 64 + 64)
                            ds_ = [d for d in range(2) if (c > 0, c < 7)[d]]
                            for d in ds_:
                                mm = nc.tensor.matmul(b[rows_, o], qd[:, sl, d, c * 64:(c + 1) * 64], St[:, d, c, :],
                                                      start=False, stop=(d == ds_[-1]))
                    mm.then_inc(gl_bank, 1)
            pe.wait_ge(gl_free, GJ * GLA_H)
            pe.wait_ge(gl_norm, 1)
            pe_transposes(pe, at, v1, ks=range(KD - 2))
            pe.wait_ge(gl_norm, 2)
            pe_transposes(pe, at, v1, ks=range(KD - 2, KD))
            pe_n_pass(pe, at, hT_hi, hT_lo, KD, 2)

        def gla_chunks(d, j):
            seq = list(range(0, 7)) if d == 0 else list(range(7, 0, -1))
            return seq[4 * (j // 2) + j % 2:4 * (j // 2) + 4:2]

        def gla_act(a, ch, at):
            for i in range(10):
                b = t_result(a, at)
                if i < 4:
                    dst, src = q1[:, i, :], b[:, :]
                elif i < 8:
                    dst, src = k1[:, i - 4, :], b[:, :]
                else:
                    d = i - 8
                    dst, src = r1[32 * d:32 * d + 16, d, :], b[32 * d:32 * d + 16, :]
                nc.scalar.activation(dst, src, ACT.Copy).then_inc(t_free, 1)
            def decays(h):
                sl = h % 2
                a.wait_ge(lg_bank, 2 * h + 2)
                if h:
                    a.wait_ge(gl_exp, 2 * h)
                for d in range(2):
                    last = nc.scalar.activation(bb[:, d, :], PS[d][:, :], ACT.Abs, bias=PR(("gla_b_f", "gla_b_b")[d], h))
                ch.link(last)
                last = nc.scalar.activation(bb[:, :, :], bb[:, :, :], ACT.Exp, scale=-1.0)
                ch.link(last)
                for d in range(2):
                    nc.scalar.activation(bb[:, d, :], bb[:, d, :], ACT.Ln, bias=1.0).then_inc(gl_soft, 1)
                if h >= 2:
                    a.wait_ge(gl_bank, GJ * (h - 1))
                    a.wait_ge(gl_ss, h - 1)
                for d in range(2):
                    n = 2 * h + d
                    a.wait_ge(gl_scan, n + 1)
                    nc.scalar.activation(qd[:, sl, d, :], bb[:, d, :], ACT.Exp, scale=1.0 / 16)
                    nc.scalar.activation(ki[:, sl, d, :], bb[:, d, :], ACT.Exp, scale=-1.0 / 16)
                    nc.scalar.activation(dch[:, sl, d, :], bb[:, d, (63, 0)[d]::64], ACT.Exp, scale=1.0 / 16)
                    a.wait_ge(gl_diff, n + 1)
                    nc.scalar.activation(ke[:, sl, d, :], ke[:, sl, d, :], ACT.Exp, scale=1.0 / 16).then_inc(gl_exp, 1)

            def projected(nbs, first):
                for nb, t in n_results(a, at, KD, nbs):
                    nb += first
                    dst = (v1 if nb < 2 else g1)[:, t, (nb % 2) * 512:(nb % 2) * 512 + 512]
                    nc.scalar.activation(dst, PS[4 + t][:, :], ACT.Copy).then_inc(n_free, 1)

            decays(0)
            projected(1, 0)
            decays(1)
            projected(3, 1)
            a.wait_ge(n_free, at.njob)
            for t in range(TT):
                nc.scalar.activation(g1[:, t, :], g1[:, t, :], ACT.Silu)
            for h in range(GLA_H):
                if 1 <= h < GLA_H - 1:
                    decays(h + 1)
                if h == GLA_H - 1:
                    a.wait_ge(gl_ms, 1)
                    nc.scalar.activation(stat[:, 48:60], stat[:, 32:44], ACT.Sqrt).then_inc(gl_sd, 1)
                a.wait_ge(gl_free, GJ * (h + 1))
                for t in range(TT):
                    last = nc.scalar.activation(ki[:, h % 2, t // 2, (t % 2) * 256:(t % 2) * 256 + 256], v1[:, t, h * 256:(h + 1) * 256],
                                                ACT.Square, accum_out=stat[:, 16 + 4 * h + t:17 + 4 * h + t])
                last.then_inc(gl_ss, 1)
            a.wait_ge(gl_ms, 2)
            nc.scalar.activation(stat[:, 60:64], stat[:, 44:48], ACT.Sqrt).then_inc(gl_sd, 1)
            act_transposed(a, at, lambda k: PR("gla_norm", k))
            act_added(a, at, KD, 2)

        def dve_add(v, at, K, nbs):
            for nb, t in n_results(v, at, K, nbs):
                x = X[:, t, nb * 512:nb * 512 + 512]
                nc.vector.tensor_tensor(x, PS[4 + t][:, :], x, ALU.add).then_inc(n_free, 1)

        def gla_dve(v, ch, at):
            c64 = lambda ap: ap.rearrange("p (c x) -> p c x", x=64)

            def cumulate(h, d):
                n = 2 * h + d
                v.wait_ge(gl_soft, n + 1)
                nc.vector.tensor_scalar(la[:, :], PS[d][:, :], PR(("gla_b_f", "gla_b_b")[d], h), 0.0,
                                        ALU.add, ALU.min).then_inc(lg_free, 1)
                v.wait_ge(lg_free, n + 1)
                ch.link(nc.vector.tensor_tensor(la[:, :], la[:, :], bb[:, d, :], ALU.subtract))
                ways = slice(None) if d == 0 else slice(None, None, -1)
                nc.vector.tensor_tensor_scan(out=bb[:, d, ways], data0=C("reset64"), data1=la[:, ways],
                                             initial=0.0, op0=ALU.mult, op1=ALU.add).then_inc(gl_scan, 1)
                v.wait_ge(gl_scan, n + 1)
                e = (63, 0)[d]
                nc.vector.tensor_tensor(c64(ke[:, h % 2, d, :]), c64(bb[:, d, :])[:, :, e:e + 1].broadcast_to([P, 8, 64]),
                                        c64(bb[:, d, :]), ALU.subtract).then_inc(gl_diff, 1)

            def operands(h, d):
                sl = h % 2
                v.wait_ge(gl_exp, 2 * h + d + 1)
                nc.vector.scalar_tensor_tensor(out=qd[:, sl, d, :], in0=q1[:, h, :], scalar=GLA_SCALE, in1=qd[:, sl, d, :],
                                               op0=ALU.mult, op1=ALU.mult)
                nc.vector.tensor_tensor(ki[:, sl, d, :], k1[:, h, :], ki[:, sl, d, :], ALU.mult)
                nc.vector.tensor_tensor(ke[:, sl, d, :], k1[:, h, :], ke[:, sl, d, :], ALU.mult).then_inc(gl_opnd, 1)

            def mean_squares(heads_):
                v.wait_ge(gl_ss, heads_[-1] + 1)
                lo, n = 4 * heads_[0], 4 * len(heads_)
                nc.vector.tensor_scalar(stat[:, 32 + lo:32 + lo + n], stat[:, 16 + lo:16 + lo + n], 1.0 / GLA_DV, EPS,
                                        ALU.mult, ALU.add).then_inc(gl_ms, 1)

            def normalise(heads_, seen):
                lo, n = 4 * heads_[0], 4 * len(heads_)
                v.wait_ge(gl_sd, seen)
                ch.link(nc.vector.reciprocal(stat[:, 64 + lo:64 + lo + n], stat[:, 48 + lo:48 + lo + n]))
                for h in heads_:
                    for t in range(TT):
                        o = slice(h * 256, (h + 1) * 256)
                        last = nc.vector.scalar_tensor_tensor(out=v1[:, t, o], in0=v1[:, t, o],
                                                              scalar=stat[:, 64 + 4 * h + t:65 + 4 * h + t],
                                                              in1=g1[:, t, o], op0=ALU.mult, op1=ALU.mult)
                last.then_inc(gl_norm, 1)

            skip_t(at, 10)
            n_advance(at, KD, 4, TT)
            ch.link(nc.vector.memset(att[:, :, :], 0.0))
            for h in range(2):
                for d in range(2):
                    cumulate(h, d)
                for d in range(2):
                    operands(h, d)
            for h in range(GLA_H):
                ahead = h + 1 if 1 <= h < GLA_H - 1 else None
                job = GJ * h
                for d in range(2):
                    v.wait_ge(gl_bank, job + 1)
                    nc.vector.tensor_copy(keN[:, d, :], PS[GB[job % 6]][:, :]).then_inc(gl_free, 1)
                    job += 1
                for d in range(2):
                    v.wait_ge(gl_bank, job + 1)
                    nc.vector.copy_predicated(att[:, d, :].rearrange("p (t x) -> p t x", x=P),
                                              gmask[:, d, :].unsqueeze(1).broadcast_to([P, TT, P]),
                                              PS[GB[job % 6]][:, :].rearrange("p (t x) -> p t x", x=P)).then_inc(gl_free, 1)
                    job += 1
                if h == GLA_H - 1:
                    mean_squares(range(GLA_H - 1))
                for d in range(2):
                    if ahead is not None:
                        cumulate(ahead, d)
                    for half in range(2):
                        v.wait_ge(gl_bank, job + 2)
                        cs = (list(range(0, 7)) if d == 0 else list(range(7, 0, -1)))[4 * half:4 * half + 4]
                        for e, c in enumerate(cs):
                            to = c + 1 if d == 0 else c - 1
                            kv = PS[GB[(job + e % 2) % 6]][:, (e // 2) * 256:(e // 2) * 256 + 256]
                            if c == (0, 7)[d]:
                                ins = nc.vector.tensor_copy(St[:, d, to, :], kv)
                            else:
                                ins = nc.vector.scalar_tensor_tensor(out=St[:, d, to, :], in0=St[:, d, c, :],
                                                                     scalar=dch[:, h % 2, d, c:c + 1], in1=kv,
                                                                     op0=ALU.mult, op1=ALU.add)
                            if e == len(cs) - 1:
                                ins.then_inc(gl_free, 2)
                                v.wait_ge(gl_free, job + 2)
                            else:
                                ch.link(ins)
                        job += 2
                if ahead is not None:
                    operands(ahead, 0)
                    operands(ahead, 1)
                if h == GLA_H - 1:
                    normalise(range(GLA_H - 1), 1)
                for j in range(2):
                    v.wait_ge(gl_bank, job + 1)
                    nc.vector.tensor_copy(v1[:, 2 * j:2 * j + 2, h * 256:(h + 1) * 256],
                                          PS[GB[job % 6]][:, :].rearrange("p (e x) -> p e x", x=256)).then_inc(gl_free, 1)
                    job += 1
            mean_squares(range(GLA_H - 1, GLA_H))
            normalise(range(GLA_H - 1, GLA_H), 2)
            dve_transposed(v, at, lambda k: PR("gla_norm", k))
            dve_add(v, at, KD, 2)

        def ffn_pe(pe, at):
            layer = at.ffn
            at.ffn += 1
            pe_norm(pe, at, XN)
            for g in range(2):
                for f in range(2 * FF_GROUP):
                    pe_t_unit(pe, at)
                pe_n_pass(pe, at, act_hi, act_lo, FF_GROUP, 2, need=(ff_ready, FF_GROUP * (2 * layer + g)))

        def ffn_act(a, ch, at, layer):
            a.dma_start(cw[:, :], T["ffn_cw"][layer]).then_inc(ff_par, 16)
            a.dma_start(cb[:, :], T["ffn_cb"][layer]).then_inc(ff_par, 16)
            act_norm(a, at, X, XN, lambda k: PR("norm_ffn", 8 * layer + k))
            a.wait_ge(ff_par, 32 * (layer + 1))
            for g in range(2):
                for f in range(FF_GROUP):
                    n = FF_GROUP * (2 * layer + g) + f
                    tile = g * FF_GROUP + f
                    for side, y in enumerate((yv, yg)):
                        b = t_result(a, at)
                        if n and side == 0:
                            a.wait_ge(ff_w, n)
                        c = side * FF_TILES + tile
                        nc.scalar.activation(y[:, :], b[:, :], ACT.Identity, bias=cb[:, c:c + 1],
                                             scale=cw[:, 3 * c + 1:3 * c + 2]).then_inc(ff_y, 1)
                    a.wait_ge(t_free, at.tjob)
                    nc.scalar.activation(ys[:, :], yg[:, :], ACT.Silu).then_inc(ff_s, 1)
                    a.wait_ge(ff_w, n + 1)
                    nc.scalar.activation(act_hi[:, f, :], yw[:, :], ACT.Copy).then_inc(ff_h, 1)
                if g == 0:
                    n_advance(at, FF_GROUP, 2, TT)
            act_added(a, at, FF_GROUP, 2)

        def ffn_dve(v, ch, at, layer):
            dve_norm(v, ch, at, X, XN, lambda k: PR("norm_ffn", 8 * layer + k))
            v.wait_ge(ff_par, 32 * (layer + 1))
            for g in range(2):
                for f in range(FF_GROUP):
                    n = FF_GROUP * (2 * layer + g) + f
                    tile = g * FF_GROUP + f
                    for side, y in enumerate((yv, yg)):
                        b = PS[at.tjob % 2]
                        at.unit += 1
                        at.tjob += 1
                        c = side * FF_TILES + tile
                        v.wait_ge(ff_y, 2 * n + side + 1)
                        ch.link(nc.vector.scalar_tensor_tensor(out=y[:, 1:S], in0=b[:, 0:S - 1], scalar=cw[:, 3 * c:3 * c + 1],
                                                               in1=y[:, 1:S], op0=ALU.mult, op1=ALU.add))
                        nc.vector.scalar_tensor_tensor(out=y[:, 0:S - 1], in0=b[:, 1:S], scalar=cw[:, 3 * c + 2:3 * c + 3],
                                                       in1=y[:, 0:S - 1], op0=ALU.mult, op1=ALU.add).then_inc(t_free, 1)
                    v.wait_ge(ff_s, n + 1)
                    nc.vector.tensor_tensor(yw[:, :], ys[:, :], yv[:, :], ALU.mult).then_inc(ff_w, 1)
                    v.wait_ge(ff_h, n + 1)
                    nc.vector.tensor_tensor(act_lo[:, f, :], yw[:, :], act_hi[:, f, :].bitcast(F32), ALU.subtract).then_inc(ff_ready, 1)
                dve_add(v, at, FF_GROUP, 2)

        SC_BANKS = (0, 1, 7)

        def pe_attend(pe, at, H, KT, NB, score, value, pbuf, pTbuf):
            jobs = H * TT
            for i in range(jobs + 3):
                if i < jobs:
                    if i >= 3:
                        pe.wait_ge(sc_exp, at.sc + i - 2)
                    mm = score(i // TT, i % TT, PS[SC_BANKS[i % 3]])
                    mm.then_inc(sc_bank, 1)
                j = i - 2
                if 0 <= j < jobs:
                    pe.wait_ge(sc_norm, at.sc + j + 1)
                    if j >= 2:
                        pe.wait_ge(pt_sbuf, at.sc + j - 1)
                    for kk in range(KT):
                        mm = nc.tensor.transpose(PS[2 + j % 2][:, kk * P:(kk + 1) * P], pbuf[:, j % 3, kk * P:(kk + 1) * P], ident)
                    mm.then_inc(pt_bank, 1)
                j = i - 3
                if j >= 0 and j % TT == TT - 1:
                    h = j // TT
                    pe.wait_ge(pt_sbuf, at.sc + j + 1)
                    for nb in range(NB):
                        q = h * NB + nb
                        if q >= 3:
                            pe.wait_ge(oT_lo, at.pv + q - 2)
                        for kk in range(KT):
                            mm = nc.tensor.matmul(PS[4 + q % 3][:, :], value(kk, h, nb), pTbuf[:, h % 2, kk, :],
                                                  start=(kk == 0), stop=(kk == KT - 1))
                        mm.then_inc(pv_bank, 1)
            pe.wait_ge(oT_lo, at.pv + H * NB)
            at.sc += jobs
            at.pv += H * NB

        def act_attend(a, at, H, KT, NB, scale, pbuf, pTbuf):
            jobs = H * TT
            n = KT * P
            for i in range(jobs + 3):
                if i < jobs:
                    a.wait_ge(sc_max, at.sc + i + 1)
                    if i >= 3:
                        a.wait_ge(pt_bank, at.sc + i - 2)
                    nc.scalar.activation(pbuf[:, i % 3, 0:n], PS[SC_BANKS[i % 3]][:, 0:n], ACT.Exp, bias=stat[:, 96 + i:97 + i],
                                         scale=scale, accum_out=stat[:, 128 + i:129 + i]).then_inc(sc_exp, 1)
                j = i - 2
                if 0 <= j < jobs:
                    h, t = j // TT, j % TT
                    a.wait_ge(pt_bank, at.sc + j + 1)
                    if h >= 2 and t == 0:
                        a.wait_ge(pv_bank, at.pv + (h - 1) * NB)
                    nc.scalar.activation(pTbuf[:, h % 2, :, t * P:(t + 1) * P],
                                         PS[2 + j % 2][:, 0:n].rearrange("p (k x) -> p k x", x=P), ACT.Copy).then_inc(pt_sbuf, 1)
                j = i - 3
                if j >= 0 and j % TT == TT - 1:
                    h = j // TT
                    for nb in range(NB):
                        q = h * NB + nb
                        a.wait_ge(pv_bank, at.pv + q + 1)
                        nc.scalar.activation(hT_hi[:, q, :], PS[4 + q % 3][:, :], ACT.Copy).then_inc(oT_hi, 1)
            at.sc += jobs
            at.pv += H * NB

        def dve_attend(v, ch, at, H, KT, NB, scale, pbuf):
            jobs = H * TT
            n = KT * P
            for i in range(jobs + 3):
                if i < jobs:
                    v.wait_ge(sc_bank, at.sc + i + 1)
                    ch.link(nc.vector.reduce_max(stat[:, 64 + i:65 + i], PS[SC_BANKS[i % 3]][:, 0:n], AX_X))
                    nc.vector.tensor_scalar(stat[:, 96 + i:97 + i], stat[:, 64 + i:65 + i], -scale, None, ALU.mult).then_inc(sc_max, 1)
                j = i - 1
                if 0 <= j < jobs:
                    v.wait_ge(sc_exp, at.sc + j + 1)
                    ch.link(nc.vector.reciprocal(stat[:, 160 + j:161 + j], stat[:, 128 + j:129 + j]))
                    nc.vector.tensor_scalar(pbuf[:, j % 3, 0:n], pbuf[:, j % 3, 0:n], stat[:, 160 + j:161 + j], None,
                                            ALU.mult).then_inc(sc_norm, 1)
                j = i - 3
                if j >= 0 and j % TT == TT - 1:
                    h = j // TT
                    for nb in range(NB):
                        q = h * NB + nb
                        v.wait_ge(oT_hi, at.pv + q + 1)
                        nc.vector.tensor_tensor(hT_lo[:, q, :], PS[4 + q % 3][:, :], hT_hi[:, q, :].bitcast(F32),
                                                ALU.subtract).then_inc(oT_lo, 1)
            at.sc += jobs
            at.pv += H * NB

        NQK = AT_H + AT_KV

        def at_block(nb):
            return (TT, TT, AT_KV)[nb], 16 * nb

        def attn_pe(pe, at):
            pe_norm(pe, at, XN)
            pe_n_pass(pe, at, hT_hi, hT_lo, KD, 3)
            for j in range(NQK):
                pe.wait_ge(at_rope, j // TT + 1)
                if j >= 4:
                    pe.wait_ge(at_sbuf, j - 3)
                for t in range(TT):
                    mm = nc.tensor.transpose(PS[j % 4][:, t * P:(t + 1) * P], qr[:, t, j * P:(j + 1) * P], ident)
                mm.then_inc(at_bank, 1)
            pe.wait_ge(at_sbuf, NQK)

            def score(h, t, bank):
                return nc.tensor.matmul(bank[:, :], qT[:, h, t * P:(t + 1) * P], kT[:, h // (AT_H // AT_KV), :], start=True, stop=True)

            def value(kk, h, nb):
                g = h // (AT_H // AT_KV)
                return qkv[:, kk, (NQK + g) * P:(NQK + g + 1) * P]

            pe_attend(pe, at, AT_H, TT, 1, score, value, at_pb, at_pT)
            pe_n_pass(pe, at, hT_hi, hT_lo, KD, 2)

        def attn_act(a, ch, at):
            act_norm(a, at, X, XN, lambda k: PR("norm_mix", 8 + k))
            for nb, t in n_results(a, at, KD, 3):
                heads, s0 = at_block(nb)
                sq = nc.scalar.activation(qr[:, t, nb * 512:nb * 512 + heads * P], PS[4 + t][:, 0:heads * P], ACT.Square)
                nc.scalar.activation(qkv[:, t, nb * 512:nb * 512 + 512], PS[4 + t][:, :], ACT.Copy).then_inc(n_free, 1)
                if t == TT - 1:
                    sq.then_inc(at_sq, 1)
                    a.wait_ge(at_ms, nb + 1)
                    nc.scalar.activation(stat[:, 64 + s0:64 + s0 + TT * heads], stat[:, 64 + s0:64 + s0 + TT * heads],
                                         ACT.Sqrt).then_inc(at_sd, 1)
            for j in range(NQK):
                a.wait_ge(at_bank, j + 1)
                dst = qT[:, j, :] if j < AT_H else kT[:, j - AT_H, :]
                nc.scalar.activation(dst, PS[j % 4][:, :], ACT.Copy).then_inc(at_sbuf, 1)
            act_attend(a, at, AT_H, TT, 1, AT_SCALE, at_pb, at_pT)
            act_added(a, at, KD, 2)

        def attn_dve(v, ch, at):
            dve_norm(v, ch, at, X, XN, lambda k: PR("norm_mix", 8 + k))
            copied = at.njob
            n_advance(at, KD, 3, TT)
            for nb in range(3):
                n, s0 = at_block(nb)
                w = TT * n
                cols_ = slice(nb * 512, nb * 512 + n * P)
                heads = lambda ap: ap.rearrange("p t (h x) -> p t h x", x=P)
                v.wait_ge(at_sq, nb + 1)
                ch.link(nc.vector.tensor_reduce(stat[:, 16 + s0:16 + s0 + w].rearrange("p (t h) -> p t h", t=TT), heads(qr[:, :, cols_]), AX_X, ALU.add))
                nc.vector.tensor_scalar(stat[:, 64 + s0:64 + s0 + w], stat[:, 16 + s0:16 + s0 + w], 1.0 / P, EPS, ALU.mult,
                                        ALU.add).then_inc(at_ms, 1)
                v.wait_ge(at_sd, nb + 1)
                v.wait_ge(n_free, copied + TT * (nb + 1))
                r = stat[:, 112 + s0:112 + s0 + w]
                ch.link(nc.vector.reciprocal(r, stat[:, 64 + s0:64 + s0 + w]))
                x, o = heads(qn[:, :, cols_]), heads(qr[:, :, cols_])
                ch.link(nc.vector.tensor_tensor(x, heads(qkv[:, :, cols_]), r.rearrange("p (t h) -> p t h", t=TT).unsqueeze(3).broadcast_to([P, TT, n, P]),
                                                ALU.mult))
                gain = PR("q_norm" if nb < 2 else "k_norm", 0, P).unsqueeze(1).unsqueeze(1).broadcast_to([P, TT, n, P])
                ch.link(nc.vector.tensor_tensor(x, x, gain, ALU.mult))
                turn = lambda name: C(name).rearrange("p (t x) -> p t x", t=TT).unsqueeze(2).broadcast_to([P, TT, n, 64])
                x1, x2, o1, o2 = x[:, :, :, 0:64], x[:, :, :, 64:128], o[:, :, :, 0:64], o[:, :, :, 64:128]
                tmp = at_tmp[:, 0:TT * n * 64].rearrange("p (t h x) -> p t h x", t=TT, x=64)
                nc.vector.tensor_tensor(o1, x1, turn("cos"), ALU.mult)
                nc.vector.tensor_tensor(o2, x1, turn("sin"), ALU.mult)
                ch.link(nc.vector.tensor_tensor(tmp, x2, turn("sin"), ALU.mult))
                ch.link(nc.vector.tensor_tensor(o1, o1, tmp, ALU.subtract))
                ch.link(nc.vector.tensor_tensor(tmp, x2, turn("cos"), ALU.mult))
                nc.vector.tensor_tensor(o2, o2, tmp, ALU.add).then_inc(at_rope, 1)
                v.wait_ge(at_rope, nb + 1)
            dve_attend(v, ch, at, AT_H, TT, 1, AT_SCALE, at_pb)
            dve_add(v, at, KD, 2)

        def st_at(b):
            return (0, 512, 1024, 896)[b]

        def mixer_pe(pe, at):
            pe_norm(pe, at, XN)
            for _ in range(18):
                pe_t_unit(pe, at)
            pe_n_pass(pe, at, hT_hi, hT_lo, KD, 3)
            pe.wait_ge(n_free, at.njob)
            pe.wait_ge(ml_rexp, 1)
            for kind, row in enumerate((0, 1, 2, 5)):
                for n in range(TT):
                    c = kind * 16 + n * 4
                    nc.tensor.transpose(PS[7][:, c:c + 4], rows[0:4, row, n * P:(n + 1) * P], ident[0:4, 0:4])
            for h in range(ML_H):
                nc.tensor.matmul(PS[6][:, 4 * h:4 * h + 4], C("sel")[0:4, h * P:(h + 1) * P], mp[0:4, 8:12], start=True, stop=True)
            for h in range(ML_H):
                mm = nc.tensor.matmul(PS[h][:, :], C("sel")[0:4, h * P:(h + 1) * P], rows[0:4, 4, :], start=True, stop=True)
            mm.then_inc(ml_bc, 1)
            for h in range(ML_H):
                pe.wait_ge(ml_out, h + 1)
                for n in range(TT):
                    c = slice(n * P, (n + 1) * P)
                    mm = nc.tensor.matmul(PS[4][:, c], ml_k[:, h, c], ml_q[:, h, c], start=True, stop=True)
                mm.then_inc(ml_qk, 1)
                for n in range(TT):
                    c = slice(n * P, (n + 1) * P)
                    mm = nc.tensor.transpose(PS[5][:, c], ml_k[:, h, c], ident)
                mm.then_inc(ml_kt, 1)
                pe.wait_ge(ml_kw, h + 1)
                for n in range(TT - 1):
                    mm = nc.tensor.matmul(PS[5][:, n * 129:(n + 1) * 129], kw[:, n, :], vx[:, n, h, :], start=True, stop=True)
                mm.then_inc(ml_upd, 1)
                pe.wait_ge(ml_A, h + 1)
                for n in range(TT):
                    mm = nc.tensor.matmul(PS[6 + n // 2][:, (n % 2) * 129:(n % 2) * 129 + 129], aT[:, n * P:(n + 1) * P],
                                          vx[:, n, h, :], start=True, stop=True)
                mm.then_inc(ml_intra, 1)
                pe.wait_ge(ml_st, h + 1)
                for n in range(1, TT):
                    mm = nc.tensor.matmul(PS[4][:, (n - 1) * 129:n * 129], ml_q[:, h, n * P:(n + 1) * P], cT[:, n, :],
                                          start=True, stop=True)
                mm.then_inc(ml_inter, 1)

            def z(h, b, banks, stop):
                rows_ = slice((h % 2) * 64, (h % 2) * 64 + 64)
                o = st_at(b)
                return nc.tensor.matmul(banks[o // 512][:, o % 512:o % 512 + S - b * P], sb_k[rows_, h // 2, b * P:(b + 1) * P],
                                        sb_q[rows_, h // 2, b * P:S], start=True, stop=stop)

            def scores(h):
                for b in range(TT):
                    mm = z(h, b, PS[0:3], True)
                mm.then_inc(st_z, 1)

            def outputs(h):
                pe.wait_ge(st_A, h + 1)
                if h >= 2:
                    pe.wait_ge(st_of, h - 1)
                for t in range(TT):
                    for b in range(t + 1):
                        o = st_at(b) + (t - b) * P
                        mm = nc.tensor.matmul(PS[3 + 4 * (h % 2)][:, t * 64:(t + 1) * 64], stA[:, h % 2, o:o + P],
                                              sb_v[:, b, h * 64:(h + 1) * 64], start=(b == 0), stop=(b == t))
                mm.then_inc(st_o, 1)

            scores(0)
            pe.wait_ge(ml_out, ML_H + 1)
            for h in range(SB_H):
                pe.wait_ge(st_L, h + 1)
                if h + 1 < SB_H:
                    scores(h + 1)
                if h:
                    pe.wait_ge(st_min, h)
                for b in range(TT):
                    z(h, b, PS[4:7], False)
                    o = st_at(b)
                    for b2 in range(b, TT):
                        c = o % 512 + (b2 - b) * P
                        mm = nc.tensor.matmul(PS[4 + o // 512][:, c:c + S - b2 * P], C("negtri" if b2 == b else "negones"),
                                              stL[:, h % 2, st_at(b2):st_at(b2) + S - b2 * P], start=False, stop=(b2 == TT - 1))
                mm.then_inc(st_r, 1)
                if h:
                    outputs(h - 1)
            outputs(SB_H - 1)
            pe.wait_ge(st_of, SB_H - 1)
            pe.wait_ge(mx_norm, 1)
            pe_transposes(pe, at, mixed, ks=range(KD // 2))
            pe.wait_ge(mx_norm, 2)
            pe_transposes(pe, at, mixed, ks=range(KD // 2, KD))
            pe_n_pass(pe, at, hT_hi, hT_lo, KD, 2)

        def mixer_act(a, ch, at):
            act_norm(a, at, X, XN, lambda k: PR("mix_norm", k))
            for c in range(8):
                b = t_result(a, at)
                y = ml_q[:, c, :] if c < 4 else ml_k[:, c - 4, :]
                nc.scalar.activation(y, b[:, :], ACT.Identity, bias=PR("conv2_b", c), scale=PR("conv2_w", 4 * c + 3)).then_inc(mx_y, 1)
                a.wait_ge(t_free, at.tjob)
                nc.scalar.activation(y, y, ACT.Silu)
            b = t_result(a, at)
            nc.scalar.activation(rows[0:4, 0, :], b[0:4, :], ACT.Identity, bias=PR("igate")[0:4, :]).then_inc(t_free, 1)
            b = t_result(a, at)
            ch.link(nc.scalar.activation(rows[0:4, 1, :], b[0:4, :], ACT.Abs, bias=PR("fgate")[0:4, :]))
            nc.scalar.activation(rows[0:4, 2, :], b[0:4, :], ACT.Identity, bias=PR("fgate")[0:4, :]).then_inc(t_free, 1)
            ch.link(nc.scalar.activation(rows[0:4, 1, :], rows[0:4, 1, :], ACT.Exp, scale=-1.0))
            a.wait_ge(t_free, at.tjob)
            nc.scalar.activation(rows[0:4, 1, :], rows[0:4, 1, :], ACT.Ln, bias=1.0).then_inc(ml_soft, 1)
            for c in range(8):
                b = t_result(a, at)
                dst, scale = (sb_q[:, c, :], SB_SCALE) if c < 4 else (sb_k[:, c - 4, :], 1.0)
                nc.scalar.activation(dst, b[:, :], ACT.Copy, scale=scale).then_inc(t_free, 1)
            a.wait_ge(ml_arg, 1)
            for r in (1, 2, 5):
                nc.scalar.activation(rows[0:4, r, :], rows[0:4, r, :], ACT.Exp)
            nc.scalar.activation(mp[0:4, 8:12], mp[0:4, 8:12], ACT.Exp).then_inc(ml_rexp, 1)
            for nb, t in n_results(a, at, KD, 3):
                src = PS[4 + t][:, :]
                if nb == 0:
                    ins = nc.scalar.activation(vx[:, t, :, 0:P], src.rearrange("p (h x) -> p h x", x=P), ACT.Copy)
                elif nb == 1:
                    ins = nc.scalar.activation(og[:, t, :], src, ACT.Sigmoid)
                else:
                    ins = nc.scalar.activation(sb_v[:, t, :], src, ACT.Copy)
                ins.then_inc(n_free, 1)
            for h in range(ML_H):
                a.wait_ge(ml_diff, h + 1)
                nc.scalar.activation(wT[:, :], wT[:, :], ACT.Exp, scale=-1.0).then_inc(ml_wexp, 1)
                a.wait_ge(ml_intra, h + 1)
                for n in range(2):
                    last = nc.scalar.activation(nd[:, 2 * n:2 * n + 2, :], PS[6 + n][:, 0:258].rearrange("p (e x) -> p e x", x=129), ACT.Copy)
                last.then_inc(ml_nd, 1)

            def squares(h):
                a.wait_ge(st_of, h + 1)
                return nc.scalar.activation(ml_k[:, :, h * 64:(h + 1) * 64], mixed[:, :, 512 + h * 64:576 + h * 64], ACT.Square)

            for h in range(SB_H + 1):
                if h < SB_H:
                    a.wait_ge(st_z, h + 1)
                    for b, n in enumerate((512, 512, 256)):
                        last = nc.scalar.activation(stT[:, b * 512:b * 512 + n], PS[b][:, 0:n], ACT.Abs)
                    ch.link(last)
                    ch.link(nc.scalar.activation(stT[:, :], stT[:, :], ACT.Exp, scale=-1.0))
                    nc.scalar.activation(stT[:, :], stT[:, :], ACT.Ln, bias=1.0).then_inc(st_ln, 1)
                if h == 1:
                    a.wait_ge(ml_out, ML_H + 2)
                    for t in range(TT):
                        last = nc.scalar.activation(ml_q[:, t, :], mixed[:, t, 0:512], ACT.Square)
                    last.then_inc(mx_sq, 1)
                if h == 4:
                    a.wait_ge(mx_ms, 1)
                    nc.scalar.activation(stat[:, 64:80], stat[:, 64:80], ACT.Sqrt).then_inc(mx_sd, 1)
                if h:
                    a.wait_ge(st_min, h)
                    nc.scalar.activation(stA[:, (h - 1) % 2, :], stA[:, (h - 1) % 2, :], ACT.Exp).then_inc(st_exp, 1)
                if h >= 2:
                    squares(h - 2)
            squares(SB_H - 1).then_inc(mx_sq, 1)
            a.wait_ge(mx_ms, 2)
            nc.scalar.activation(stat[:, 80:112], stat[:, 80:112], ACT.Sqrt).then_inc(mx_sd, 1)
            act_transposed(a, at, lambda k: PR("head_gain", k))
            act_added(a, at, KD, 2)

        def mixer_dve(v, ch, at):
            dve_norm(v, ch, at, X, XN, lambda k: PR("mix_norm", k))
            nc.vector.memset(vx[:, :, :, P:P + 1], 1.0)
            for c in range(8):
                b = PS[at.tjob % 2]
                skip_t(at)
                y = ml_q[:, c, :] if c < 4 else ml_k[:, c - 4, :]
                v.wait_ge(mx_y, c + 1)
                for j in range(1, 4):
                    ins = nc.vector.scalar_tensor_tensor(out=y[:, j:S], in0=b[:, 0:S - j], scalar=PR("conv2_w", 4 * c + 3 - j),
                                                         in1=y[:, j:S], op0=ALU.mult, op1=ALU.add)
                    if j < 3:
                        ch.link(ins)
                    else:
                        ins.then_inc(t_free, 1)
            v.wait_ge(ml_soft, 1)
            R = lambda i: rows[0:4, i, :]
            lastcol = lambda i: rows[0:4, i, P - 1::P]
            ch.link(nc.vector.memset(mp[0:4, 0:1], 0.0))
            ch.link(nc.vector.memset(kw[0:4, :, :], 0.0))
            zrow = kw[0:4, :, :].rearrange("p a x -> p (a x)")
            ch.link(nc.vector.scalar_tensor_tensor(out=R(2), in0=R(2), scalar=0.0, in1=R(1), op0=ALU.min, op1=ALU.subtract))
            ch.link(nc.vector.tensor_tensor_scan(out=R(3), data0=C("reset128")[0:4, :], data1=R(2), initial=0.0, op0=ALU.mult, op1=ALU.add))
            ch.link(nc.vector.tensor_tensor(R(0), R(0), R(3), ALU.subtract))
            for n in range(TT):
                c = slice(n * P, (n + 1) * P)
                e = (n + 1) * P - 1
                ch.link(nc.vector.tensor_tensor_scan(out=rows[0:4, 4, c], data0=zrow[:, c], data1=rows[0:4, 0, c],
                                                     initial=mp[0:4, n:n + 1], op0=ALU.add, op1=ALU.max))
                ch.link(nc.vector.tensor_tensor(mp[0:4, n + 1:n + 2], rows[0:4, 3, e:e + 1], rows[0:4, 4, e:e + 1], ALU.add))
                nc.vector.tensor_scalar(rows[0:4, 1, c], rows[0:4, 4, c], -1.0, mp[0:4, n:n + 1], ALU.mult, ALU.add)
                nc.vector.tensor_scalar(rows[0:4, 5, c], rows[0:4, 0, c], rows[0:4, 4, e:e + 1], None, ALU.subtract)
            nc.vector.scalar_tensor_tensor(out=R(2), in0=R(3), scalar=-1.0, in1=R(4), op0=ALU.mult, op1=ALU.subtract)
            nc.vector.tensor_tensor(mp[0:4, 8:12], mp[0:4, 0:4], lastcol(4), ALU.subtract).then_inc(ml_arg, 1)
            skip_t(at, 10)
            n_advance(at, KD, 3, TT)
            v.wait_ge(ml_bc, 1)
            ch.link(nc.vector.tensor_copy(cols[:, :], PS[7][:, 0:64]))
            nc.vector.tensor_copy(dec[:, :], PS[6][:, 0:16]).then_inc(ml_out, 1)
            v.wait_ge(ml_out, 1)
            col = lambda kind, n, h: cols[:, kind * 16 + n * 4 + h:kind * 16 + n * 4 + h + 1]
            for h in range(ML_H):
                for n in range(TT):
                    c = slice(n * P, (n + 1) * P)
                    last = nc.vector.tensor_scalar(wT[:, c], PS[h][:, c], col(0, n, h), 0.0, ALU.subtract, ALU.max)
                last.then_inc(ml_diff, 1)
                v.wait_ge(ml_kt, h + 1)
                for n in range(TT):
                    last = nc.vector.tensor_scalar(kw[:, n, :], PS[5][:, n * P:(n + 1) * P], col(3, n, h), ML_SCALE, ALU.mult, ALU.mult)
                last.then_inc(ml_kw, 1)
                v.wait_ge(ml_wexp, h + 1)
                w3 = wT[:, :].rearrange("p (n x) -> p n x", x=P)
                ch.link(nc.vector.tensor_tensor(w3, w3, C("causal").unsqueeze(1).broadcast_to([P, TT, P]), ALU.mult))
                nc.vector.scalar_tensor_tensor(out=aT[:, :], in0=PS[4][:, :], scalar=ML_SCALE, in1=wT[:, :], op0=ALU.mult,
                                               op1=ALU.mult).then_inc(ml_A, 1)
                v.wait_ge(ml_upd, h + 1)
                ch.link(nc.vector.tensor_copy(cT[:, 1, :], PS[5][:, 0:129]))
                ch.link(nc.vector.scalar_tensor_tensor(out=cT[:, 2, :], in0=cT[:, 1, :], scalar=dec[:, 4 * h + 1:4 * h + 2],
                                                       in1=PS[5][:, 129:258], op0=ALU.mult, op1=ALU.add))
                nc.vector.scalar_tensor_tensor(out=cT[:, 3, :], in0=cT[:, 2, :], scalar=dec[:, 4 * h + 2:4 * h + 3],
                                               in1=PS[5][:, 258:387], op0=ALU.mult, op1=ALU.add).then_inc(ml_st, 1)
                v.wait_ge(ml_nd, h + 1)
                v.wait_ge(ml_inter, h + 1)
                for n in range(1, TT):
                    last = nc.vector.scalar_tensor_tensor(out=nd[:, n, :], in0=PS[4][:, (n - 1) * 129:n * 129], scalar=col(1, n, h),
                                                          in1=nd[:, n, :], op0=ALU.mult, op1=ALU.add)
                ch.link(last)
                guard = cols[:, 32 + h:32 + h + 13:4]
                den = nd[:, :, P:P + 1].rearrange("p n x -> p (n x)")
                ch.link(nc.vector.scalar_tensor_tensor(out=stat[:, 16:20], in0=den, scalar=-1.0, in1=den, op0=ALU.mult, op1=ALU.max))
                ch.link(nc.vector.tensor_tensor(stat[:, 16:20], stat[:, 16:20], guard, ALU.max))
                ch.link(nc.vector.reciprocal(stat[:, 20:24], stat[:, 16:20]))
                for n in range(TT):
                    last = nc.vector.tensor_scalar(mixed[:, n, h * P:(h + 1) * P], nd[:, n, 0:P], stat[:, 20 + n:21 + n], None, ALU.mult)
                last.then_inc(ml_out, 1)
            strict = C("strict")

            def masked(x):
                v3 = x[:, 0:1024].rearrange("p (b x) -> p b x", x=512)[:, :, 0:P]
                nc.vector.tensor_tensor(v3, v3, strict.unsqueeze(1).broadcast_to([P, 2, P]), ALU.mult)
                v2 = x[:, 896:1152].rearrange("p (b x) -> p b x", x=P)
                return nc.vector.tensor_tensor(v2, v2, strict.unsqueeze(1).broadcast_to([P, 2, P]), ALU.mult)

            def head_norm(n, w, s0, c0, squares, seen):
                m, r = stat[:, 64 + s0:64 + s0 + TT * n], stat[:, 112 + s0:112 + s0 + TT * n]
                v.wait_ge(mx_sq, seen)
                ch.link(nc.vector.tensor_reduce(stat[:, 16 + s0:16 + s0 + TT * n], squares.rearrange("p t (h x) -> p (t h) x", x=w), AX_X, ALU.add))
                nc.vector.tensor_scalar(m, stat[:, 16 + s0:16 + s0 + TT * n], 1.0 / w, EPS, ALU.mult, ALU.add).then_inc(mx_ms, 1)
                yield
                v.wait_ge(mx_sd, seen)
                ch.link(nc.vector.reciprocal(r, m))
                part = mixed[:, :, c0:c0 + 512].rearrange("p t (h x) -> p t h x", x=w)
                nc.vector.tensor_tensor(part, part, r.rearrange("p (t h) -> p t h", t=TT).unsqueeze(3).broadcast_to([P, TT, n, w]),
                                        ALU.mult).then_inc(mx_norm, 1)
                yield

            def head_outputs(h):
                v.wait_ge(st_o, h + 1)
                nc.vector.tensor_copy(mixed[:, :, 512 + h * 64:576 + h * 64],
                                      PS[3 + 4 * (h % 2)][:, 0:256].rearrange("p (t x) -> p t x", x=64)).then_inc(st_of, 1)

            norm = head_norm(4, P, 0, 0, ml_q[:, :, :], 1)
            for h in range(SB_H + 1):
                if h < SB_H:
                    v.wait_ge(st_ln, h + 1)
                    for b, n in enumerate((512, 512, 256)):
                        last = nc.vector.scalar_tensor_tensor(out=stL[:, h % 2, b * 512:b * 512 + n], in0=PS[b][:, 0:n], scalar=0.0,
                                                              in1=stT[:, b * 512:b * 512 + n], op0=ALU.max, op1=ALU.add)
                    ch.link(last)
                    masked(stL[:, h % 2, :]).then_inc(st_L, 1)
                if h:
                    g = h - 1
                    v.wait_ge(st_r, g + 1)
                    for b, n in enumerate((512, 512, 256)):
                        last = nc.vector.tensor_scalar(stA[:, g % 2, b * 512:b * 512 + n], PS[4 + b][:, 0:n], 80.0, None, ALU.min)
                    last.then_inc(st_min, 1)
                    v.wait_ge(st_exp, g + 1)
                    masked(stA[:, g % 2, :]).then_inc(st_A, 1)
                if h == 0:
                    v.wait_ge(ml_out, ML_H + 1)
                    nc.vector.tensor_tensor(mixed[:, :, 0:512], mixed[:, :, 0:512], og[:, :, :], ALU.mult).then_inc(ml_out, 1)
                    v.wait_ge(ml_out, ML_H + 2)
                if h == 3 or h == 5:
                    next(norm)
                if h >= 2:
                    head_outputs(h - 2)
            head_outputs(SB_H - 1)
            norm = head_norm(8, SB_D, 16, 512, ml_k[:, :, :], 2)
            next(norm)
            next(norm)
            dve_transposed(v, at, lambda k: PR("head_gain", k))
            dve_add(v, at, KD, 2)

        def xattn_pe(pe, at):
            pe_norm(pe, at, XN)
            for _ in range(8):
                pe_t_unit(pe, at)
            phase_over(pe, at)
            pe_norm(pe, at, mem, MEM_T)
            for _ in range(8):
                pe_t_unit(pe, at, 256)
            pe_n_pass(pe, at, hT_hi, hT_lo, KD, 2, toks=MEM_T)
            pe.wait_ge(t_free, at.tjob)
            pe.wait_ge(n_free, at.njob)

            def score(h, t, bank):
                for c in range(2):
                    mm = nc.tensor.matmul(bank[:, 0:256], xq[:, 2 * h + c, t * P:(t + 1) * P], xk[:, 2 * h + c, :],
                                          start=(c == 0), stop=(c == 1))
                return mm

            def value(kk, h, nb):
                return xv[:, kk, h * 256 + nb * P:h * 256 + (nb + 1) * P]

            pe_attend(pe, at, XA_H, MEM_T, 2, score, value, xp, xpT)
            pe_n_pass(pe, at, hT_hi, hT_lo, KD, 2)

        def xattn_act(a, ch, at):
            act_norm(a, at, X, XN, lambda k: PR("xattn_norm", k))
            a.dma_start(mem[:, :, :], T["mem"]).then_inc(m_in, 16)
            for c in range(8):
                b = t_result(a, at)
                nc.scalar.activation(xq[:, c, :], b[:, :], ACT.Copy).then_inc(t_free, 1)
            a.wait_ge(m_in, 16)
            phase_over(a, at)
            act_squares(a, mem, xv, MEM_T)
            act_norm(a, at, mem, mem, lambda k: PR("mem_norm", k), MEM_T)
            for c in range(8):
                b = t_result(a, at)
                nc.scalar.activation(xk[:, c, :], b[:, 0:256], ACT.Copy).then_inc(t_free, 1)
            for nb, t in n_results(a, at, KD, 2, MEM_T):
                nc.scalar.activation(xv[:, t, nb * 512:nb * 512 + 512], PS[4 + t][:, :], ACT.Copy).then_inc(n_free, 1)
            act_attend(a, at, XA_H, MEM_T, 2, XA_SCALE, xp, xpT)
            act_added(a, at, KD, 2)

        def xattn_dve(v, ch, at):
            dve_norm(v, ch, at, X, XN, lambda k: PR("xattn_norm", k))
            skip_t(at, 8)
            phase_over(v, at)
            v.wait_ge(m_in, 16)
            dve_norm(v, ch, at, mem, mem, lambda k: PR("mem_norm", k), MEM_T)
            skip_t(at, 8)
            n_advance(at, KD, 2, MEM_T)
            dve_attend(v, ch, at, XA_H, MEM_T, 2, XA_SCALE, xp)
            dve_add(v, at, KD, 2)

        def peer_pe(pe, at):
            pe_norm(pe, at, XN)
            pe.wait_ge(m_in, 32)
            for j in range(2 * PH + 1):
                if j < 2 * PH:
                    pe_t_unit(pe, at)
                if j:
                    i = j - 1
                    pe.wait_ge(t_free, at.tjob - (1 if j < 2 * PH else 0))
                    if i >= 4:
                        pe.wait_ge(ro_sbuf, i - 3)
                    for t in range(TT):
                        mm = nc.tensor.matmul(PS[4 + i % 4][:, t * P:(t + 1) * P], rq[:, i % 2, t * P:(t + 1) * P],
                                              subT[:, i * NKEY:(i + 1) * NKEY], start=True, stop=True)
                    mm.then_inc(ro_bank, 1)
            phase_over(pe, at)

            def tokens(n):
                for k in range(8):
                    pe.wait_ge(oh_ready, at.val(n + k + 1, "token"))
                    if k % 4 == 0 and n + k >= 8:
                        pe.wait_ge(g_evac, at.val((n + k) // 4 - 1, "bank"))
                    nc.tensor.matmul(PS[2 + k // 4 % 2][:, (k % 4) * P:(k % 4 + 1) * P], ohI[:, k % 8, :], ohJ[:, k % 8, :],
                                     start=True, stop=True).then_inc(oh_used, 1)

            def token_tile(t):
                for _ in range(SEARCH_UNITS):
                    pe_t_unit(pe, at)
                pe.wait_ge(ro_gate, at.val(t + 1, "tiles"))
                if t:
                    pe.wait_ge(ro_idx_in, at.val(t, "tiles"))
                for kind in range(3):
                    mm = nc.tensor.transpose(PS[4][:, kind * P:(kind + 1) * P], sel_ij[:, kind, :], ident)
                mm.then_inc(ro_tr, 1)
                for k in range(0, P, 8):
                    tokens(t * P + k)
                    pe_t_unit(pe, at)

            token_tile(0)
            with pe.Fori(0, TT - 1) as i:
                at.enter(i, **TILE)
                token_tile(1)
            at.leave(TT - 1)
            for _ in range(REST):
                pe_t_unit(pe, at)

            with pe.Fori(0, PEER_LOOPS) as i:
                at.enter(i, **GROUP)
                pe_n_pass(pe, at, pv_hi, pv_lo, PG, 2, need=(peer_ready, 0))
            at.leave(PEER_LOOPS)
            pe_n_pass(pe, at, pv_hi, pv_lo, PEER_TAIL, 2, need=(peer_ready, PEER_LOOPS * PG))

        SEARCH_UNITS = 14
        PER_TILE = SEARCH_UNITS + P // 8
        TILE = {"unit": PER_TILE, "tjob": PER_TILE, "tile": PER_TILE, "tile_ring": PER_TILE // 3, "token": P, "bank": P // 4,
                "chunk": P // GT, "chunk2": P // GT // 2, "tiles": 1}
        STEP = {"token": 2 * GT}
        GROUP = {"unit": PG, "njob": 8, "nready": 6, "tile": PG, "group": 1}
        REST = NKEY - PER_TILE * TT

        def peer_act(a, ch, at):
            a.dma_start(subT[:, :], T["subkeys"]).then_inc(m_in, 16)
            act_norm(a, at, X, XN, lambda k: PR("ffn_norm_2", k))
            for j in range(2 * PH):
                b = t_result(a, at)
                if j >= 2:
                    a.wait_ge(ro_bank, j - 1)
                nc.scalar.activation(rq[:, j % 2, :], b[:, :], ACT.Copy).then_inc(t_free, 1)
            phase_over(a, at)
            tile = [0]

            def units(n):
                for _ in range(n):
                    j = tile[0]
                    b = t_result(a, at)
                    if j >= 3:
                        a.wait_ge(a_out[j % 3], at.val(j // 3, "tile_ring") * 16)
                    nc.scalar.activation(ga[:, j % 3, :], b[:, :], ACT.Gelu).then_inc(t_free, 1)
                    a.wait_ge(t_free, at.val(at.tjob, "tjob"))
                    jj = at.val(j, "tile")
                    dst = acts[jj] if isinstance(jj, int) else acts[bass.ds(jj, 1)].rearrange("a p t -> p (a t)")
                    a.dma_start(dst, ga[:, j % 3, :]).then_inc(a_out[j % 3], 16)
                    tile[0] += 1

            def token_tile(t):
                units(SEARCH_UNITS)
                a.wait_ge(ro_arg, at.val(t + 1, "tiles"))
                nc.scalar.activation(sel_ij[:, 2, :], sel_ij[:, 2, :], ACT.Exp).then_inc(ro_exp, 1)
                a.wait_ge(ro_tr, at.val(t + 1, "tiles"))
                nc.scalar.activation(idxT[:, :, :], PS[4][:, 0:384].rearrange("p (k x) -> p k x", x=P), ACT.Copy).then_inc(ro_idx_in, 1)
                for c in range(P // GT):
                    chunk = t * (P // GT) + c
                    if chunk >= 2:
                        a.wait_ge(g_out[c % 2], at.val(chunk // 2, "chunk2") * 16)
                    for q in range(GT // 4):
                        a.wait_ge(oh_used, at.val(chunk * GT + 4 * (q + 1), "token"))
                        nc.scalar.activation(stage[:, c % 2, :, 4 * q:4 * q + 4], PS[2 + q % 2][:, :].rearrange("p (t j) -> p j t", j=NKEY),
                                             ACT.Copy).then_inc(g_evac, 1)
                        if q == GT // 4 - 1:
                            a.wait_ge(g_evac, at.val((chunk + 1) * GT // 4, "bank"))
                            cc = at.val(chunk, "chunk")
                            dst = gates[cc] if isinstance(cc, int) else gates[bass.ds(cc, 1)].rearrange("a p j t -> p (a j) t")
                            a.dma_start(dst, stage[:, c % 2, :, :]).then_inc(g_out[c % 2], 16)
                        if q % 2:
                            units(1)

            token_tile(0)
            with a.Fori(0, TT - 1) as i:
                at.enter(i, **TILE)
                token_tile(1)
            at.leave(TT - 1)
            tile[0] += PER_TILE * (TT - 2)
            def load_act(j, s):
                src = acts[j] if isinstance(j, int) else acts[bass.ds(j, 1)].rearrange("a p t -> p (a t)")
                a.dma_start(act_in[:, s, :], src).then_inc(a_in[s], 16)

            def load_gates(j, half, n=PG // 2):
                cols_ = slice(j, j + n) if isinstance(j, int) else bass.ds(j, n)
                a.dma_start(gh[:, half, :, 0:n, :], gates[:, :, cols_, :].rearrange("c p j t -> p c j t")).then_inc(g_in[half], 16)

            def prepare(n, j0, last):
                for jj in range(n):
                    j = at.val(j0 + jj, "tile")
                    if jj == 0:
                        a.wait_ge(peer_w, j + 4)
                        load_gates(j + PG // 2, 1, min(PG // 2, n - PG // 2))
                    if jj == PG // 2 and not last:
                        a.wait_ge(peer_w, j + 4)
                        load_gates(j + PG // 2, 0)
                    if jj + 3 < n or not last:
                        a.wait_ge(peer_w, j + 4)
                        load_act(j + 3, (jj + 3) % 4)
                    a.wait_ge(w_used, at.val(at.unit - PG // 2 + jj // 2 + 1, "unit"))
                    a.wait_ge(peer_w, j + 5)
                    nc.scalar.activation(pv_hi[:, jj, :], gw[:, jj % 2, :], ACT.Copy).then_inc(peer_h, 1)
                if not last:
                    n_advance(at, n, 2, TT)

            for s in range(2):
                a.wait_ge(g_out[s], 16 * (S // GT // 2))
            load_gates(0, 0)
            for j in range(3):
                load_act(j, j)
            a.dma_start(fgain[:, :], T["final_gain"]).then_inc(m_in, 16)
            units(REST)
            for s in range(3):
                a.wait_ge(a_out[s], 16 * len(range(s, NKEY, 3)))
            with a.Fori(0, PEER_LOOPS) as i:
                at.enter(i, **GROUP)
                prepare(PG, 0, False)
            at.leave(PEER_LOOPS)
            prepare(PEER_TAIL, PEER_LOOPS * PG, True)
            act_added(a, at, PEER_TAIL, 2, fout)
            a.wait_ge(ms_ready, at.norm + 1)
            nc.scalar.activation(stat[:, 8:12], stat[:, 4:8], ACT.Sqrt).then_inc(sd_ready, 1)
            for t in range(TT):
                a.wait_ge(fin, t + 1)
                a.dma_start(out[:, t, :], fout[:, t, :]).then_inc(o_sem, 16)
            a.wait_ge(o_sem, 16 * TT)

        def peer_search(v, ch, t):
            iota16 = C("iota")[:, 0:TOPK]
            for j in range(2 * PH):
                top, idx, s_ = tv[:, j, :], ti[:, j, :], rs[:, t, j, :]
                ch.link(nc.vector.max(top[:, 0:8], s_))
                nc.vector.max_index(idx[:, 0:8], top[:, 0:8], s_)
                ch.link(nc.vector.match_replace(srep[:, :], top[:, 0:8], s_, LOWEST))
                ch.link(nc.vector.max(top[:, 8:16], srep[:, :]))
                ch.link(nc.vector.max_index(idx[:, 8:16], top[:, 8:16], srep[:, :]))
            tv4 = tv[:, :, :].rearrange("p (h e) k -> p h e k", e=2)
            c4 = cand[:, :, :].rearrange("p h (a b) -> p h a b", a=TOPK)
            ch.link(nc.vector.tensor_copy(tif[:, :, :], ti[:, :, :]))
            ch.link(nc.vector.tensor_tensor(c4, tv4[:, :, 0, :].unsqueeze(3).broadcast_to([P, PH, TOPK, TOPK]),
                                            tv4[:, :, 1, :].unsqueeze(2).broadcast_to([P, PH, TOPK, TOPK]), ALU.add))
            for h in range(PH):
                top, idx, s_ = best[:, h, :], pos[:, h, :], cand[:, h, :]
                ch.link(nc.vector.max(top[:, 0:8], s_))
                nc.vector.max_index(idx[:, 0:8], top[:, 0:8], s_)
                ch.link(nc.vector.match_replace(crep[:, :], top[:, 0:8], s_, LOWEST))
                ch.link(nc.vector.max(top[:, 8:16], crep[:, :]))
                ch.link(nc.vector.max_index(idx[:, 8:16], top[:, 8:16], crep[:, :]))
            flat = pos[:, :, :].rearrange("p h k -> p (h k)")
            nc.vector.tensor_single_scalar(ab[:, 0, :], flat, 4, ALU.logical_shift_right)
            ch.link(nc.vector.tensor_single_scalar(ab[:, 1, :], flat, 15, ALU.bitwise_and))
            ch.link(nc.vector.tensor_copy(abf[:, :, :], ab[:, :, :]))
            if t:
                v.wait_ge(ro_tr, t)
            tif4 = tif[:, :, :].rearrange("p (h e) k -> p h e k", e=2)
            eq4 = eqt.rearrange("p (h k a) -> p h k a", h=PH, k=TOPK)
            eq3 = eqt.rearrange("p (k a) -> p k a", a=TOPK)
            for e in range(2):
                ch.link(nc.vector.tensor_tensor(eq3, abf[:, e, :].unsqueeze(2).broadcast_to([P, P, TOPK]),
                                                iota16.unsqueeze(1).broadcast_to([P, P, TOPK]), ALU.is_equal))
                ch.link(nc.vector.tensor_tensor(eq4, eq4, tif4[:, :, e, :].unsqueeze(2).broadcast_to([P, PH, TOPK, TOPK]), ALU.mult))
                ch.link(nc.vector.tensor_reduce(sel_ij[:, e, :], eq3, AX_X, ALU.add))
            g3 = sel_ij[:, 2, :].rearrange("p (h k) -> p h k", h=PH)
            nc.vector.tensor_tensor(g3, best[:, :, :], best[:, :, 0:1].broadcast_to([P, PH, TOPK]), ALU.subtract).then_inc(ro_arg, 1)
            v.wait_ge(ro_exp, t + 1)
            ch.link(nc.vector.tensor_reduce(stat[:, 16:24], g3, AX_X, ALU.add))
            ch.link(nc.vector.reciprocal(stat[:, 24:32], stat[:, 16:24]))
            nc.vector.tensor_tensor(g3, g3, stat[:, 24:32].unsqueeze(2).broadcast_to([P, PH, TOPK]), ALU.mult).then_inc(ro_gate, 1)

        def peer_dve(v, ch, at):
            dve_norm(v, ch, at, X, XN, lambda k: PR("ffn_norm_2", k))
            skip_t(at, 2 * PH)
            for j in range(2 * PH):
                v.wait_ge(ro_bank, j + 1)
                nc.vector.tensor_copy(rs[:, :, j, :], PS[4 + j % 4][:, :].rearrange("p (t x) -> p t x", x=P)).then_inc(ro_sbuf, 1)
            phase_over(v, at)

            def tokens(n0, c0, count):
                for k in range(count):
                    n = n0 + k
                    if n >= 8:
                        v.wait_ge(oh_used, at.val(n - 7, "token"))
                    c = at.val(c0 + k, "token")
                    col = slice(c, c + 1) if isinstance(c, int) else bass.ds(c, 1)
                    nc.vector.tensor_scalar(ohI[:, k % 8, :], C("iota"), idxT[:, 0, col], None, ALU.is_equal)
                    nc.vector.tensor_scalar(ohJ[:, k % 8, :], C("iota"), idxT[:, 1, col], idxT[:, 2, col], ALU.is_equal, ALU.mult).then_inc(oh_ready, 1)

            for t in range(TT):
                peer_search(v, ch, t)
                v.wait_ge(ro_idx_in, t + 1)
                if t == 0:
                    tokens(0, 0, P)
                else:
                    with v.Fori(0, 2) as i:
                        at.enter(i, **STEP)
                        tokens(t * P, 0, 2 * GT)
                    at.loop = None
            skip_t(at, NKEY)
            v.wait_ge(oh_used, S)
            nc.vector.memset(stat[:, 0:1], 0.0).then_inc(peer_w, 4)

            def prepare(tiles_, unit0, g, j0):
                for jj in tiles_:
                    if jj % (PG // 2) == 0:
                        v.wait_ge(g_in[jj // (PG // 2)], (at.val(g, "group") + 1) * 16)
                    v.wait_ge(a_in[jj % 4], (at.val(g, "group") * 3 + jj // 4 + 1) * 16)
                    view = lambda ap: ap.rearrange("p (c t) -> p c t", t=GT)
                    nc.vector.tensor_tensor(view(gw[:, jj % 2, :]), view(act_in[:, jj % 4, :]), gh[:, jj // (PG // 2), :, jj % (PG // 2), :],
                                            ALU.mult).then_inc(peer_w, 1)
                    v.wait_ge(w_used, at.val(unit0 - PG // 2 + jj // 2 + 1, "unit"))
                    v.wait_ge(peer_h, at.val(j0 + jj + 1, "tile"))
                    nc.vector.tensor_tensor(pv_lo[:, jj, :], gw[:, jj % 2, :], pv_hi[:, jj, :].bitcast(F32), ALU.subtract).then_inc(peer_ready, 1)

            def add_and_prepare(g, n_next):
                unit = at.unit
                for nb, t in n_results(v, at, PG, 2):
                    x = X[:, t, nb * 512:nb * 512 + 512]
                    nc.vector.tensor_tensor(x, PS[4 + t][:, :], x, ALU.add).then_inc(n_free, 1)
                    if t == TT - 1:
                        tiles_ = range(n_next - 2) if nb == 0 else range(n_next - 2, n_next)
                        prepare(tiles_, unit + PG, g + 1, (g + 1) * PG)

            prepare(range(PG), at.unit, 0, 0)
            with v.Fori(0, PEER_LOOPS - 1) as i:
                at.enter(i, **GROUP)
                add_and_prepare(0, PG)
            at.leave(PEER_LOOPS - 1)
            add_and_prepare(PEER_LOOPS - 1, PEER_TAIL)
            dve_add(v, at, PEER_TAIL, 2)
            v.wait_ge(ss_ready, at.norm + 1)
            nc.vector.tensor_scalar(stat[:, 4:8], stat[:, 0:4], 1.0 / D, EPS, ALU.mult, ALU.add).then_inc(ms_ready, 1)
            v.wait_ge(sd_ready, at.norm + 1)
            ch.link(nc.vector.reciprocal(stat[:, 12:16], stat[:, 8:12]))
            v.wait_ge(m_in, 48)
            for t in range(TT):
                nc.vector.scalar_tensor_tensor(out=fout[:, t, :], in0=X[:, t, :], scalar=stat[:, 12 + t:13 + t], in1=fgain[:, :],
                                               op0=ALU.mult, op1=ALU.mult).then_inc(fin, 1)


        block = ctx.enter_context(nc.Block())

        @block.sync
        def _(sp):
            ws = T["weights"]
            NU = ws.shape[0]

            def load(u, s):
                src = ws[u] if isinstance(u, int) else ws[bass.ds(u, 1)].rearrange("a p n -> p (a n)")
                sp.dma_start(w_raw[:, s, :], src).then_inc(raw_landed[s], 16)

            for u in range(RING):
                load(u, u)
            loops = NU // RING - 1
            with sp.Fori(0, loops) as i:
                for s in range(RING):
                    sp.wait_ge(w_split, i * RING + (s + 1))
                    load(i * RING + (s + RING), s)
            for u in range((loops + 1) * RING, NU):
                sp.wait_ge(w_split, u - RING + 1)
                load(u, u % RING)

        @block.gpsimd
        def _(pool):
            NU = T["weights"].shape[0]
            nc.gpsimd.memset(zero[:, :], 0.0).then_inc(zero_set, 1)
            pool.wait_ge(zero_set, 1)
            zeros = zero[:, 0:1].broadcast_to([P, UNIT])

            def split(s, landed, hi_count, used):
                pool.wait_ge(raw_landed[s], landed)
                if used is not None:
                    pool.wait_ge(w_used, used)
                nc.gpsimd.tensor_tensor(w_hi[:, s, :], w_raw[:, s, :], zeros, ALU.add).then_inc(w_hi_done, 1)
                pool.wait_ge(w_hi_done, hi_count)
                nc.gpsimd.tensor_tensor(w_lo[:, s, :], w_raw[:, s, :], w_hi[:, s, :].bitcast(F32), ALU.subtract).then_inc(w_split, 1)

            for u in range(RING):
                split(u, 16, u + 1, None)
            loops = NU // RING - 1
            with pool.Fori(0, loops) as i:
                for s in range(RING):
                    split(s, i * 16 + 32, i * RING + (s + RING + 1), i * RING + (s + 1))
            for u in range((loops + 1) * RING, NU):
                split(u % RING, 16 * (u // RING + 1), u + 1, u - RING + 1)

        @block.tensor
        def _(pe):
            at = Place()
            pe.wait_ge(c_in, 64)
            pe_norm(pe, at, XN)
            gla_pe(pe, at)
            ffn_pe(pe, at)
            attn_pe(pe, at)
            ffn_pe(pe, at)
            mixer_pe(pe, at)
            xattn_pe(pe, at)
            peer_pe(pe, at)

        @block.scalar
        def _(a):
            at = Place()
            ch = Chain(a, a_chain)
            for t in range(TT):
                a.dma_start(X[:, t, :], T["x"][:, t, :]).then_inc(x_in[t], 16)
            a.dma_start(par[:, :], T["params"]).then_inc(p_in, 16)
            a.dma_start(cst[:, :], T["consts"]).then_inc(c_in, 16)
            a.dma_start(gmask[:, :, :], T["masks"]).then_inc(c_in, 16)
            a.dma_start(wup[0:16, :], T["gate_up_f"]).then_inc(c_in, 16)
            a.dma_start(wup[32:48, :], T["gate_up_b"]).then_inc(c_in, 16)
            a.wait_ge(zero_set, 1)
            for t in range(TT):
                a.wait_ge(x_in[t], 16)
                last = nc.scalar.activation(XN[:, t, :], X[:, t, :], ACT.Square, accum_out=stat[:, t:t + 1])
            last.then_inc(ss_ready, 1)
            a.wait_ge(p_in, 16)
            act_norm(a, at, X, XN, lambda k: PR("norm_mix", k))
            gla_act(a, ch, at)
            ffn_act(a, ch, at, 0)
            attn_act(a, ch, at)
            ffn_act(a, ch, at, 1)
            mixer_act(a, ch, at)
            xattn_act(a, ch, at)
            peer_act(a, ch, at)

        @block.vector
        def _(v):
            at = Place()
            ch = Chain(v, v_chain)
            v.wait_ge(p_in, 16)
            dve_norm(v, ch, at, X, XN, lambda k: PR("norm_mix", k))
            v.wait_ge(c_in, 64)
            gla_dve(v, ch, at)
            ffn_dve(v, ch, at, 0)
            attn_dve(v, ch, at)
            ffn_dve(v, ch, at, 1)
            mixer_dve(v, ch, at)
            xattn_dve(v, ch, at)
            peer_dve(v, ch, at)


def constants():
    import numpy as np
    c = np.zeros((P, N_CONST), np.float32)

    def put(name, a):
        at, n = CONST[name]
        c[:, at:at + n] = a

    s, t = np.arange(P)[:, None], np.arange(P)[None, :]
    put("ident", s == t)
    put("negtri", -(s >= t).astype(np.float32))
    put("negones", -1.0)
    put("iota", np.broadcast_to(t, (P, P)))
    put("reset64", np.broadcast_to((np.arange(S) % 64 != 0), (P, S)))
    put("reset128", np.broadcast_to((np.arange(S) % P != 0), (P, S)))
    put("causal", s <= t)
    put("strict", s < t)
    rows = S // 64
    row = np.repeat(np.arange(rows, dtype=np.float32), 64)
    col = np.tile(np.arange(64, dtype=np.float32), rows)
    inv = (np.float32(10000.0) ** (-np.arange(32, dtype=np.float32) / np.float32(32))).astype(np.float32)
    ang = np.concatenate([row[:, None] * inv, col[:, None] * inv], axis=-1).astype(np.float32)
    for name, f in (("cos", np.cos), ("sin", np.sin)):
        put(name, f(ang).astype(np.float32).reshape(TT, P, 64).transpose(1, 0, 2).reshape(P, -1))
    sel = np.zeros((P, 4, P), np.float32)
    for h in range(4):
        sel[h, h, :] = 1.0
    put("sel", sel.reshape(P, -1))
    same = (s // 64) == (t // 64)
    masks = np.stack([same & (s <= t), same & (s > t)], axis=1).astype(np.uint32)
    return c, masks


def t_units(w):
    n = w.shape[1]
    return w.reshape(KD, P, n // P, P).transpose(2, 1, 0, 3).reshape(n // P, P, UNIT)


def n_units(w):
    import numpy as np
    k = w.shape[0] // P
    n = w.shape[1]
    halves = w.reshape(k, P, n // 512, 512).transpose(2, 0, 1, 3).reshape(k * n // 512, P, 512)
    return halves.reshape(-1, 2, P, 512).transpose(0, 2, 1, 3).reshape(-1, P, UNIT)


def weight_stream(a):
    import numpy as np

    def padded(w, at=0):
        z = np.zeros((D, P), w.dtype)
        z[:, at:at + w.shape[1]] = w
        return z

    parts = []
    w = a["gla_w_in"][0]
    parts += [t_units(w[:, 0:1024]), t_units(padded(w[:, 3072:3088])), t_units(padded(w[:, 3088:3104], 32)),
              n_units(w[:, 1024:3072]), n_units(a["gla_w_out"][0])]

    def ffn(layer):
        up, down = a["ffn_w_up"][layer], a["ffn_w_down"][layer]
        out = []
        for g in range(2):
            lo, hi = g * FF_GROUP * P, (g + 1) * FF_GROUP * P
            val, gate = t_units(up[:, lo:hi]), t_units(up[:, FF + lo:FF + hi])
            out.append(np.stack([val, gate], axis=1).reshape(-1, P, UNIT))
            out.append(n_units(down[lo:hi]))
        return out

    parts += ffn(0)
    parts += [n_units(a["attn_w_qkv"][0]), n_units(a["attn_w_out"][0])]
    parts += ffn(1)
    w = a["w_in_2"][0]
    parts += [t_units(w[:, 0:1024]), t_units(padded(w[:, 2048:2052])), t_units(padded(w[:, 2052:2056])),
              t_units(w[:, 2056:3080]), n_units(w[:, 1024:1536]), n_units(w[:, 1536:2048]), n_units(w[:, 3080:3592]),
              n_units(a["w_out_2"][0])]
    kv = a["xattn_wkv_2"][0]
    parts += [t_units(a["xattn_wq_2"][0]), t_units(kv[:, 0:D]), n_units(kv[:, D:]), n_units(a["xattn_wo_2"][0])]
    parts.append(t_units(a["peer_wq_2"][0]))
    u = a["peer_u_2"][0].reshape(NKEY, NKEY, KD, P).transpose(1, 3, 2, 0).reshape(NKEY, P, UNIT)
    v = a["peer_v_2"][0].reshape(NKEY, NKEY, D).transpose(1, 0, 2)
    parts.append(u)
    for j in range(0, NKEY, PG):
        parts.append(n_units(v[j:j + PG].reshape(-1, D)))
    return np.concatenate(parts, axis=0)


def columns(v):
    return v.reshape(-1, P).T


def parameters(a):
    import numpy as np
    p = np.zeros((P, N_PARAM), np.float32)

    def put(name, v):
        at, n = PARAM[name]
        p[:v.shape[0], at:at + n] = v

    put("norm_mix", columns(a["norm_mix"]))
    put("norm_ffn", columns(a["norm_ffn"]))
    put("gla_b_f", columns(a["gla_b_gate_f"][0]))
    put("gla_b_b", columns(a["gla_b_gate_b"][0]))
    put("gla_norm", np.tile(columns(a["gla_norm"][0]), (1, GLA_H)))
    put("mix_norm", columns(a["mix_norm_g_2"][0]))
    put("head_gain", columns(np.concatenate([a["mlstm_norm_g_2"][0], a["sb_norm_g_2"][0]])))
    put("xattn_norm", columns(a["xattn_norm_g_2"][0]))
    put("mem_norm", columns(a["mem_norm_g_2"][0]))
    put("ffn_norm_2", columns(a["ffn_norm_g_2"][0]))
    put("conv2_w", a["conv_w_2"][0].reshape(4, 8, P).transpose(2, 1, 0).reshape(P, 32))
    put("conv2_b", columns(a["conv_b_2"][0]))
    put("igate", a["igate_b_2"][0][:, None])
    put("fgate", a["fgate_b_2"][0][:, None])
    put("q_norm", np.broadcast_to(a["attn_q_norm"][0], (P, P)))
    put("k_norm", np.broadcast_to(a["attn_k_norm"][0], (P, P)))
    return p


def tiles(x):
    return x.reshape(-1, P, x.shape[-1]).transpose(1, 0, 2)


def kernel(**inputs):
    import numpy as np
    import concourse.bacc as bacc
    from concourse import mybir as mb
    from concourse.bass_utils import run_bass_kernel_spmd as run

    a = {k: np.asarray(v) for k, v in inputs.items()}
    consts, masks = constants()
    data = {
        "x": tiles(a["x"][0]), "mem": tiles(a["mem_2"][0]), "weights": weight_stream(a),
        "consts": consts, "masks": masks, "params": parameters(a),
        "gate_up_f": a["gla_w_gate_up_f"][0], "gate_up_b": a["gla_w_gate_up_b"][0],
        "ffn_cw": a["ffn_w_conv"].reshape(2, 3, 2 * FF_TILES, P).transpose(0, 3, 2, 1).reshape(2, P, -1),
        "ffn_cb": a["ffn_b_conv"].reshape(2, 2 * FF_TILES, P).transpose(0, 2, 1),
        "subkeys": a["peer_subkeys_2"][0].reshape(16, NKEY, P).transpose(2, 0, 1).reshape(P, -1),
        "final_gain": np.broadcast_to(a["final_norm_g_2"], (P, D)),
    }
    nc = bacc.Bacc("TRN2", target_bir_lowering=False, num_devices=1)
    arrays, T = {}, {}
    for name, v in data.items():
        v = np.ascontiguousarray(v)
        arrays[f"in_{name}"] = v
        T[name] = nc.dram_tensor(f"in_{name}", v.shape, mb.dt.from_np(v.dtype), kind="ExternalInput").ap()
    o = nc.dram_tensor("out_0", (S, D), mb.dt.float32, kind="ExternalOutput").ap()
    build(nc, T, o.rearrange("(t p) d -> p t d", p=P))
    r = run(nc, [arrays], core_ids=[0])
    return r.results[0]["out_0"].reshape(1, S, D)
```
